# Optimizing a Trainium2 kernel written in Bass

```python
import math
import jax, jax.numpy as jnp
from jax import lax
import numpy as np

D_MODEL = 1024
BATCH = 1
SEQ = 256
DEPTH = 2
DEC_BATCH = 8
DEC_SEQ = 8
PAST_LEN = 256
PAGE_SIZE = 128

N_META = 16
N_A_LAYERS = DEPTH // 2
N_B_LAYERS = DEPTH - N_A_LAYERS
RWKV_HEAD = 64
RWKV_HEADS = D_MODEL // RWKV_HEAD
DECAY_LORA = 64
AAA_LORA = 64
GATE_LORA = 128
LNX_EPS = 64e-5
DIFF_HEAD = 64
DIFF_HEADS = D_MODEL // (2 * DIFF_HEAD)
QK_WIDTH = 2 * DIFF_HEADS * DIFF_HEAD
V_WIDTH = DIFF_HEADS * 2 * DIFF_HEAD
Q_BLOCK = 128
SUBLN_EPS = 1e-5
N_EXPERTS = 16
N_GROUPS = 4
EXPERTS_PER_GROUP = N_EXPERTS // N_GROUPS
TOPK_GROUPS = 1
TOP_K = 2
D_EXPERT = 512
LN_EPS = 1e-5
DEEPNORM_ALPHA = (2 * DEPTH) ** 0.25
DEEPNORM_BETA = (8 * DEPTH) ** -0.25

kernel_name = 'yoco_rwkv7_diffattn_grouped_moe_step'

def _layernorm(x, g, b):
    xf = x.astype(jnp.float32)
    mu = xf.mean(-1, keepdims=True)
    var = jnp.square(xf - mu).mean(-1, keepdims=True)
    return ((xf - mu) * lax.rsqrt(var + LN_EPS) * g + b).astype(x.dtype)

def _lambda_init(layer_idx):
    return 0.8 - 0.6 * math.exp(-0.3 * layer_idx)

def _rwkv7_step(S, inp):
    r, w, k, v, a, b = inp
    sa = jnp.einsum('bhij,bhj->bhi', S, a)
    S = S * w[:, :, None, :] + sa[..., None] * b[:, :, None, :] + v[..., None] * k[:, :, None, :]
    return S, jnp.einsum('bhij,bhj->bhi', S, r)

def _rwkv7_time_mix(x, wkv0, x_prev, mix, w_rkv, dw0, dw1, dw2, aw0, aw1, aw2, gw1, gw2, kk_ka, r_k, lnx, w_out):
    B, T, D = x.shape
    H, N = RWKV_HEADS, RWKV_HEAD
    f32 = jnp.float32
    xx = jnp.concatenate([x_prev[:, None, :].astype(x.dtype), x[:, :-1]], axis=1) - x
    xr, xw, xk, xv, xa, xg = (x + xx * mix[i] for i in range(6))
    r = xr @ w_rkv[0]
    k = xk @ w_rkv[1]
    v = xv @ w_rkv[2]
    w_log = -jax.nn.softplus(-(dw0 + jnp.tanh(xw @ dw1) @ dw2)) - 0.5
    decay = jnp.exp(-jnp.exp(w_log.astype(f32)))
    a = jax.nn.sigmoid(aw0 + (xa @ aw1) @ aw2)
    g = jax.nn.sigmoid(xg @ gw1) @ gw2
    kk = (k * kk_ka[0]).astype(f32).reshape(B, T, H, N)
    kk = kk / jnp.maximum(jnp.linalg.norm(kk, axis=-1, keepdims=True), 1e-12)
    k = k * (1 + (a - 1) * kk_ka[1])

    def heads(t):
        return t.astype(f32).reshape(B, T, H, N)

    def tmaj(t):
        return jnp.swapaxes(t, 0, 1)

    rh, kh, vh, ah = heads(r), heads(k), heads(v), heads(a)
    S_fin, o = lax.scan(_rwkv7_step, wkv0.astype(f32),
                        (tmaj(rh), tmaj(heads(decay)), tmaj(kh), tmaj(vh), tmaj(-kk), tmaj(kk * ah)))
    o = tmaj(o)
    mu = o.mean(-1, keepdims=True)
    var = jnp.square(o - mu).mean(-1, keepdims=True)
    o = ((o - mu) * lax.rsqrt(var + LNX_EPS)).reshape(B, T, D) * lnx[0] + lnx[1]
    o = o + (jnp.sum(rh * kh * r_k, -1, keepdims=True) * vh).reshape(B, T, D)
    out = (o.astype(x.dtype) * g) @ w_out
    return out, S_fin.astype(wkv0.dtype), x[:, -1]

def _shared_kv(x, w_kv):
    B, T, _ = x.shape
    kv = x @ w_kv
    k = kv[..., :QK_WIDTH].reshape(B, T, 2 * DIFF_HEADS, DIFF_HEAD)
    v = kv[..., QK_WIDTH:].reshape(B, T, DIFF_HEADS, 2 * DIFF_HEAD)
    return k, v

def _diff_attend(q, k, v, q_offset, lam):
    B, Tq = q.shape[0], q.shape[1]
    S = k.shape[1]
    qblk = min(Q_BLOCK, Tq)
    nb = -(-Tq // qblk)
    qb = jnp.pad(q, ((0, 0), (0, nb * qblk - Tq), (0, 0), (0, 0)))
    qb = qb.reshape(B, nb, qblk, 2 * DIFF_HEADS, DIFF_HEAD).swapaxes(0, 1)
    key_pos = jnp.arange(S)

    def block(args):
        qi, start = args
        qpos = q_offset + start + jnp.arange(qblk)
        s = jnp.einsum('bqhd,bkhd->bhqk', qi, k).astype(jnp.float32) * (DIFF_HEAD ** -0.5)
        s = jnp.where(key_pos[None, :] <= qpos[:, None], s, -jnp.inf)
        p = jax.nn.softmax(s, axis=-1).reshape(B, DIFF_HEADS, 2, qblk, S)
        amap = p[:, :, 0] - lam * p[:, :, 1]
        return jnp.einsum('bhqk,bkhe->bqhe', amap.astype(v.dtype), v)

    o = lax.map(block, (qb, jnp.arange(nb) * qblk))
    return o.swapaxes(0, 1).reshape(B, nb * qblk, DIFF_HEADS, 2 * DIFF_HEAD)[:, :Tq]

def _diff_attn_layer(x, k_all, v_all, w_q, lam_vecs, subln, w_out, lambda_init):
    B, T, _ = x.shape
    q = (x @ w_q).reshape(B, T, 2 * DIFF_HEADS, DIFF_HEAD)
    lf = lam_vecs.astype(jnp.float32)
    lam = jnp.exp(jnp.sum(lf[0] * lf[1])) - jnp.exp(jnp.sum(lf[2] * lf[3])) + lambda_init
    o = _diff_attend(q, k_all, v_all, k_all.shape[1] - T, lam).astype(jnp.float32)
    o = o * lax.rsqrt(jnp.mean(jnp.square(o), -1, keepdims=True) + SUBLN_EPS) * subln
    o = o * (1.0 - lambda_init)
    return o.reshape(B, T, D_MODEL).astype(x.dtype) @ w_out

def _moe(x, router_w, router_b, w_gate, w_up, w_down):
    B, T, D = x.shape
    f32 = jnp.float32
    xt = x.reshape(B * T, D)
    s = jax.nn.sigmoid((xt @ router_w).astype(f32))
    sel = s + router_b.astype(f32)
    grp = lax.top_k(sel.reshape(-1, N_GROUPS, EXPERTS_PER_GROUP), 2)[0].sum(-1)
    _, gidx = lax.top_k(grp, TOPK_GROUPS)
    gmask = jax.nn.one_hot(gidx, N_GROUPS, dtype=f32).sum(1)
    emask = jnp.repeat(gmask, EXPERTS_PER_GROUP, axis=-1) > 0
    _, eidx = lax.top_k(jnp.where(emask, sel, -jnp.inf), TOP_K)
    wts = jnp.take_along_axis(s, eidx, -1)
    wts = wts / wts.sum(-1, keepdims=True)
    gates = jnp.einsum('nk,nke->ne', wts, jax.nn.one_hot(eidx, N_EXPERTS, dtype=f32)).astype(x.dtype)
    y = jnp.zeros_like(xt)
    for e in range(N_EXPERTS):
        h = jax.nn.silu(xt @ w_gate[e]) * (xt @ w_up[e])
        y = y + gates[:, e:e + 1] * (h @ w_down[e])
    return y.reshape(B, T, D)

def setup_inputs(seed: int = 0) -> dict:
    key = jax.random.key(seed)
    ks = jax.random.split(key, 40)
    f32 = jnp.float32
    D, H, N = D_MODEL, RWKV_HEADS, RWKV_HEAD
    NA, NB = N_A_LAYERS, N_B_LAYERS
    n_pages = PAST_LEN // PAGE_SIZE
    n_used = DEC_BATCH * n_pages
    n_pool = n_used + n_used // 4

    def nrm(i, shape, scale):
        return jax.random.normal(ks[i], shape, f32) * scale

    page_table = jax.random.permutation(ks[4], n_pool)[:n_used].reshape(DEC_BATCH, n_pages).astype(jnp.int32)
    w_rkv = nrm(8, (NA, 3, D, D), D ** -0.5) * jnp.array([1.0, 1.0, DEEPNORM_BETA], f32)[None, :, None, None]
    w_kv = nrm(22, (D, QK_WIDTH + V_WIDTH), D ** -0.5) * jnp.concatenate(
        [jnp.ones((QK_WIDTH,), f32), jnp.full((V_WIDTH,), DEEPNORM_BETA, f32)])
    post_ln = jnp.stack([1.0 + nrm(33, (DEPTH, 2, D), 0.05), nrm(34, (DEPTH, 2, D), 0.01)], axis=2)
    return {
        'x_prompt': nrm(0, (BATCH, SEQ, D), 1.0),
        'x_sample': nrm(1, (DEC_BATCH, DEC_SEQ, D), 1.0),
        'cache_k': nrm(2, (n_pool, PAGE_SIZE, 2 * DIFF_HEADS, DIFF_HEAD), 1.0),
        'cache_v': nrm(3, (n_pool, PAGE_SIZE, DIFF_HEADS, 2 * DIFF_HEAD), 1.0),
        'page_table': page_table,
        'state_wkv': nrm(5, (DEC_BATCH, NA, H, N, N), 0.3),
        'state_shift': nrm(6, (DEC_BATCH, NA, D), 1.0),
        'meta_tokens': nrm(7, (N_META, D), 1.0),
        'rwkv_mix': jax.random.uniform(ks[9], (NA, 6, D), f32),
        'rwkv_w_rkv': w_rkv,
        'rwkv_decay_w0': jax.random.uniform(ks[10], (NA, D), f32, -5.0, -1.0),
        'rwkv_decay_w1': nrm(11, (NA, D, DECAY_LORA), D ** -0.5),
        'rwkv_decay_w2': nrm(12, (NA, DECAY_LORA, D), 0.3 * DECAY_LORA ** -0.5),
        'rwkv_a_w0': nrm(13, (NA, D), 0.1),
        'rwkv_a_w1': nrm(14, (NA, D, AAA_LORA), D ** -0.5),
        'rwkv_a_w2': nrm(15, (NA, AAA_LORA, D), 0.5 * AAA_LORA ** -0.5),
        'rwkv_g_w1': nrm(16, (NA, D, GATE_LORA), D ** -0.5),
        'rwkv_g_w2': nrm(17, (NA, GATE_LORA, D), GATE_LORA ** -0.5),
        'rwkv_kk_ka': jnp.stack([0.85 + nrm(18, (NA, D), 0.05), 1.0 + nrm(19, (NA, D), 0.05)], axis=1),
        'rwkv_r_k': nrm(20, (NA, H, N), 0.1),
        'rwkv_lnx': jnp.stack([1.0 + nrm(21, (NA, D), 0.05), nrm(35, (NA, D), 0.01)], axis=1),
        'rwkv_w_out': nrm(23, (NA, D, D), D ** -0.5 * DEEPNORM_BETA),
        'w_kv_shared': w_kv,
        'diff_w_q': nrm(24, (NB, D, QK_WIDTH), D ** -0.5),
        'diff_lambda': nrm(25, (NB, 4, DIFF_HEAD), 0.1),
        'diff_subln': 1.0 + nrm(26, (NB, 2 * DIFF_HEAD), 0.05),
        'diff_w_out': nrm(27, (NB, V_WIDTH, D), V_WIDTH ** -0.5 * DEEPNORM_BETA),
        'router_w': nrm(28, (D, N_EXPERTS), D ** -0.5),
        'router_b': nrm(29, (N_EXPERTS,), 0.01),
        'moe_w_gate': nrm(30, (DEPTH, N_EXPERTS, D, D_EXPERT), D ** -0.5),
        'moe_w_up': nrm(31, (DEPTH, N_EXPERTS, D, D_EXPERT), D ** -0.5),
        'moe_w_down': nrm(32, (DEPTH, N_EXPERTS, D_EXPERT, D), D_EXPERT ** -0.5 * DEEPNORM_BETA),
        'post_ln': post_ln,
    }

def reference(x_prompt, x_sample, cache_k, cache_v, page_table, state_wkv, state_shift, meta_tokens,
              rwkv_mix, rwkv_w_rkv, rwkv_decay_w0, rwkv_decay_w1, rwkv_decay_w2, rwkv_a_w0, rwkv_a_w1,
              rwkv_a_w2, rwkv_g_w1, rwkv_g_w2, rwkv_kk_ka, rwkv_r_k, rwkv_lnx, rwkv_w_out, w_kv_shared,
              diff_w_q, diff_lambda, diff_subln, diff_w_out, router_w, router_b, moe_w_gate, moe_w_up,
              moe_w_down, post_ln):
    def run(x, wkv_in, shift_in, k_past, v_past):
        new_wkv, new_shift = [], []
        k_new = v_new = k_all = v_all = None
        for l in range(DEPTH):
            if l < N_A_LAYERS:
                h, s_out, x_last = _rwkv7_time_mix(
                    x, wkv_in[:, l], shift_in[:, l], rwkv_mix[l], rwkv_w_rkv[l], rwkv_decay_w0[l],
                    rwkv_decay_w1[l], rwkv_decay_w2[l], rwkv_a_w0[l], rwkv_a_w1[l], rwkv_a_w2[l],
                    rwkv_g_w1[l], rwkv_g_w2[l], rwkv_kk_ka[l], rwkv_r_k[l], rwkv_lnx[l], rwkv_w_out[l])
                new_wkv.append(s_out)
                new_shift.append(x_last)
            else:
                j = l - N_A_LAYERS
                h = _diff_attn_layer(x, k_all, v_all, diff_w_q[j], diff_lambda[j], diff_subln[j],
                                     diff_w_out[j], _lambda_init(l))
            x = _layernorm(DEEPNORM_ALPHA * x + h, post_ln[l, 0, 0], post_ln[l, 0, 1])
            x = _layernorm(DEEPNORM_ALPHA * x + _moe(x, router_w, router_b, moe_w_gate[l], moe_w_up[l], moe_w_down[l]),
                           post_ln[l, 1, 0], post_ln[l, 1, 1])
            if l == N_A_LAYERS - 1:
                k_new, v_new = _shared_kv(x, w_kv_shared)
                if k_past is None:
                    k_all, v_all = k_new, v_new
                else:
                    k_all = jnp.concatenate([k_past, k_new.astype(k_past.dtype)], axis=1)
                    v_all = jnp.concatenate([v_past, v_new.astype(v_past.dtype)], axis=1)
        return x, k_new, v_new, jnp.stack(new_wkv, axis=1), jnp.stack(new_shift, axis=1)

    B = x_prompt.shape[0]
    meta = jnp.broadcast_to(meta_tokens[None].astype(x_prompt.dtype), (B, N_META, D_MODEL))
    xp = jnp.concatenate([meta, x_prompt], axis=1)
    wkv0 = jnp.zeros((B, N_A_LAYERS, RWKV_HEADS, RWKV_HEAD, RWKV_HEAD), x_prompt.dtype)
    shift0 = jnp.zeros((B, N_A_LAYERS, D_MODEL), x_prompt.dtype)
    yp, new_k_prompt, new_v_prompt, new_wkv_prompt, new_shift_prompt = run(xp, wkv0, shift0, None, None)
    y_prompt = yp[:, N_META:]

    DB, n_pages = page_table.shape
    past = n_pages * cache_k.shape[1]
    k_past = cache_k[page_table].reshape(DB, past, 2 * DIFF_HEADS, DIFF_HEAD)
    v_past = cache_v[page_table].reshape(DB, past, DIFF_HEADS, 2 * DIFF_HEAD)
    y_sample, new_k_sample, new_v_sample, new_wkv_sample, new_shift_sample = run(
        x_sample, state_wkv, state_shift, k_past, v_past)
    return (y_prompt, y_sample, new_k_prompt, new_v_prompt, new_wkv_prompt, new_shift_prompt,
            new_k_sample, new_v_sample, new_wkv_sample, new_shift_sample)


_drawn_inputs = setup_inputs


def setup_inputs(seed=0):
    import zlib

    import numpy as np

    out = dict(_drawn_inputs(seed))
    spreads = {}
    factors = {'rwkv_decay_w1': 3.011, 'rwkv_decay_w2': 3.056, 'diff_subln': 2.694}
    for name, (base, spread) in spreads.items():
        noise = np.random.default_rng([zlib.crc32(name.encode()), seed]).standard_normal(out[name].shape)
        drawn = base * np.exp(spread * noise) if base else spread * noise
        out[name] = __import__('jax').numpy.asarray(drawn.astype(out[name].dtype))
    for name, factor in factors.items():
        out[name] = (out[name] * factor).astype(out[name].dtype)
    return out
```

```python
from contextlib import ExitStack
import math

import numpy as np

import concourse.bass as bass
from concourse import mybir

ALU = mybir.AluOpType
ACT = mybir.ActivationFunctionType
AX = mybir.AxisListType.X
F32 = mybir.dt.float32
I32 = mybir.dt.int32
U32 = mybir.dt.uint32

P = 128
D = 1024
NC = D // P
N_META, SEQ = 16, 256
TP = N_META + SEQ
SB, SS = 8, 8
TS = SB * SS
T = TP + TS
H, N = 16, 64
C = 64
NFULL = TP // C
LEVELS = 6
NH = 8
PAGE, NPG = 128, 2
E_, G_, F_ = 16, 4, 512
NF = F_ // P
PAIRS = E_ // 2
CAP = 64
NBLK = -(-T // CAP)
ALPHA = 4.0 ** 0.25
KAPPA = math.exp(-0.5)
LI = 0.8 - 0.6 * math.exp(-0.3)
BIG = 1e30
TOK = [(0, 128), (128, 128), (256, T - 256)]
KTILE = [(0, 128), (128, 128), (256, TP - 256), (TP, TS)]
SLOT, NSLOT = 4096, 6
L_RKV, L_WO, L_MOE0, L_KV, L_Q, L_DO, L_MOE1 = 0, 6, 8, 56, 60, 62, 64


CHAINS = {
    "stage_mm": (("rkv_mm", 24), ("lora_mm", 3), ("lz_mm", 16), ("kks_mm", 8), ("nat_in_mm", 8), ("ss_mm", 16),
                 ("wkvp_mm", 2), ("wkvs_mm", 8), ("gn_mm", 8), ("gn_vm", 8), ("bn_mm", 8), ("g_mm", 8)),
    "stage_act": (("rkv_ev", 24), ("lora_ev", 3), ("lz_ev", 16), ("kksq_ready", 8), ("kks_ev", 8), ("nat_ev", 8),
                  ("wkvp_ready", 2), ("wkvs_ready", 8), ("gn_sq", 8), ("gn_s", 8)),
    "stage_dve": (("mix_ready", 48), ("kk_ready", 8), ("gn_c", 8), ("rkr_ready", 8), ("bn_ev", 8), ("z_ready", 8)),
    "kv_mm": (("ktr_mm", 8), ("vtr_mm", 8), ("sl_mm", 8)),
    "kv_dve": (("ktm_ready", 8), ("vtm_ready", 8), ("z2_ready", 8)),
    "sub_act": (("sl_sq", 8), ("sl_s", 8)),
}
SHARED = {stage: (name, sum(k for _, k in chain[:i])) for name, chain in CHAINS.items()
          for i, (stage, _) in enumerate(chain)}


CHUNK_PRIMED = {"pe": ("o_mm", "sa_mm"), "act": ("o_ready", "sa_ready"), "dve": ("u_ready", "ops_ready")}
BLOCK_PRIMED = {
    "pe": ("ga_mm", "gb_mm", "gate_mm", "up_mm", "sgt_mm", "down_mm", "yta_mm", "ytb_mm", "sc_mm"),
    "act": ("xga_ready", "hs_ready", "yt_ready", "ya_ready"),
    "dve": ("sel_ready", "xgb_ready", "h_ready", "sg_ready", "y_ready_", "add_done"),
}
PER_BLOCK = {"gate_mm": 2, "up_mm": 2, "down_mm": 2, "sc_mm": 8, "hs_ready": 2, "yt_ready": 2, "h_ready": 2,
             "add_done": 8}
PRIMED = {name for t in (CHUNK_PRIMED, BLOCK_PRIMED) for names in t.values() for name in names}


def after(stage, n):
    return n + (SHARED[stage][1] if stage in SHARED else 1 if stage in PRIMED else 0)


def constants():
    p = np.arange(P)[:, None]
    q = np.arange(P)[None, :]
    c64 = np.arange(64)[None, :]
    s, t = p % 64, c64
    parts = {}
    parts["ident"] = (p == q)
    parts["onesd"] = np.full((P, P), 1.0 / D)
    parts["ones"] = np.ones((P, P))
    parts["bones"] = (p // 64 == q // 64)
    parts["eps"] = np.concatenate([np.full((P, 1), 1e-5), np.full((P, 1), 64e-5)], 1)
    parts["maskp"] = np.concatenate([s <= t, s < t], 1)
    same = s // SS == t // SS
    parts["masks"] = np.concatenate([(s <= t) & same, (s < t) & same], 1)
    scan = np.ones(T)
    scan[0:TP:C] = 0
    scan[TP::SS] = 0
    parts["scan"] = np.tile(scan, (P, 1))
    parts["bm"] = (s // SS == np.arange(SB)[None, :])
    low = [((s // (2 * m) == t // (2 * m)) & (s % (2 * m) >= m) & (t % (2 * m) < m)) for m in (1, 2, 4, 8, 16, 32)]
    up = [((s // (2 * m) == t // (2 * m)) & (t % (2 * m) >= m) & (s % (2 * m) < m)) for m in (1, 2, 4, 8, 16, 32)]
    parts["low"] = np.concatenate(low, 1)
    parts["up"] = np.concatenate(up, 1)
    parts["ustrict"] = (p < q)
    parts["iota"] = np.tile(np.arange(CAP), (P, 1))
    parts["w16"] = np.tile(np.arange(E_, 0, -1), (P, 1))
    parts["w4"] = np.tile(np.arange(G_, 0, -1), (P, 1))
    parts["valid"] = np.concatenate([p < n for _, n in TOK], 1)
    parts["caus"] = np.where(q > p, -BIG, 0.0)
    win = np.arange(2 * TS - SS)[None, :] - (TS - SS)
    parts["win"] = np.where((win >= 0) & (win <= p % SS), 0.0, -BIG)
    parts["odd"] = (p // SS) % 2
    at, out = {}, []
    n = 0
    for k, v in parts.items():
        at[k] = (n, v.shape[1])
        n += v.shape[1]
        out.append(np.broadcast_to(v, v.shape).astype(np.float32))
    return np.ascontiguousarray(np.concatenate(out, 1)), at


def build(nc, I, O, const, at):
    ctx = ExitStack()
    with ctx:
        sems = {}

        def S(name):
            name = SHARED.get(name, (name, 0))[0]
            if name not in sems:
                sems[name] = ctx.enter_context(nc.semaphore(name))
            return sems[name]

        A = ctx.enter_context(nc.sbuf_tensor("arena", [P, 53184], F32))
        ps = ctx.enter_context(nc.psum_tensor("ps", [P, 8, 512], F32))
        cnt_i = ctx.enter_context(nc.sbuf_tensor("cnt_i", [1, PAIRS], I32))
        pt_i = ctx.enter_context(nc.sbuf_tensor("pt_i", [1, SB * NPG], I32))

        top = [0]

        def cut(n, where=None):
            if where is not None:
                return A[:, where:where + n]
            v = A[:, top[0]:top[0] + n]
            top[0] += n
            assert top[0] <= 53184, top
            return v

        cut(NSLOT * SLOT)

        def slot(n):
            return A[:, (n % NSLOT) * SLOT:(n % NSLOT + 1) * SLOT]

        def w_in(n):
            return slot(n).rearrange("p (k n) -> p k n", k=NC)

        def w_down(n):
            return slot(n).rearrange("p (k n) -> p k n", k=NF)

        def landed(n):
            return 16 * (n // NSLOT + 1)

        def chan(v):
            return v.rearrange("p (c t) -> p c t", c=NC)

        xT = chan(cut(NC * T))
        c0 = at["maskp"][0]
        common = cut(c0)
        par = cut(104 + 65)
        ssT = cut(64)
        oneka = cut(8)

        def cst(name, n=None):
            o, w = at[name]
            return common[:, o:o + w]

        ident, onesd, ones, bones = cst("ident"), cst("onesd"), cst("ones"), cst("bones")
        eps_ln, eps_lnx = common[:, at["eps"][0]:at["eps"][0] + 1], common[:, at["eps"][0] + 1:at["eps"][0] + 2]
        mixv = [par[:, 8 * i:8 * i + 8] for i in range(6)]
        dw0, aw0, kk0, ka, rkv_, lnx0, lnx1 = [par[:, 48 + 8 * i:56 + 8 * i] for i in range(7)]
        plv = [[[par[:, 104 + 8 * (4 * l + 2 * j + k):112 + 8 * (4 * l + 2 * j + k)] for k in range(2)]
                for j in range(2)] for l in range(2)]
        subv = par[:, 168:169]
        base = top[0]

        rT, kT_, vT_, sgT, T1, T2, T3 = [chan(cut(NC * T)) for _ in range(7)]
        lora0 = top[0]
        dw1 = cut(512).rearrange("p (k n) -> p k n", k=NC)
        aw1 = cut(512).rearrange("p (k n) -> p k n", k=NC)
        gw1 = cut(1024).rearrange("p (k n) -> p k n", k=NC)
        dw2, aw2 = cut(1024), cut(1024)
        gw2 = cut(1024)
        hg = cut(T)
        hw, ha = cut(T)[0:64, :], cut(T)[0:64, :]
        XI, XU, YI, LM = [cut(1024, lora0 + 1024 * i)[0:64, :].rearrange("p (h s) -> p h s", h=H) for i in range(4)]
        o = SLOT
        nR = at["ustrict"][0] - c0
        rconst = cut(nR, o)

        def rc(name):
            a, w = at[name]
            return rconst[:, a - c0:a - c0 + w]

        STZ = cut(1024, o + 2048).rearrange("p (c n) -> p c n", c=NC)
        QW = cut(1024, o + 3072).rearrange("p (c n) -> p c n", c=NC)
        o = 2 * SLOT
        RAV = cut(NC * 192, o).rearrange("p (c n) -> p c n", c=NC)
        BK = cut(NC * 128, o + 1536).rearrange("p (c n) -> p c n", c=NC)
        EX = [cut(512, o + 2560 + 512 * i).rearrange("p (c n) -> p c n", c=NC) for i in range(3)]
        o = 3 * SLOT
        SAV = cut(1024, o).rearrange("p (h n) -> p h n", h=H)
        BKt = cut(1024, o + 1024).rearrange("p (c n) -> p c n", c=NC)
        GH = cut(2048, o + 2048).rearrange("p (h n) -> p h n", h=H)
        STS = cut(4096, 4 * SLOT).rearrange("p (c b n) -> p c b n", c=NC, b=SB)
        NAT = [cut(1024, 5 * SLOT + 1024 * i) for i in range(2)]
        U = cut(1024, 5 * SLOT + 2048)[0:64, :].rearrange("p (h n) -> p h n", h=H)
        MV = cut(1024, 5 * SLOT + 3072)[0:64, :].rearrange("p (h n) -> p h n", h=H)
        QS = NAT[0].rearrange("p (c w t) -> p c w t", c=NC, w=2)
        SAVB = [cut(512, 2 * SLOT + 3072 + 512 * i).rearrange("p (b n) -> p b n", b=SB) for i in range(2)]

        top[0] = base
        YA = chan(cut(NC * T))
        CT = chan(cut(NC * T))
        SQ = chan(cut(NC * T))
        assert top[0] <= base + 3 * NC * T
        RS = cut(T)
        XTM = cut(3 * D).rearrange("p (t n) -> p t n", t=3)
        SelM = cut(3 * 2 * CAP).rearrange("p (a n) -> p a n", a=6)
        SelG = cut(3 * 2 * CAP).rearrange("p (a n) -> p a n", a=6)
        SG = cut(T)
        Xg = cut(D).rearrange("p (c n) -> p c n", c=NC)
        HS = cut(512).rearrange("p (e n) -> p e n", e=2)
        HH = cut(512).rearrange("p (e f n) -> p e f n", e=2, f=NF)
        YT = cut(D).rearrange("p (c n) -> p c n", c=NC)
        YY = cut(D)
        rw = cut(NC * E_).rearrange("p (c n) -> p c n", c=NC)
        rbB = cut(E_)
        mconst0 = at["ustrict"][0]
        nM = at["caus"][0] - mconst0
        mconst = cut(nM)

        def mc(name):
            a, w = at[name]
            return mconst[:, a - mconst0:a - mconst0 + w]

        rt = [cut(48) for _ in range(8)]
        pr6 = cut(72).rearrange("p (g n) -> p g n", g=12)
        gs = [cut(12) for _ in range(4)]
        rank3 = cut(48).rearrange("p (t n) -> p t n", t=3)
        gate3 = cut(48).rearrange("p (t n) -> p t n", t=3)
        cntf = cut(16)
        cntp = cut(8)
        rkp, gtp = cut(6), cut(6)
        top[0] = base
        aKT, aQT, aOT = [chan(cut(NC * T)) for _ in range(3)]
        assert top[0] == base + 3 * NC * T
        aVT = aOT
        VTM = cut(4 * D).rearrange("p (t n) -> p t n", t=4)
        KTM0 = top[0]
        KTM = cut(4 * D).rearrange("p (t n) -> p t n", t=4)
        PGK = [cut(2048, KTM0), cut(2048)]
        PGV = [cut(2048, KTM0 + 2048), cut(2048)]
        PGK = [v.rearrange("p (g n) -> p g n", g=2) for v in PGK]
        PGV = [v.rearrange("p (g n) -> p g n", g=2) for v in PGV]
        k0_ = top[0]
        KTs = cut(2048).rearrange("p (c n) -> p c n", c=NC)
        PP = [cut(544, k0_ + 544 * i).rearrange("p (j n) -> p j n", j=2) for i in range(2)]
        AT = [cut(384, k0_ + 1088 + 384 * i).rearrange("p (k n) -> p k n", k=3) for i in range(2)]
        Qbd = cut(1168)
        PS = cut(320)
        ATs = cut(192).rearrange("p (k n) -> p k n", k=3)
        aconst0 = at["caus"][0]
        aconst = cut(const.shape[1] - aconst0)

        def ac(name):
            a, w = at[name]
            return aconst[:, a - aconst0:a - aconst0 + w]

        lamt = cut(256)
        lamp = cut(128)
        lams = cut(8)
        st4 = [cut(8) for _ in range(2)]
        aRS = cut(T, k0_)
        aSQ = chan(cut(NC * T, KTM0))
        OUTT = A[:, base:base + 3 * D].rearrange("p (t n) -> p t n", t=3)

        def bank(b, n=512):
            return ps[:, b, 0:n]

        def heads(v):
            return v

        pw = [(0, 112), (112, 112), (224, 32)]

        block = ctx.enter_context(nc.Block())
        xp_rows = I["x_prompt"][0]
        xs_rows = I["x_sample"].rearrange("b s d -> (b s) d")

        def prime(eng, who):
            for name in CHUNK_PRIMED[who]:
                eng.sem_inc(S(name), 1)
            for name in BLOCK_PRIMED[who]:
                eng.sem_inc(S(name), 1)
                eng.sem_inc(S("o_" + name), 1)

        def apart(eng):
            eng.sem_inc(S("apart"), 1)

        def pair_engine(eng, i, g, who, block):
            def skip(k, n):
                for name in BLOCK_PRIMED[who]:
                    eng.wait_ge(S("o_" + name), after(name, PER_BLOCK.get(name, 1) * n))
                    eng.sem_inc(S("o_" + name), PER_BLOCK.get(name, 1) * k)

            cnt = eng.value_load(cnt_i[0:1, bass.ds(i, 1)], min_val=0, max_val=T)
            more = NBLK - 1
            with eng.If(cnt > CAP):
                with eng.Fori(1, NBLK) as b:
                    with eng.If(cnt > b * CAP):
                        block("o_", more * g + b - 1)
                    with eng.Else():
                        skip(1, more * g + b - 1)
            with eng.Else():
                skip(more, more * g)
            block("", g)

        @block.sync
        def _(sp):
            def load(n, src):
                sp.dma_start(w_in(n) if src.shape[0] == D else w_down(n),
                             src.rearrange("(k p) n -> p k n", p=P)).then_inc(S(f"w_full{n % NSLOT}"), 16)

            wrkv = I["rwkv_w_rkv"][0]
            for i in range(3):
                for j in range(2):
                    load(L_RKV + 2 * i + j, wrkv[i][:, 512 * j:512 * j + 512])
            wout = I["rwkv_w_out"][0]
            sp.wait_ge(S("rkv_mm"), after("rkv_mm", 4))
            load(L_WO, wout[:, 0:512])
            sp.wait_ge(S("out_wkvp"), 32)
            sp.wait_ge(S("out_wkvs0"), 64)
            sp.wait_ge(S("out_wkvs1"), 64)
            load(L_WO + 1, wout[:, 512:1024])

            def experts(layer, n0):
                wg, wu, wd = I["moe_w_gate"][layer], I["moe_w_up"][layer], I["moe_w_down"][layer]
                names = ("gate_mm", "up_mm", "down_mm")
                for first, count in ((True, 1), (False, PAIRS - 1)):
                    def body(i):
                        for e in range(2):
                            for k, w in enumerate((wg, wu, wd)):
                                j = 3 * e + k
                                if first:
                                    n = n0 + j
                                    if layer == 0 and j >= 4:
                                        sp.wait_ge(S("proj_mm"), 4 * (j - 3))
                                    if layer == 1 and j < 4:
                                        sp.wait_ge(S("proj_mm"), 8 + 4 * ((2, 3, 4, 5)[j] + 1))
                                    if layer == 1 and j >= 4:
                                        sp.wait_ge(S("proj_mm"), 8 + 24 + 4 * (j - 3))
                                else:
                                    sp.wait_ge(S(names[k]), after(names[k], 2 * (PAIRS * layer + i - 1) + e + 1))
                                src = w[bass.ds(2 * i + e, 1)] if not first else w[e:e + 1]
                                sp.dma_start(w_in(n0 + j) if k < 2 else w_down(n0 + j),
                                             src.rearrange("a (k p) n -> p (a k) n", p=P)
                                             ).then_inc(S(f"w_full{(n0 + j) % NSLOT}"), 16)
                    if first:
                        body(0)
                    else:
                        with sp.Fori(1, PAIRS) as i:
                            body(i)

            experts(0, L_MOE0)
            wkv = I["w_kv_shared"]
            g = 2 * PAIRS
            last = [("gate_mm", g - 1), ("up_mm", g - 1), ("down_mm", g - 1), ("gate_mm", g), ("up_mm", g), ("down_mm", g)]
            for j in range(4):
                sp.wait_ge(S(last[j][0]), after(*last[j]))
                load(L_KV + j, wkv[:, 512 * j:512 * j + 512])
            for j in range(2):
                sp.wait_ge(S(last[4 + j][0]), after(*last[4 + j]))
                load(L_Q + j, I["diff_w_q"][0][:, 512 * j:512 * j + 512])
            for j in range(2):
                sp.wait_ge(S("proj_mm"), 8 + 4 * (j + 1))
                load(L_DO + j, I["diff_w_out"][0][:, 512 * j:512 * j + 512])
            experts(1, L_MOE1)

        @block.gpsimd
        def _(pool):
            def ld(dst, src, name):
                pool.dma_start(dst, src).then_inc(S(name), 16)

            cd = I["const"]
            ld(common, cd[:, 0:c0], "in_common")
            rows = T3.rearrange("p c t -> p (c t)")
            xrow = A[:, base:base + 3 * D].rearrange("p (t n) -> p t n", t=3)
            prow = A[:, base + 3 * D:base + 3 * D + 128]
            prow2 = A[:, base + 3 * D + 128:base + 3 * D + 256]
            srow = A[:, base + 3 * D + 256:base + 3 * D + 384]
            ld(xrow[0:N_META, 0, :], I["meta_tokens"], "in_x")
            ld(xrow[N_META:P, 0, :], xp_rows[0:P - N_META, :], "in_x")
            ld(xrow[:, 1, :], xp_rows[P - N_META:2 * P - N_META, :], "in_x")
            ld(xrow[0:16, 2, :], xp_rows[2 * P - N_META:SEQ, :], "in_x")
            ld(xrow[16:80, 2, :], xs_rows, "in_x")
            ld(prow[0:48, :], I["rwkv_mix"][0].rearrange("i (c p) -> (i c) p", p=P), "in_par")
            ld(prow[48:56, :], I["rwkv_decay_w0"][0].rearrange("(c p) -> c p", p=P), "in_par")
            ld(prow[56:64, :], I["rwkv_a_w0"][0].rearrange("(c p) -> c p", p=P), "in_par")
            ld(prow[64:80, :], I["rwkv_kk_ka"][0].rearrange("i (c p) -> (i c) p", p=P), "in_par")
            ld(prow[80:88, :], I["rwkv_r_k"][0].rearrange("(c h) n -> c (h n)", h=2), "in_par")
            ld(prow[88:104, :], I["rwkv_lnx"][0].rearrange("i (c p) -> (i c) p", p=P), "in_par")
            ld(prow2[0:64, :], I["post_ln"].rearrange("l j k (c p) -> (l j k c) p", p=P), "in_par")
            ld(prow2[64:65, :], I["diff_subln"], "in_par")
            ld(srow[0:64, :], I["state_shift"].rearrange("b a (c p) -> (b a c) p", p=P), "in_par")
            ld(dw1, I["rwkv_decay_w1"][0].rearrange("(k p) n -> p k n", p=P), "in_lora")
            ld(aw1, I["rwkv_a_w1"][0].rearrange("(k p) n -> p k n", p=P), "in_lora")
            ld(gw1, I["rwkv_g_w1"][0].rearrange("(k p) n -> p k n", p=P), "in_lora")
            ld(dw2[0:64, :], I["rwkv_decay_w2"][0], "in_lora")
            ld(aw2[0:64, :], I["rwkv_a_w2"][0], "in_lora")
            ld(gw2, I["rwkv_g_w2"][0], "in_lora")
            ld(O["new_shift_prompt"][0], I["x_prompt"][0, SEQ - 1:SEQ, :], "out")
            ld(O["new_shift_sample"].rearrange("b a d -> (b a) d"), I["x_sample"][:, SS - 1, :], "out")
            pool.wait_ge(S("rkv_mm"), after("rkv_mm", 8))
            ld(rconst, cd[:, c0:c0 + nR], "in_rconst")
            pool.wait_ge(S("rkv_mm"), after("rkv_mm", 24))
            sw = I["state_wkv"]
            for bp in range(4):
                if bp >= 2:
                    pool.wait_ge(S("nat_in_mm"), after("nat_in_mm", 2 * (bp - 1)))
                for e in range(2):
                    ld(NAT[bp % 2][64 * e:64 * e + 64, :].rearrange("p (h j) -> p h j", h=H),
                       sw[2 * bp + e, 0].rearrange("h i j -> i h j"), f"in_nat{bp % 2}")
            pool.wait_ge(S("wkvp_ready"), after("wkvp_ready", 2))
            for hp in range(2):
                pool.dma_start(O["new_wkv_prompt"][0, 0].rearrange("(c e) i j -> e i c j", e=2)[hp],
                               QW[64 * hp:64 * hp + 64, :, 64 * hp:64 * hp + 64]).then_inc(S("out_wkvp"), 16)
            for bp in range(4):
                pool.wait_ge(S("wkvs_ready"), after("wkvs_ready", 2 * (bp + 1)))
                for e in range(2):
                    pool.dma_start(O["new_wkv_sample"][2 * bp + e, 0].rearrange("h i j -> i h j"),
                                   NAT[bp % 2][64 * e:64 * e + 64, :].rearrange("p (h j) -> p h j", h=H)
                                   ).then_inc(S(f"out_wkvs{bp % 2}"), 16)
            pool.wait_ge(S("x_ready"), 8)
            ld(mconst, cd[:, mconst0:mconst0 + nM], "in_mconst")
            ld(rw, I["router_w"].rearrange("(c p) n -> p c n", p=P), "in_mconst")
            ld(rbB, I["router_b"].unsqueeze(0).to_broadcast([P, E_]), "in_mconst")
            pool.wait_ge(S("x_ready"), 16)
            ld(aconst, cd[:, aconst0:const.shape[1]], "in_aconst")
            ld(lamt, I["diff_lambda"][0].rearrange("i n -> (i n)").unsqueeze(0).to_broadcast([P, 256]), "in_aconst")
            ld(pt_i[:, :], I["page_table"].rearrange("b n -> (b n)").unsqueeze(0), "in_pt")
            for name, ready, tile in (("k", "ktm_ready", KTM), ("v", "vtm_ready", VTM)):
                op = O[f"new_{name}_prompt"][0].rearrange("t h n -> t (h n)")
                os_ = O[f"new_{name}_sample"].rearrange("b s h n -> (b s) (h n)")
                pool.wait_ge(S(ready), after(ready, 8))
                for t, (t0, n) in enumerate(KTILE):
                    dst = op[t0:t0 + n, :] if t < 3 else os_
                    pool.dma_start(dst, tile[0:n, t, :]).then_inc(S(f"out_{name}tm"), 16)
            pool.wait_ge(S("in_pt"), 16)
            pool.wait_ge(S("out_ktm"), 64)
            for b in range(SB):
                if b >= 2:
                    pool.wait_ge(S("past_mm"), b - 1)
                for g in range(NPG):
                    pg = pool.value_load(pt_i[0:1, NPG * b + g:NPG * b + g + 1], min_val=0,
                                         max_val=I["cache_k"].shape[0] - 1)
                    ck = I["cache_k"].rearrange("a p h n -> a p (h n)")
                    cv = I["cache_v"].rearrange("a p h n -> a p (h n)")
                    pool.dma_start(PGK[b % 2][:, g, :], ck[bass.ds(pg, 1)].rearrange("a p n -> p (a n)")
                                   ).then_inc(S(f"in_pg{b % 2}"), 16)
                    pool.dma_start(PGV[b % 2][:, g, :], cv[bass.ds(pg, 1)].rearrange("a p n -> p (a n)")
                                   ).then_inc(S(f"in_pg{b % 2}"), 16)
            pool.wait_ge(S("x_ready"), 24)
            ld(mconst, cd[:, mconst0:mconst0 + nM], "in_mconst")
            ld(rw, I["router_w"].rearrange("(c p) n -> p c n", p=P), "in_mconst")
            ld(rbB, I["router_b"].unsqueeze(0).to_broadcast([P, E_]), "in_mconst")
            pool.wait_ge(S("y_rows"), 6)
            yp = O["y_prompt"][0]
            ld(yp[0:128, :], OUTT[:, 0, :], "out")
            ld(yp[128:256, :], OUTT[:, 1, :], "out")
            ld(O["y_sample"].rearrange("b s d -> (b s) d"), OUTT[0:64, 2, :], "out")
            pool.wait_ge(S("out"), 16 * 5)
            pool.wait_ge(S("out_wkvp"), 32)
            pool.wait_ge(S("out_wkvs0"), 64)
            pool.wait_ge(S("out_wkvs1"), 64)
            pool.wait_ge(S("out_ktm"), 64)
            pool.wait_ge(S("out_vtm"), 64)


        @block.tensor
        def _(pe):
            prime(pe, "pe")
            def mm(out, lhsT, rhs, start=True, stop=True):
                return pe.matmul(out, lhsT, rhs, start=start, stop=stop)

            def wait_w(n, more=0):
                pe.wait_ge(S(f"w_full{n % NSLOT}"), landed(n) + more)

            pe.wait_ge(S("in_common"), 16)
            pe.wait_ge(S("in_par"), 16 * 9)
            prow = A[:, base + 3 * D:base + 3 * D + 128]
            prow2 = A[:, base + 3 * D + 128:base + 3 * D + 256]
            srow = A[:, base + 3 * D + 256:base + 3 * D + 384]
            xrow = A[:, base:base + 3 * D].rearrange("p (t n) -> p t n", t=3)
            pe.transpose(ps[:, 0, 0:104], prow[0:104, :], ident[0:104, 0:104])
            pe.transpose(ps[:, 0, 128:193], prow2[0:65, :], ident[0:65, 0:65])
            pe.transpose(ps[:, 0, 256:320], srow[0:64, :], ident[0:64, 0:64]).then_inc(S("par_mm"), 1)
            pe.wait_ge(S("in_x"), 16 * 5)
            for t, (t0, n) in enumerate(TOK):
                for hf in range(2):
                    for c in range(4):
                        i = pe.transpose(ps[:, 1 + 2 * t + hf, n * c:n * c + n],
                                         xrow[0:n, t, P * (4 * hf + c):P * (4 * hf + c) + P], ident[0:n, 0:n])
                    i.then_inc(S("xt_mm"), 1)

            for i, X in enumerate((T1, T2, T3)):
                for co in range(NC):
                    n = 8 * i + co
                    w = w_in(L_RKV + 2 * i + co // 4)
                    wait_w(L_RKV + 2 * i + co // 4)
                    if n >= 4:
                        pe.wait_ge(S("rkv_ev"), after("rkv_ev", n - 3))
                    for k in range(NC):
                        if co == 0:
                            pe.wait_ge(S("mix_ready"), after("mix_ready", 8 * i + k + 1))
                        m = mm(bank(n % 4, T), w[:, k, P * (co % 4):P * (co % 4) + P], X[:, k, :], k == 0, k == NC - 1)
                    m.then_inc(S("rkv_mm"), 1)
            pe.wait_ge(S("in_lora"), 96)
            for i, (w, X, M) in enumerate(((dw1, T1, 64), (aw1, T2, 64), (gw1, T3, 128))):
                pe.wait_ge(S("mix_ready"), after("mix_ready", 8 * (i + 4)))
                for k in range(NC):
                    m = mm(ps[0:M, 4 + i, 0:T], w[:, k, :], X[:, k, :], k == 0, k == NC - 1)
                m.then_inc(S("lora_mm"), 1)
            pe.wait_ge(S("lora_ev"), after("lora_ev", 3))
            for i, (w, X) in enumerate(((dw2, hw), (aw2, ha))):
                for co in range(NC):
                    n = 8 * i + co
                    if n >= 4:
                        pe.wait_ge(S("lz_ev"), after("lz_ev", n - 3))
                    mm(bank(4 + n % 4, T), w[0:64, P * co:P * co + P], X).then_inc(S("lz_mm"), 1)
            pe.wait_ge(S("rkv_ev"), after("rkv_ev", 24))
            for c in range(NC):
                pe.wait_ge(S("kksq_ready"), after("kksq_ready", c + 1))
                if c >= 4:
                    pe.wait_ge(S("kks_ev"), after("kks_ev", c - 3))
                mm(bank(c % 4, T), bones, T2[:, c, :]).then_inc(S("kks_mm"), 1)
            pe.wait_ge(S("lz_ev"), after("lz_ev", 16))
            for bp in range(4):
                pe.wait_ge(S(f"in_nat{bp % 2}"), 32 * (bp // 2 + 1))
                for hf in range(2):
                    n = 2 * bp + hf
                    if n >= 4:
                        pe.wait_ge(S("nat_ev"), after("nat_ev", n - 3))
                    for c in range(4):
                        m = pe.transpose(ps[:, 4 + n % 4, P * c:P * c + P],
                                         NAT[bp % 2][:, P * (4 * hf + c):P * (4 * hf + c) + P], ident)
                    m.then_inc(S("nat_in_mm"), 1)
            pe.wait_ge(S("nat_ev"), after("nat_ev", 8))
            pe.wait_ge(S("kks_ev"), after("kks_ev", 8))

            def chunk(n, sample):
                pe.wait_ge(S("ops_ready"), after("ops_ready", 1 * n + 1))
                pe.wait_ge(S("u_ready"), after("u_ready", 2 * n))
                for b, src, o0, name in ((0, BK, 0, "bkt_mm"), (2, RAV, 64, "avt_mm")):
                    for hf in range(2):
                        for c in range(4):
                            m = pe.transpose(ps[:, b + hf, P * c:P * c + P], src[:, 4 * hf + c, o0:o0 + P], ident)
                        m.then_inc(S(name), 1)
                pe.wait_ge(S("sa_ready"), after("sa_ready", 2 * n))
                pe.wait_ge(S("o_ready"), after("o_ready", 1 * n))
                pe.wait_ge(S("st_ready"), 1 * n + 1)
                for hp in range(2):
                    for hf in range(2):
                        for c in range(4):
                            q = slice(64 * hp, 64 * hp + 64)
                            m = mm(ps[:, 4 + 2 * hp + hf, P * c:P * c + P], BK[q, 4 * hf + c, :], RAV[q, 4 * hf + c, 0:128])
                        m.then_inc(S("gh_mm"), 1)
                pe.wait_ge(S("bkt_ready"), 2 * n + 2)
                apart(pe)
                for hp in range(2):
                    q = slice(64 * hp, 64 * hp + 64)
                    for c in range(NC):
                        m = mm(ps[0:64, hp, 64 * c:64 * c + 64], RAV[q, c, 64:128], BK[q, c, 0:64])
                    m.then_inc(S("l_mm"), 1)
                pe.wait_ge(S("sv_ready"), 2 * n + 2)
                apart(pe)
                for hp in range(2):
                    q = slice(64 * hp, 64 * hp + 64)
                    for c in range(NC):
                        m = mm(ps[0:64, 2 + hp, 64 * c:64 * c + 64], BK[q, c, 0:64], RAV[q, c, 64:128])
                    m.then_inc(S("lt_mm"), 1)
                pe.wait_ge(S("gh_ready"), 4 * n + 4)
                pe.wait_ge(S("lm_ready"), 2 * n + 2)
                levels = 2 if sample else LEVELS - 1
                for lv in range(1, levels + 1):
                    for hf in range(2):
                        if lv == 1:
                            pe.wait_ge(S("inv_ready"), 11 * n + 1)
                        else:
                            pe.wait_ge(S("inv_ready"), 11 * n + 1 + 2 * (lv - 2) + hf + 1)
                            pe.wait_ge(S("y_ready"), 10 * n + 2 * (lv - 2) + hf + 1)
                        apart(pe)
                        for h in range(8 * hf, 8 * hf + 8):
                            m = mm(ps[0:64, 4 + hf, 64 * (h % 8):64 * (h % 8) + 64], LM[:, h, :], XU[:, h, :])
                        m.then_inc(S("y_mm"), 1)
                    for hf in range(2):
                        pe.wait_ge(S("y_ready"), 10 * n + 2 * (lv - 1) + hf + 1)
                        apart(pe)
                        bx = (6, 7) if hf == 0 else (0, 1)
                        if lv < levels:
                            for h in range(8 * hf, 8 * hf + 8):
                                mm(ps[0:64, bx[0], 64 * (h % 8):64 * (h % 8) + 64], YI[:, h, :], XI[:, h, :])
                        for h in range(8 * hf, 8 * hf + 8):
                            m = mm(ps[0:64, bx[1], 64 * (h % 8):64 * (h % 8) + 64], XI[:, h, :], YI[:, h, :])
                        m.then_inc(S("xu_mm"), 1)
                    if lv == 1:
                        for hf in range(2):
                            for h in range(8 * hf, 8 * hf + 8):
                                m = mm(ps[0:64, 2 + hf, 64 * (h % 8):64 * (h % 8) + 64],
                                       GH[64:128, h, 64:128], SAV[64:128, h, :])
                            m.then_inc(S("mv_mm"), 1)
                pe.wait_ge(S("mv_ready"), 2 * n + 2)
                pe.wait_ge(S("inv_ready"), 11 * n + 2 * levels + 1)
                if sample:
                    for hp in range(2):
                        q = slice(64 * hp, 64 * hp + 64)
                        for hf in range(2):
                            for c in range(4):
                                ov = ps[q, 2 * hp + hf, P * c:P * c + P].rearrange("p (w t) -> p w t", w=2)
                                rv = RAV[q, 4 * hf + c, 0:128].rearrange("p (w t) -> p w t", w=2)
                                for b in range(SB):
                                    m = mm(ov[:, :, 8 * b:8 * b + 8], STS[q, 4 * hf + c, b, :], rv[:, :, 8 * b:8 * b + 8])
                            m.then_inc(S("qs_mm"), 1)
                    pe.wait_ge(S("qs_ready"), 4)
                    for hf in range(2):
                        for c in range(4):
                            m = pe.transpose(ps[0:64, 2 + hf, P * c:P * c + P], QS[:, 4 * hf + c, 1, :], ident)
                        m.then_inc(S("u_mm"), 1)
                else:
                    for hf in range(2):
                        for c in range(4):
                            m = mm(ps[0:64, 2 + hf, P * c:P * c + P], RAV[:, 4 * hf + c, 64:128], STZ[:, 4 * hf + c, :])
                        m.then_inc(S("u_mm"), 1)
                for hf in range(2):
                    pe.wait_ge(S("u_ready"), after("u_ready", 2 * n + hf + 1))
                    apart(pe)
                    for h in range(8 * hf, 8 * hf + 8):
                        m = mm(ps[0:64, 4 + hf, 64 * (h % 8):64 * (h % 8) + 64], XU[:, 8 * (h % 2) + h // 2, :], U[:, h, :])
                    m.then_inc(S("sa_mm"), 1)
                pe.wait_ge(S("sa_ready"), after("sa_ready", 2 * n + 2))
                for c in range(NC):
                    if not sample:
                        mm(ps[:, 6, 64 * c:64 * c + 64], STZ[:, c, :], RAV[:, c, 0:64], True, False)
                    for hp in range(2):
                        m = mm(ps[64 * hp:64 * hp + 64, 6, 64 * c:64 * c + 64], SAV[:, 2 * c + hp, :],
                               GH[:, 2 * c + hp, 0:64], sample, True)
                m.then_inc(S("o_mm"), 1)
                if not sample:
                    for c in range(NC):
                        for hp in range(2):
                            m = mm(ps[64 * hp:64 * hp + 64, 7, 64 * c:64 * c + 64], BKt[:, c, 64 * hp:64 * hp + 64],
                                   SAV[:, 2 * c + hp, :])
                    m.then_inc(S("st_mm"), 1)

            with pe.Fori(0, NFULL) as i:
                chunk(i, False)
            chunk(NFULL, False)
            chunk(NFULL + 1, True)
            for h in range(H):
                c, hp = h // 2, h % 2
                pe.wait_ge(S("savb_ready"), h + 1)
                if c >= 2:
                    pe.wait_ge(S("sts_ready"), c - 1)
                if h == 0:
                    pe.wait_ge(S("o_ready"), after("o_ready", NFULL + 2))
                mm(ps[64 * hp:64 * hp + 64, 6 + c % 2, :], BKt[:, c, 64 * hp:64 * hp + 64],
                   SAVB[h % 2].rearrange("p b n -> p (b n)")).then_inc(S("ss_mm"), 1)
            for hf in range(2):
                for c in range(4):
                    m = pe.transpose(ps[:, 4 + hf, P * c:P * c + P], STZ[:, 4 * hf + c, :], ident)
                m.then_inc(S("wkvp_mm"), 1)
            pe.wait_ge(S("sts_ready"), 8)
            for bp in range(4):
                for hf in range(2):
                    n = 2 * bp + hf
                    if n >= 4:
                        pe.wait_ge(S("wkvs_ready"), after("wkvs_ready", n - 3))
                    for c in range(4):
                        m = pe.transpose(ps[:, n % 4, P * c:P * c + P],
                                         STS[:, 4 * hf + c, 2 * bp:2 * bp + 2, :].rearrange("p b n -> p (b n)"), ident)
                    m.then_inc(S("wkvs_mm"), 1)
            pe.wait_ge(S("wkvp_ready"), after("wkvp_ready", 2))
            for c in range(NC):
                if c >= 4:
                    pe.wait_ge(S("gn_c"), after("gn_c", c - 3))
                else:
                    pe.wait_ge(S("wkvs_ready"), after("wkvs_ready", 8))
                mm(bank(c % 4, T), bones, T3[:, c, :]).then_inc(S("gn_mm"), 1)
            for c in range(NC):
                pe.wait_ge(S("gn_sq"), after("gn_sq", c + 1))
                if c >= 4:
                    pe.wait_ge(S("gn_s"), after("gn_s", c - 3))
                mm(bank(4 + c % 4, T), bones, T1[:, c, :]).then_inc(S("gn_vm"), 1)
            for c in range(NC):
                pe.wait_ge(S("rkr_ready"), after("rkr_ready", c + 1))
                if c >= 4:
                    pe.wait_ge(S("bn_ev"), after("bn_ev", c - 3))
                mm(bank(c % 4, T), bones, rT[:, c, :]).then_inc(S("bn_mm"), 1)
            pe.wait_ge(S("gn_s"), after("gn_s", 8))
            for c in range(NC):
                if c >= 4:
                    pe.wait_ge(S("z_ready"), after("z_ready", c - 3))
                mm(bank(4 + c % 4, T), gw2[:, P * c:P * c + P], hg).then_inc(S("g_mm"), 1)
            pe.wait_ge(S("bn_ev"), after("bn_ev", 8))
            pe.wait_ge(S("z_ready"), after("z_ready", 8))

            def proj(n0, X, outs, freed, base_ev):
                for co in range(outs):
                    wait_w(n0 + co // 4)
                    w = w_in(n0 + co // 4)
                    if co >= 4:
                        pe.wait_ge(S(freed), base_ev + co - 3)
                    for k in range(NC):
                        m = mm(bank(co % 4, T), w[:, k, P * (co % 4):P * (co % 4) + P], X[:, k, :], k == 0, k == NC - 1)
                    m.then_inc(S("proj_mm"), 1)

            def layer_norm(i):
                for c in range(NC):
                    pe.wait_ge(S("ln_in"), 8 * i + c + 1)
                    m = mm(bank(6, T), onesd, YA[:, c, :], c == 0, c == NC - 1)
                m.then_inc(S("ln_mean"), 1)
                for c in range(NC):
                    pe.wait_ge(S("ln_sq"), 8 * i + c + 1)
                    m = mm(bank(7, T), onesd, SQ[:, c, :], c == 0, c == NC - 1)
                m.then_inc(S("ln_var"), 1)

            def expert_block(pre, n, n0, g):
                def s(name):
                    return S(pre + name)
                if pre:
                    pe.wait_ge(S("add_done"), after("add_done", 8 * g))
                    pe.wait_ge(s("add_done"), after("add_done", 8 * n))
                else:
                    pe.wait_ge(S("o_add_done"), after("add_done", 8 * (NBLK - 1) * (g + 1)))
                pe.wait_ge(s("sel_ready"), after("sel_ready", 1 * n + 1))
                pe.wait_ge(s("ya_ready"), after("ya_ready", 1 * n))
                pe.wait_ge(s("y_ready_"), after("y_ready_", 1 * n))
                for c in range(NC):
                    for t, (t0, k) in enumerate(TOK):
                        m = mm(ps[:, c // 4, P * (c % 4):P * (c % 4) + P], XTM[0:k, t, P * c:P * c + P],
                               SelM[0:k, 2 * t:2 * t + 2, :].rearrange("p a n -> p (a n)"), t == 0, t == 2)
                    if c % 4 == 3:
                        m.then_inc(s("ga_mm" if c < 4 else "gb_mm"), 1)
                pe.wait_ge(s("xga_ready"), after("xga_ready", 1 * n + 1))
                pe.wait_ge(s("xgb_ready"), after("xgb_ready", 1 * n + 1))
                pe.wait_ge(s("sg_ready"), after("sg_ready", 1 * n))
                for e in range(2):
                    for k, name in enumerate(("gate_mm", "up_mm")):
                        j = 3 * e + k
                        pe.wait_ge(S(f"w_full{(n0 + j) % NSLOT}"), landed(n0 + j) + 16 * g_local[0])
                        pe.wait_ge(s("hs_ready" if k == 0 else "h_ready"), after("hs_ready", 2 * n))
                        w = w_in(n0 + j)
                        for f in range(NF):
                            for c in range(NC):
                                m = mm(ps[:, 2 + 2 * e + k, CAP * f:CAP * f + CAP], w[:, c, P * f:P * f + P],
                                       Xg[:, c, CAP * e:CAP * e + CAP], c == 0, c == NC - 1)
                        m.then_inc(s(name), 1)
                pe.wait_ge(s("hs_ready"), after("hs_ready", 2 * n + 1))
                for t, (t0, k) in enumerate(TOK):
                    m = pe.transpose(ps[:, 2, t0:t0 + k], SelG[0:k, 2 * t:2 * t + 2, :].rearrange("p a n -> p (a n)"),
                                     ident[0:k, 0:k])
                m.then_inc(s("sgt_mm"), 1)
                pe.wait_ge(s("add_done"), after("add_done", 8 * n))
                for e in range(2):
                    j = 3 * e + 2
                    pe.wait_ge(S(f"w_full{(n0 + j) % NSLOT}"), landed(n0 + j) + 16 * g_local[0])
                    pe.wait_ge(s("h_ready"), after("h_ready", 2 * n + e + 1))
                    w = w_down(n0 + j)
                    for c in range(NC):
                        for f in range(NF):
                            m = mm(ps[:, 6 + e, CAP * c:CAP * c + CAP], w[:, f, P * c:P * c + P], HH[:, e, f, :],
                                   f == 0, f == NF - 1)
                    m.then_inc(s("down_mm"), 1)
                pe.wait_ge(s("yt_ready"), after("yt_ready", 2 * n + 2))
                for c in range(NC):
                    m = pe.transpose(ps[:, c // 4, P * (c % 4):P * (c % 4) + P], YT[:, c, :], ident)
                    if c % 4 == 3:
                        m.then_inc(s("yta_mm" if c < 4 else "ytb_mm"), 1)
                pe.wait_ge(s("ya_ready"), after("ya_ready", 1 * n + 1))
                pe.wait_ge(s("y_ready_"), after("y_ready_", 1 * n + 1))
                pe.wait_ge(s("sg_ready"), after("sg_ready", 1 * n + 1))
                for c in range(NC):
                    if c >= 2:
                        pe.wait_ge(s("add_done"), after("add_done", 8 * n + c - 1))
                    mm(bank(6 + c % 2, T), YY[:, P * c:P * c + P], SG).then_inc(s("sc_mm"), 1)

            g_local = [0]

            def experts(l, n0):
                pe.wait_ge(S("x_ready"), 16 * l + 8)
                for t, (t0, n) in enumerate(TOK):
                    for hf in range(2):
                        for c in range(4):
                            m = pe.transpose(ps[0:n, 2 * t + hf, P * c:P * c + P], xT[:, 4 * hf + c, t0:t0 + n], ident)
                        m.then_inc(S("xtm_mm"), 1)
                pe.wait_ge(S("in_mconst"), 48 * (l + 1))
                for t, (t0, n) in enumerate(TOK):
                    for c in range(NC):
                        m = mm(ps[0:n, 6, E_ * t:E_ * t + E_], xT[:, c, t0:t0 + n], rw[:, c, :], c == 0, c == NC - 1)
                m.then_inc(S("rt_mm"), 1)
                pe.wait_ge(S("msk_ready"), l + 1)
                for t in range(3):
                    for u in range(t + 1):
                        mm(ps[:, 7, E_ * t:E_ * t + E_], mc("ustrict") if u == t else ones, rt[6][:, E_ * u:E_ * u + E_],
                           u == 0, u == t)
                for u in range(3):
                    m = mm(ps[:, 7, 64:64 + E_], ones, rt[6][:, E_ * u:E_ * u + E_], u == 0, u == 2)
                m.then_inc(S("rk_mm"), 1)
                pe.wait_ge(S("xtm_a"), 3 * (l + 1))
                pe.wait_ge(S("xtm_d"), 3 * (l + 1))
                pe.wait_ge(S("route_ready"), l + 1)
                with pe.Fori(0, PAIRS) as i:
                    g = i + PAIRS * l
                    g_local[0] = i
                    pair_engine(pe, i, g, "pe", lambda pre, n: expert_block(pre, n, n0, g))

            proj(L_WO, T3, NC, "ln_in", 0)
            layer_norm(0)
            experts(0, L_MOE0)
            layer_norm(1)
            pe.wait_ge(S("x_ready"), 16)
            proj(L_KV, xT, 16, "kvq_ev", 0)
            for i, (X, name) in enumerate(((aKT, "ktr_mm"), (aVT, "vtr_mm"))):
                pe.wait_ge(S("kvq_ev"), 8 * (i + 1))
                for t, (t0, n) in enumerate(KTILE):
                    for hf in range(2):
                        j = 8 * i + 2 * t + hf
                        if j >= 4:
                            if j < 12:
                                pe.wait_ge(S("ktm_ready"), after("ktm_ready", min(j - 3, 8)))
                            else:
                                pe.wait_ge(S("vtm_ready"), after("vtm_ready", j - 11))
                        for c in range(4):
                            m = pe.transpose(ps[0:n, 4 + j % 4, P * c:P * c + P], X[:, 4 * hf + c, t0:t0 + n], ident)
                        m.then_inc(S(name), 1)
            pe.wait_ge(S("kvq_ev"), 16)
            proj(L_Q, xT, NC, "kvq_ev", 16)
            pe.wait_ge(S("kvq_ev"), 24)
            pe.wait_ge(S("vtm_ready"), after("vtm_ready", 8))
            pe.wait_ge(S("in_aconst"), 32)

            units = [(t, h) for t in range(3) for h in range(NH)]

            def scores(u):
                t, h = units[u]
                q0, nq = KTILE[t]
                nk = q0 + nq
                if u >= 2:
                    pe.wait_ge(S("p_exp"), 2 * (u - 1))
                for j in range(2):
                    q = slice(64 * j, 64 * j + 64)
                    b = 2 * (u % 2) + j
                    mm(ps[0:nq, b, 0:nk], aQT[q, h, q0:q0 + nq], aKT[q, h, 0:nk], True, False)
                    m = mm(ps[0:nq, b, q0:nk], ident[:, 0:nq], ac("caus")[:, 0:nq], False, True)
                m.then_inc(S("p_sc"), 1)

            def turn(u):
                t, h = units[u]
                q0, nq = KTILE[t]
                pe.wait_ge(S("p_am"), u + 1)
                if u >= 2:
                    pe.wait_ge(S("p_at"), u - 1)
                for kt in range(t + 1):
                    k0, n = KTILE[kt]
                    m = pe.transpose(ps[0:n, 4 + u % 2, P * kt:P * kt + nq], PP[u % 2][0:nq, 0, k0:k0 + n], ident[0:nq, 0:nq])
                m.then_inc(S("p_tr"), 1)

            def values(u):
                t, h = units[u]
                q0, nq = KTILE[t]
                pe.wait_ge(S("p_at"), u + 1)
                if u >= 2:
                    pe.wait_ge(S("p_oev"), u - 1)
                for kt in range(t + 1):
                    k0, n = KTILE[kt]
                    m = mm(ps[:, 6 + u % 2, 0:nq], VTM[0:n, kt, P * h:P * h + P], AT[u % 2][0:n, kt, 0:nq], kt == 0, kt == t)
                m.then_inc(S("p_av"), 1)

            NU = len(units)
            for i in range(NU + 2):
                if i < NU:
                    scores(i)
                if 1 <= i <= NU:
                    turn(i - 1)
                if i >= 2:
                    values(i - 2)
            pe.wait_ge(S("p_exp"), 2 * NU)
            pe.wait_ge(S("p_oev"), NU)
            for b in range(SB):
                pe.wait_ge(S(f"in_pg{b % 2}"), 64 * (b // 2 + 1))
                if b:
                    pe.wait_ge(S("kts_a"), 2 * b)
                    pe.wait_ge(S("kts_d"), 2 * b)
                for g in range(NPG):
                    for hf in range(2):
                        for c in range(4):
                            m = pe.transpose(ps[:, 2 * g + hf, P * c:P * c + P],
                                             PGK[b % 2][:, g, P * (4 * hf + c):P * (4 * hf + c) + P], ident)
                        m.then_inc(S("kt_mm"), 1)
                pe.wait_ge(S("kts_a"), 2 * b + 2)
                pe.wait_ge(S("kts_d"), 2 * b + 2)
                pe.wait_ge(S("qbd_ready"), b + 1)
                pe.wait_ge(S("s_exp"), b)
                qb = Qbd[:, 0:1024].rearrange("p (c n) -> p c n", c=NC)
                for c in range(NC):
                    mm(ps[:, 4, 0:256], qb[:, c, :], KTs[:, c, :], c == 0, c == NC - 1)
                for c in range(NC):
                    mm(ps[:, 4, 256:320], qb[:, c, :], aKT[:, c, TP:T], c == 0, False)
                w0 = TS - SS - 8 * b
                mm(ps[:, 4, 256:320], ident, ac("win")[:, w0:w0 + TS], False, True).then_inc(S("s_sc"), 1)
                pe.wait_ge(S("s_am"), b + 1)
                pe.wait_ge(S("s_at"), 2 * b)
                for kt in range(3):
                    n = P if kt < 2 else TS
                    m = pe.transpose(ps[0:n, 5, P * kt:P * kt + P], PS[:, P * kt:P * kt + n], ident)
                m.then_inc(S("s_tr"), 1)
                pe.wait_ge(S("s_at"), 2 * b + 2)
                pe.wait_ge(S("s_oev"), b)
                for h in range(NH):
                    o = ps[:, 6, SS * h:SS * h + SS]
                    for g in range(2):
                        mm(o, PGV[b % 2][:, g, P * h:P * h + P], ATs[:, g, SS * h:SS * h + SS], g == 0, False)
                    m = mm(o, VTM[0:TS, 3, P * h:P * h + P], ATs[0:TS, 2, SS * h:SS * h + SS], False, True)
                m.then_inc(S("past_mm"), 1)
            for c in range(NC):
                pe.wait_ge(S("sl_sq"), after("sl_sq", c + 1))
                if c >= 4:
                    pe.wait_ge(S("sl_s"), after("sl_s", c - 3))
                mm(bank(c % 4, T), ones, aSQ[:, c, :]).then_inc(S("sl_mm"), 1)
            pe.wait_ge(S("z2_ready"), after("z2_ready", 8))
            proj(L_DO, aOT, NC, "ln_in", 16)
            layer_norm(2)
            experts(1, L_MOE1)
            layer_norm(3)
            pe.wait_ge(S("x_ready"), 32)
            for t, (t0, n) in enumerate(((N_META, P), (N_META + P, P), (TP, TS))):
                for hf in range(2):
                    for c in range(4):
                        m = pe.transpose(ps[0:n, 2 * t + hf, P * c:P * c + P], xT[:, 4 * hf + c, t0:t0 + n], ident)
                    m.then_inc(S("yo_mm"), 1)

        @block.scalar
        def _(act):
            prime(act, "act")
            def f(out, in_, func, **k):
                return act.activation(out, in_, func, **k)

            def copy(out, in_):
                return act.copy(out, in_)

            for i, X in enumerate((rT, kT_, vT_)):
                for c in range(NC):
                    n = 8 * i + c
                    act.wait_ge(S("rkv_mm"), after("rkv_mm", n + 1))
                    copy(X[:, c, :], bank(n % 4, T)).then_inc(S("rkv_ev"), 1)
            act.wait_ge(S("lora_mm"), after("lora_mm", 1))
            f(hw, ps[0:64, 4, 0:T], ACT.Tanh).then_inc(S("lora_ev"), 1)
            act.wait_ge(S("lora_mm"), after("lora_mm", 2))
            copy(ha, ps[0:64, 5, 0:T]).then_inc(S("lora_ev"), 1)
            act.wait_ge(S("lora_mm"), after("lora_mm", 3))
            f(hg, ps[:, 6, 0:T], ACT.Sigmoid).then_inc(S("lora_ev"), 1)
            act.wait_ge(S("mix_ready"), after("mix_ready", 48))
            for i, (X, w0) in enumerate(((sgT, dw0), (T3, aw0))):
                for c in range(NC):
                    act.wait_ge(S("lz_mm"), after("lz_mm", 8 * i + c + 1))
                    f(X[:, c, :], bank(4 + c % 4, T), ACT.Sigmoid, bias=w0[:, c:c + 1]).then_inc(S("lz_ev"), 1)
            for c in range(NC):
                act.wait_ge(S("kk_ready"), after("kk_ready", c + 1))
                f(T2[:, c, :], T1[:, c, :], ACT.Square).then_inc(S("kksq_ready"), 1)
            for c in range(NC):
                act.wait_ge(S("kks_mm"), after("kks_mm", c + 1))
                f(T2[:, c, :], bank(c % 4, T), ACT.Sqrt).then_inc(S("kks_ev"), 1)
            for n in range(8):
                bp, hf = n // 2, n % 2
                act.wait_ge(S("nat_in_mm"), after("nat_in_mm", n + 1))
                copy(STS[:, 4 * hf:4 * hf + 4, 2 * bp:2 * bp + 2, :].rearrange("p c b n -> p c (b n)"),
                     bank(4 + n % 4).rearrange("p (c n) -> p c n", c=4)).then_inc(S("nat_ev"), 1)
            act.wait_ge(S("prep_ready"), 1)

            def chunk(n, t0, w, sample):
                cols = bass.ds(t0, w)
                act.wait_ge(S("st_ready"), 1 * n + 1)
                act.wait_ge(S("ops_ready"), after("ops_ready", 1 * n))
                f(EX[0][:, :, 0:w], T3[:, :, cols], ACT.Exp, scale=-KAPPA).then_inc(S("ex_ready"), 1)
                f(EX[1][:, :, 0:w], T3[:, :, cols], ACT.Exp, scale=KAPPA).then_inc(S("ex_ready"), 1)
                act.wait_ge(S("lx_ready"), 1 * n + 1)
                f(EX[2][:, :, 0:w], EX[2][:, :, 0:w], ACT.Exp, scale=-KAPPA).then_inc(S("ex_ready"), 1)
                for hp in range(2):
                    act.wait_ge(S("l_mm"), 2 * n + hp + 1)
                    copy(LM[:, 8 * hp:8 * hp + 8, :].rearrange("p h n -> p (h n)"), ps[0:64, hp, :]).then_inc(S("lm_ready"), 1)
                levels = 2 if sample else LEVELS - 1
                for lv in range(1, levels + 1):
                    for hf in range(2):
                        act.wait_ge(S("y_mm"), 10 * n + 2 * (lv - 1) + hf + 1)
                        copy(YI[:, 8 * hf:8 * hf + 8, :].rearrange("p h n -> p (h n)"), ps[0:64, 4 + hf, :]
                             ).then_inc(S("y_ready"), 1)
                    if lv == 1:
                        for hf in range(2):
                            act.wait_ge(S("mv_mm"), 2 * n + hf + 1)
                            act.wait_ge(S("u_ready"), after("u_ready", 2 * n))
                            copy(MV[:, 8 * hf:8 * hf + 8, :].rearrange("p h n -> p (h n)"), ps[0:64, 2 + hf, :]
                                 ).then_inc(S("mv_ready"), 1)
                if sample:
                    for hp in range(2):
                        for hf in range(2):
                            q = slice(64 * hp, 64 * hp + 64)
                            act.wait_ge(S("qs_mm"), 2 * hp + hf + 1)
                            copy(QS[q, 4 * hf:4 * hf + 4, :, :].rearrange("p c w t -> p (c w t)"), ps[q, 2 * hp + hf, :]
                                 ).then_inc(S("qs_ready"), 1)
                for hf in range(2):
                    act.wait_ge(S("sa_mm"), after("sa_mm", 2 * n + hf + 1))
                    copy(SAV[0:64, 8 * hf:8 * hf + 8, :].rearrange("p h n -> p (h n)"), ps[0:64, 4 + hf, :]
                         ).then_inc(S("sa_ready"), 1)
                if not sample:
                    act.wait_ge(S("o_mm"), after("o_mm", 1 * n + 1))
                    apart(act)
                    copy(T3[:, :, cols], bank(6).rearrange("p (c t) -> p c t", c=NC)[:, :, 0:w]).then_inc(S("o_ready"), 1)

            with act.Fori(0, NFULL) as i:
                chunk(i, i * C, C, False)
            chunk(NFULL, NFULL * C, TP - NFULL * C, False)
            chunk(NFULL + 1, TP, TS, True)
            for hf in range(2):
                act.wait_ge(S("wkvp_mm"), after("wkvp_mm", hf + 1))
                copy(QW[:, 4 * hf:4 * hf + 4, :].rearrange("p c n -> p (c n)"), bank(4 + hf)).then_inc(S("wkvp_ready"), 1)
            for n in range(8):
                bp, hf = n // 2, n % 2
                act.wait_ge(S("wkvs_mm"), after("wkvs_mm", n + 1))
                if n == 0:
                    act.wait_ge(S("o_ready"), after("o_ready", NFULL + 2))
                if bp >= 2 and hf == 0:
                    act.wait_ge(S(f"out_wkvs{bp % 2}"), 32)
                copy(NAT[bp % 2][:, 512 * hf:512 * hf + 512], bank(n % 4)).then_inc(S("wkvs_ready"), 1)
            for c in range(NC):
                act.wait_ge(S("gn_c"), after("gn_c", c + 1))
                f(T1[:, c, :], sgT[:, c, :], ACT.Square).then_inc(S("gn_sq"), 1)
            for c in range(NC):
                act.wait_ge(S("gn_vm"), after("gn_vm", c + 1))
                f(T1[:, c, :], bank(4 + c % 4, T), ACT.Sqrt, scale=1.0 / N, bias=eps_lnx).then_inc(S("gn_s"), 1)

            def layer_norm(i, l, j):
                for c in range(NC):
                    act.wait_ge(S("ln_c"), 8 * i + c + 1)
                    f(SQ[:, c, :], CT[:, c, :], ACT.Square).then_inc(S("ln_sq"), 1)
                act.wait_ge(S("ln_var"), i + 1)
                f(RS, bank(7, T), ACT.Sqrt, bias=eps_ln).then_inc(S("ln_rs"), 1)
                for c in range(NC):
                    act.wait_ge(S("ln_n"), 8 * i + c + 1)
                    f(xT[:, c, :], CT[:, c, :], ACT.Identity, scale=plv[l][j][0][:, c:c + 1],
                      bias=plv[l][j][1][:, c:c + 1]).then_inc(S("x_ready"), 1)

            def expert_block(pre, n):
                def s(name):
                    return S(pre + name)
                act.wait_ge(s("ga_mm"), after("ga_mm", 1 * n + 1))
                copy(Xg[:, 0:4, :].rearrange("p c n -> p (c n)"), bank(0)).then_inc(s("xga_ready"), 1)
                for e in range(2):
                    act.wait_ge(s("gate_mm"), after("gate_mm", 2 * n + e + 1))
                    act.wait_ge(s("h_ready"), after("h_ready", 2 * n))
                    f(HS[:, e, :], bank(2 + 2 * e, 256), ACT.Silu).then_inc(s("hs_ready"), 1)
                for e in range(2):
                    act.wait_ge(s("down_mm"), after("down_mm", 2 * n + e + 1))
                    copy(YT[:, :, CAP * e:CAP * e + CAP], bank(6 + e).rearrange("p (c n) -> p c n", c=NC)
                         ).then_inc(s("yt_ready"), 1)
                act.wait_ge(s("yta_mm"), after("yta_mm", 1 * n + 1))
                copy(YY[:, 0:512], bank(0)).then_inc(s("ya_ready"), 1)


            def experts(l):
                for t, (t0, n) in enumerate(TOK):
                    act.wait_ge(S("xtm_mm"), 6 * l + 2 * t + 1)
                    copy(XTM[0:n, t, 0:512], ps[0:n, 2 * t, :]).then_inc(S("xtm_a"), 1)
                act.wait_ge(S("rt_mm"), l + 1)
                act.wait_ge(S("rt_zero"), l + 1)
                f(rt[0][:, 0:32], ps[:, 6, 0:32], ACT.Sigmoid)
                f(rt[0][0:TOK[2][1], 32:48], ps[0:TOK[2][1], 6, 32:48], ACT.Sigmoid).then_inc(S("s_ready"), 1)
                act.wait_ge(S("route_ready"), l + 1)
                with act.Fori(0, PAIRS) as i:
                    pair_engine(act, i, i + PAIRS * l, "act", expert_block)

            layer_norm(0, 0, 0)
            experts(0)
            layer_norm(1, 0, 1)
            for i, X in enumerate((aKT, aVT, aQT)):
                for c in range(NC):
                    act.wait_ge(S("proj_mm"), 8 + 8 * i + c + 1)
                    copy(X[:, c, :], bank(c % 4, T)).then_inc(S("kvq_ev"), 1)
            act.wait_ge(S("lam_s"), 1)
            f(lams[:, 2:4], lams[:, 0:2], ACT.Exp).then_inc(S("lam_e"), 1)
            units = [(t, h) for t in range(3) for h in range(NH)]

            def weights_out(u):
                t, h = units[u]
                nq = KTILE[t][1]
                act.wait_ge(S("p_tr"), u + 1)
                if u >= 2:
                    act.wait_ge(S("p_av"), u - 1)
                for lo, hi in ((0, min(t + 1, 2)), (2, t + 1)):
                    if lo < hi:
                        k = KTILE[lo][1]
                        i = copy(AT[u % 2][0:k, lo:hi, 0:nq],
                                 ps[0:k, 4 + u % 2, P * lo:P * hi].rearrange("p (k n) -> p k n", n=P)[:, :, 0:nq])
                i.then_inc(S("p_at"), 1)

            NU = len(units)
            for u in range(NU + 1):
                if u < NU:
                    t, h = units[u]
                    nq = KTILE[t][1]
                    nk = KTILE[t][0] + nq
                    act.wait_ge(S("p_nb"), u + 1)
                    if u >= 2:
                        act.wait_ge(S("p_tr"), u - 1)
                    for j in range(2):
                        f(PP[u % 2][0:nq, j, 0:nk], ps[0:nq, 2 * (u % 2) + j, 0:nk], ACT.Exp, scale=0.125,
                          bias=st4[u % 2][0:nq, j:j + 1], accum_out=st4[u % 2][0:nq, 2 + j:3 + j]).then_inc(S("p_exp"), 1)
                if u >= 1:
                    weights_out(u - 1)
            for b in range(SB):
                act.wait_ge(S("kt_mm"), 4 * b + 1)
                for hf in range(2):
                    act.wait_ge(S("kt_mm"), 4 * b + hf + 1)
                    copy(KTs[:, 4 * hf:4 * hf + 4, 0:P], bank(hf).rearrange("p (c n) -> p c n", c=4)).then_inc(S("kts_a"), 1)
                act.wait_ge(S("s_nb"), b + 1)
                act.wait_ge(S("s_tr"), b)
                f(PS, ps[:, 4, 0:320], ACT.Exp, scale=0.125, bias=st4[0][:, 0:1],
                  accum_out=st4[0][:, 2:3]).then_inc(S("s_exp"), 1)
            act.wait_ge(S("s_oev"), SB)
            for c in range(NC):
                f(aSQ[:, c, :], aOT[:, c, :], ACT.Square).then_inc(S("sl_sq"), 1)
            for c in range(NC):
                act.wait_ge(S("sl_mm"), after("sl_mm", c + 1))
                f(aSQ[:, c, :], bank(c % 4, T), ACT.Sqrt, scale=1.0 / P, bias=eps_ln).then_inc(S("sl_s"), 1)
            layer_norm(2, 1, 0)
            experts(1)
            layer_norm(3, 1, 1)
            for t in range(3):
                n = P if t < 2 else TS
                act.wait_ge(S("yo_mm"), 2 * t + 1)
                copy(OUTT[0:n, t, 0:512], ps[0:n, 2 * t, :]).then_inc(S("y_rows"), 1)

        @block.vector
        def _(dve):
            prime(dve, "dve")
            tt, tsc, stt, cp = dve.tensor_tensor, dve.tensor_scalar, dve.scalar_tensor_tensor, dve.tensor_copy
            dve.wait_ge(S("par_mm"), 1)
            cp(par[:, 0:104], ps[:, 0, 0:104])
            cp(par[:, 104:169], ps[:, 0, 128:193])
            cp(ssT, ps[:, 0, 256:320])
            dve.drain()
            tsc(oneka, ka, -1.0, 1.0, ALU.mult, ALU.add)
            for t, (t0, n) in enumerate(TOK):
                for hf in range(2):
                    dve.wait_ge(S("xt_mm"), 2 * t + hf + 1)
                    cp(xT[:, 4 * hf:4 * hf + 4, t0:t0 + n], ps[:, 1 + 2 * t + hf, 0:4 * n].rearrange("p (c n) -> p c n", c=4))
            dve.drain()
            tt(sgT[:, :, 1:T], xT[:, :, 0:T - 1], xT[:, :, 1:T], ALU.subtract)
            dve.drain()
            tsc(sgT[:, :, 0:1], xT[:, :, 0:1], -1.0, None, ALU.mult)
            tt(sgT[:, :, TP:T:SS], ssT.rearrange("p (b c) -> p c b", c=NC), xT[:, :, TP:T:SS], ALU.subtract)
            dve.drain()
            for i, (m, X) in enumerate(((0, T1), (2, T2), (3, T3), (1, T1), (4, T2), (5, T3))):
                if i >= 3:
                    dve.wait_ge(S("rkv_mm"), after("rkv_mm", 8 * (i - 2)))
                for c in range(NC):
                    stt(X[:, c, :], sgT[:, c, :], mixv[m][:, c:c + 1], xT[:, c, :], ALU.mult, ALU.add
                        ).then_inc(S("mix_ready"), 1)
            dve.wait_ge(S("lora_mm"), after("lora_mm", 1))
            dve.wait_ge(S("rkv_ev"), after("rkv_ev", 16))
            for c in range(NC):
                tsc(T1[:, c, :], kT_[:, c, :], kk0[:, c:c + 1], None, ALU.mult).then_inc(S("kk_ready"), 1)
            dve.wait_ge(S("kks_ev"), after("kks_ev", 8))
            tsc(T2, T2, 1e-12, None, ALU.max)
            dve.drain()
            dve.reciprocal(T2, T2)
            dve.drain()
            stt(T1, T1, -1.0, T2, ALU.mult, ALU.mult)
            dve.wait_ge(S("lz_ev"), after("lz_ev", 16))
            dve.drain()
            stt(T2, T1, -1.0, T3, ALU.mult, ALU.mult)
            dve.drain()
            for c in range(NC):
                tsc(T3[:, c, :], T3[:, c, :], ka[:, c:c + 1], oneka[:, c:c + 1], ALU.mult, ALU.add)
            dve.drain()
            tt(kT_, kT_, T3, ALU.mult)
            dve.drain()
            dve.wait_ge(S("in_rconst"), 16)
            for c in range(NC):
                dve.tensor_tensor_scan(T3[:, c, :], rc("scan"), sgT[:, c, :], 0.0, ALU.mult, ALU.add)
            dve.memset(STZ, 0.0)
            dve.drain().then_inc(S("prep_ready"), 1)
            dve.wait_ge(S("nat_ev"), after("nat_ev", 8))
            dve.nop().then_inc(S("st_ready"), 1)
            dve.wait_ge(S("prep_ready"), 1)

            def chunk(n, t0, w, sample):
                cols = bass.ds(t0, w)
                tt(EX[2][:, :, 0:w], T3[:, :, cols], sgT[:, :, cols], ALU.subtract).then_inc(S("lx_ready"), 1)
                dve.wait_ge(S("sa_mm"), after("sa_mm", 2 * n))
                cp(XI, ident[0:64, 0:64].unsqueeze(1).to_broadcast([64, H, 64]))
                cp(XU, ident[0:64, 0:64].unsqueeze(1).to_broadcast([64, H, 64]))
                dve.wait_ge(S("o_mm"), after("o_mm", 1 * n))
                if w < C:
                    dve.memset(RAV, 0.0)
                    dve.memset(BK, 0.0)
                    dve.drain()
                dve.wait_ge(S("ex_ready"), 3 * n + 3)
                tt(RAV[:, :, 0:w], rT[:, :, cols], EX[0][:, :, 0:w], ALU.mult)
                tt(RAV[:, :, 64:64 + w], T1[:, :, cols], EX[2][:, :, 0:w], ALU.mult)
                cp(RAV[:, :, 128:128 + w], vT_[:, :, cols])
                tt(BK[:, :, 0:w], T2[:, :, cols], EX[1][:, :, 0:w], ALU.mult)
                tt(BK[:, :, 64:64 + w], kT_[:, :, cols], EX[1][:, :, 0:w], ALU.mult).then_inc(S("ops_ready"), 1)
                for hf in range(2):
                    dve.wait_ge(S("bkt_mm"), 2 * n + hf + 1)
                    cp(BKt[:, 4 * hf:4 * hf + 4, :].rearrange("p c n -> p (c n)"), bank(hf)).then_inc(S("bkt_ready"), 1)
                for hf in range(2):
                    dve.wait_ge(S("avt_mm"), 2 * n + hf + 1)
                    cp(SAV[64:128, 8 * hf:8 * hf + 8, :].rearrange("p h n -> p (h n)"), ps[64:128, 2 + hf, :]
                       ).then_inc(S("sv_ready"), 1)
                mask = rc("masks" if sample else "maskp").unsqueeze(1).to_broadcast([P, 4, P])
                gv = GH.rearrange("p (c e) n -> p e c n", e=2)
                for hp in range(2):
                    for hf in range(2):
                        dve.wait_ge(S("gh_mm"), 4 * n + 2 * hp + hf + 1)
                        tt(gv[:, hp, 4 * hf:4 * hf + 4, :], bank(4 + 2 * hp + hf).rearrange("p (c n) -> p c n", c=4),
                           mask, ALU.mult).then_inc(S("gh_ready"), 1)

                def level(name, m):
                    return rc(name)[0:64, 64 * m:64 * m + 64].bitcast(U32).unsqueeze(1).to_broadcast([64, 8, 64])

                for hp in range(2):
                    h8 = slice(8 * hp, 8 * hp + 8)
                    dve.wait_ge(S("lm_ready"), 2 * n + hp + 1)
                    apart(dve)
                    dve.copy_predicated(XI[:, h8, :], level("low", 0), LM[:, h8, :])
                for hp in range(2):
                    h8 = slice(8 * hp, 8 * hp + 8)
                    dve.wait_ge(S("lt_mm"), 2 * n + hp + 1)
                    apart(dve)
                    i = dve.copy_predicated(XU[:, h8, :], level("up", 0), ps[0:64, 2 + hp, :].rearrange("p (h n) -> p h n", h=8))
                i.then_inc(S("inv_ready"), 1)
                levels = 2 if sample else LEVELS - 1
                for lv in range(1, levels + 1):
                    for hf in range(2):
                        h8 = slice(8 * hf, 8 * hf + 8)
                        bx = (6, 7) if hf == 0 else (0, 1)
                        dve.wait_ge(S("xu_mm"), 10 * n + 2 * (lv - 1) + hf + 1)
                        apart(dve)
                        if lv < levels:
                            dve.copy_predicated(XI[:, h8, :], level("low", lv), ps[0:64, bx[0], :].rearrange("p (h n) -> p h n", h=8))
                        dve.copy_predicated(XU[:, h8, :], level("up", lv), ps[0:64, bx[1], :].rearrange("p (h n) -> p h n", h=8)
                                            ).then_inc(S("inv_ready"), 1)
                for hf in range(2):
                    h8 = slice(8 * hf, 8 * hf + 8)
                    dve.wait_ge(S("u_mm"), 2 * n + hf + 1)
                    dve.wait_ge(S("mv_ready"), 2 * n + hf + 1)
                    tt(U[:, h8, :].rearrange("p h n -> p (h n)"), ps[0:64, 2 + hf, :],
                       MV[:, h8, :].rearrange("p h n -> p (h n)"), ALU.add).then_inc(S("u_ready"), 1)
                if sample:
                    dve.wait_ge(S("o_mm"), after("o_mm", 1 * n + 1))
                    tt(T3[:, :, cols], bank(6).rearrange("p (c t) -> p c t", c=NC), QS[:, :, 0, :], ALU.add
                       ).then_inc(S("o_ready"), 1)
                else:
                    dve.wait_ge(S("st_mm"), 1 * n + 1)
                    for hp in range(2):
                        q = slice(64 * hp, 64 * hp + 64)
                        tt(STZ[q, :, q], bank(7).rearrange("p (c n) -> p c n", c=NC)[q], STZ[q, :, q], ALU.add)
                    dve.drain()
                    for hp in range(2):
                        q = slice(64 * hp, 64 * hp + 64)
                        i = tt(STZ[q, :, q], STZ[q, :, q], EX[0][q, :, w - 1:w].to_broadcast([64, NC, 64]), ALU.mult)
                    i.then_inc(S("st_ready"), 1)

            with dve.Fori(0, NFULL) as i:
                chunk(i, i * C, C, False)
            chunk(NFULL, NFULL * C, TP - NFULL * C, False)
            chunk(NFULL + 1, TP, TS, True)
            def state_update(dve, c):
                dve.wait_ge(S("ss_mm"), after("ss_mm", 2 * c + 2))
                v = STS[:, c, :, :]
                tt(v, bank(6 + c % 2).rearrange("p (b n) -> p b n", b=SB), v, ALU.add)
                dve.drain()
                tt(v, v, EX[0][:, c, SS - 1:TS:SS].unsqueeze(2).to_broadcast([P, SB, N]), ALU.mult
                   ).then_inc(S("sts_ready"), 1)

            for h in range(H):
                c, hp = h // 2, h % 2
                if h >= 2:
                    dve.wait_ge(S("ss_mm"), after("ss_mm", h - 1))
                if h == 0:
                    dve.wait_ge(S("sa_ready"), after("sa_ready", 2 * (NFULL + 2)))
                tt(SAVB[h % 2], SAV[:, h, :].unsqueeze(1).to_broadcast([P, SB, N]),
                   rc("bm").unsqueeze(2).to_broadcast([P, SB, N]), ALU.mult).then_inc(S("savb_ready"), 1)
                if hp and c >= 1:
                    state_update(dve, c - 1)
            state_update(dve, NC - 1)

            for c in range(NC):
                dve.wait_ge(S("gn_mm"), after("gn_mm", c + 1))
                stt(sgT[:, c, :], bank(c % 4, T), -1.0 / N, T3[:, c, :], ALU.mult, ALU.add).then_inc(S("gn_c"), 1)
            tt(rT, rT, kT_, ALU.mult)
            dve.drain()
            for c in range(NC):
                tsc(rT[:, c, :], rT[:, c, :], rkv_[:, c:c + 1], None, ALU.mult).then_inc(S("rkr_ready"), 1)
            dve.wait_ge(S("gn_s"), after("gn_s", 8))
            dve.reciprocal(T1, T1)
            dve.drain()
            tt(sgT, sgT, T1, ALU.mult)
            dve.drain()
            for c in range(NC):
                tsc(sgT[:, c, :], sgT[:, c, :], lnx0[:, c:c + 1], lnx1[:, c:c + 1], ALU.mult, ALU.add)
            for c in range(NC):
                dve.wait_ge(S("bn_mm"), after("bn_mm", c + 1))
                tt(T2[:, c, :], bank(c % 4, T), vT_[:, c, :], ALU.mult).then_inc(S("bn_ev"), 1)
            dve.drain()
            tt(sgT, sgT, T2, ALU.add)
            dve.drain()
            for c in range(NC):
                dve.wait_ge(S("g_mm"), after("g_mm", c + 1))
                tt(T3[:, c, :], sgT[:, c, :], bank(4 + c % 4, T), ALU.mult).then_inc(S("z_ready"), 1)

            def residual(base_mm):
                for c in range(NC):
                    dve.wait_ge(S("proj_mm"), base_mm + c + 1)
                    stt(YA[:, c, :], xT[:, c, :], ALPHA, bank(c % 4, T), ALU.mult, ALU.add).then_inc(S("ln_in"), 1)

            def layer_norm(i):
                dve.wait_ge(S("ln_mean"), i + 1)
                for c in range(NC):
                    tt(CT[:, c, :], YA[:, c, :], bank(6, T), ALU.subtract).then_inc(S("ln_c"), 1)
                dve.wait_ge(S("ln_rs"), i + 1)
                dve.reciprocal(RS, RS)
                dve.drain()
                for c in range(NC):
                    tt(CT[:, c, :], CT[:, c, :], RS, ALU.mult).then_inc(S("ln_n"), 1)

            def expert_block(pre, n, pick):
                def s(name):
                    return S(pre + name)
                if pre:
                    tsc(rkp, rkp, -float(CAP), None, ALU.add)
                else:
                    pick()
                dve.drain()
                tt(SelM, mc("iota").unsqueeze(1).to_broadcast([P, 6, CAP]), rkp.unsqueeze(2).to_broadcast([P, 6, CAP]),
                   ALU.is_equal)
                dve.drain()
                tt(SelG, SelM, gtp.unsqueeze(2).to_broadcast([P, 6, CAP]), ALU.mult).then_inc(s("sel_ready"), 1)
                dve.wait_ge(s("gb_mm"), after("gb_mm", 1 * n + 1))
                cp(Xg[:, 4:8, :].rearrange("p c n -> p (c n)"), bank(1)).then_inc(s("xgb_ready"), 1)
                for e in range(2):
                    dve.wait_ge(s("up_mm"), after("up_mm", 2 * n + e + 1))
                    dve.wait_ge(s("hs_ready"), after("hs_ready", 2 * n + e + 1))
                    tt(HH[:, e, :, :].rearrange("p f n -> p (f n)"), bank(3 + 2 * e, 256), HS[:, e, :], ALU.mult
                       ).then_inc(s("h_ready"), 1)
                dve.wait_ge(s("sgt_mm"), after("sgt_mm", 1 * n + 1))
                cp(SG, bank(2, T)).then_inc(s("sg_ready"), 1)
                dve.wait_ge(s("ytb_mm"), after("ytb_mm", 1 * n + 1))
                cp(YY[:, 512:1024], bank(1)).then_inc(s("y_ready_"), 1)
                for c in range(NC):
                    dve.wait_ge(s("sc_mm"), after("sc_mm", 8 * n + c + 1))
                    tt(YA[:, c, :], YA[:, c, :], bank(6 + c % 2, T), ALU.add).then_inc(s("add_done"), 1)


            def experts(l):
                dve.memset(rt[0], 0.0).then_inc(S("rt_zero"), 1)
                dve.wait_ge(S("x_ready"), 16 * l + 8)
                dve.memset(YA, 0.0)
                for t, (t0, n) in enumerate(TOK):
                    dve.wait_ge(S("xtm_mm"), 6 * l + 2 * t + 2)
                    cp(XTM[0:n, t, 512:1024], ps[0:n, 2 * t + 1, :]).then_inc(S("xtm_d"), 1)
                dve.wait_ge(S("in_mconst"), 48 * (l + 1))
                dve.wait_ge(S("s_ready"), l + 1)

                def v3(x):
                    return x.rearrange("p (t n) -> p t n", t=3)

                def g12(x):
                    return x.rearrange("p (g n) -> p g n", n=4)

                score, sel, a1, a2, oh, msk0, msk, _ = rt
                gm, ga, gb, gc = gs
                m12 = ga[:, 0:12]
                tt(v3(sel), v3(score), rbB.unsqueeze(1).to_broadcast([P, 3, E_]), ALU.add)
                dve.drain()
                for d, o, k in ((1, 0, 3), (2, 3, 2), (3, 5, 1)):
                    tt(pr6[:, :, o:o + k], g12(sel)[:, :, 0:k], g12(sel)[:, :, d:d + k], ALU.add)
                dve.drain()
                dve.tensor_reduce(gm, pr6, AX, ALU.max)
                dve.drain()
                top1 = cntf[:, 0:3]

                def first_best(dst, val, tmp, width, weight):
                    dve.tensor_reduce(top1, v3(val), AX, ALU.max)
                    dve.drain()
                    tt(v3(tmp), v3(val), top1.unsqueeze(2).to_broadcast([P, 3, width]), ALU.is_equal)
                    dve.drain()
                    tt(v3(tmp), v3(tmp), weight.unsqueeze(1).to_broadcast([P, 3, width]), ALU.mult)
                    dve.drain()
                    dve.tensor_reduce(top1, v3(tmp), AX, ALU.max)
                    dve.drain()
                    tt(v3(dst), top1.unsqueeze(2).to_broadcast([P, 3, width]),
                       weight.unsqueeze(1).to_broadcast([P, 3, width]), ALU.is_equal)
                    dve.drain()

                first_best(gb, gm, ga, G_, mc("w4"))
                gmask = gb.unsqueeze(2).to_broadcast([P, 12, 4])
                tsc(gc, gb, BIG, -BIG, ALU.mult, ALU.add)
                tt(g12(a1), g12(sel), gmask, ALU.mult)
                dve.drain()
                tt(g12(a1), g12(a1), gc.unsqueeze(2).to_broadcast([P, 12, 4]), ALU.add)
                dve.drain()
                first_best(msk0, a1, a2, E_, mc("w16"))
                stt(a1, msk0, -2 * BIG, a1, ALU.mult, ALU.add)
                dve.drain()
                first_best(oh, a1, a2, E_, mc("w16"))
                tt(msk, msk0, oh, ALU.add)
                dve.drain()
                tt(v3(msk), v3(msk), mc("valid").unsqueeze(2).to_broadcast([P, 3, E_]), ALU.mult).then_inc(S("msk_ready"), 1)
                dve.drain()
                tt(a1, score, msk, ALU.mult)
                dve.drain()
                dve.tensor_reduce(top1, v3(a1), AX, ALU.add)
                dve.drain()
                tsc(top1, top1, 1e-37, None, ALU.max)
                dve.drain()
                dve.reciprocal(top1, top1)
                dve.drain()
                tt(gate3, v3(a1), top1.unsqueeze(2).to_broadcast([P, 3, E_]), ALU.mult)
                tsc(a2, msk, -1e6, 1e6, ALU.mult, ALU.add)
                dve.wait_ge(S("rk_mm"), l + 1)
                dve.drain()
                tt(rank3.rearrange("p t n -> p (t n)"), a2, ps[:, 7, 0:48], ALU.add)
                dve.tensor_reduce(cntp, ps[:, 7, 64:80].rearrange("p (a b) -> p a b", b=2), AX, ALU.max)
                dve.drain()
                cp(cnt_i[0:1, :], cntp[0:1, :])
                dve.drain().then_inc(S("route_ready"), 1)
                dve.wait_ge(S("route_ready"), l + 1)
                with dve.Fori(0, PAIRS) as i:
                    def pick():
                        cp(rkp.rearrange("p (t e) -> p t e", t=3), rank3[:, :, bass.ds(2 * i, 2)])
                        cp(gtp.rearrange("p (t e) -> p t e", t=3), gate3[:, :, bass.ds(2 * i, 2)])
                    pick()
                    dve.drain()
                    pair_engine(dve, i, i + PAIRS * l, "dve", lambda pre, n: expert_block(pre, n, pick))
                dve.drain()
                for c in range(NC):
                    stt(YA[:, c, :], xT[:, c, :], ALPHA, YA[:, c, :], ALU.mult, ALU.add).then_inc(S("ln_in"), 1)

            residual(0)
            layer_norm(0)
            experts(0)
            layer_norm(1)
            dve.wait_ge(S("in_aconst"), 32)
            lt4 = lamt.rearrange("p (a b n) -> p a b n", a=2, b=2)
            tt(lamp.rearrange("p (a n) -> p a n", a=2), lt4[:, :, 0, :], lt4[:, :, 1, :], ALU.mult)
            dve.drain()
            dve.tensor_reduce(lams[:, 0:2], lamp.rearrange("p (a n) -> p a n", a=2), AX, ALU.add).then_inc(S("lam_s"), 1)
            for i, (X, name) in enumerate(((KTM, "k"), (VTM, "v"))):
                for t, (t0, n) in enumerate(KTILE):
                    for hf in range(2):
                        j = 2 * t + hf
                        dve.wait_ge(S(f"{name}tr_mm"), after(f"{name}tr_mm", j + 1))
                        cp(X[0:n, t, 512 * hf:512 * hf + 512], ps[0:n, 4 + j % 4, :]).then_inc(S(f"{name}tm_ready"), 1)
            dve.wait_ge(S("lam_e"), 1)
            tt(lams[:, 4:5], lams[:, 3:4], lams[:, 2:3], ALU.subtract)
            dve.drain()
            tsc(lams[:, 4:5], lams[:, 4:5], -LI, None, ALU.add)
            dve.drain()
            tsc(lams[:, 6:7], lams[:, 4:5], -1.0, None, ALU.add)
            dve.drain()
            tt(lams[:, 5:6], lams[:, 6:7], ac("odd"), ALU.mult)
            dve.drain()
            tsc(lams[:, 5:6], lams[:, 5:6], 1.0, None, ALU.add)
            dve.memset(Qbd, 0.0)
            dve.drain()
            units = [(t, h) for t in range(3) for h in range(NH)]
            NU = len(units)
            for u in range(NU + 2):
                if u < NU:
                    t, h = units[u]
                    nq = KTILE[t][1]
                    nk = KTILE[t][0] + nq
                    st = st4[u % 2]
                    dve.wait_ge(S("p_sc"), u + 1)
                    b = 2 * (u % 2)
                    dve.tensor_reduce(st[0:nq, 0:2], ps[0:nq, b:b + 2, 0:nk], AX, ALU.max)
                    dve.drain()
                    tsc(st[0:nq, 0:2], st[0:nq, 0:2], -0.125, None, ALU.mult).then_inc(S("p_nb"), 1)
                if 1 <= u <= NU:
                    t, h = units[u - 1]
                    nq = KTILE[t][1]
                    nk = KTILE[t][0] + nq
                    st, p = st4[(u - 1) % 2], PP[(u - 1) % 2]
                    dve.wait_ge(S("p_exp"), 2 * u)
                    dve.reciprocal(st[0:nq, 4:6], st[0:nq, 2:4])
                    dve.drain()
                    tt(st[0:nq, 5:6], st[0:nq, 5:6], lams[0:nq, 4:5], ALU.mult)
                    tsc(p[0:nq, 0, 0:nk], p[0:nq, 0, 0:nk], st[0:nq, 4:5], None, ALU.mult)
                    dve.drain()
                    stt(p[0:nq, 0, 0:nk], p[0:nq, 1, 0:nk], st[0:nq, 5:6], p[0:nq, 0, 0:nk], ALU.mult, ALU.add
                        ).then_inc(S("p_am"), 1)
                if u >= 2:
                    t, h = units[u - 2]
                    q0, nq = KTILE[t]
                    dve.wait_ge(S("p_av"), u - 1)
                    cp(aOT[:, h, q0:q0 + nq], ps[:, 6 + u % 2, 0:nq]).then_inc(S("p_oev"), 1)
            for b in range(SB):
                dve.wait_ge(S("s_sc"), b)
                for hp in range(2):
                    q = slice(64 * hp, 64 * hp + 64)
                    qv = Qbd[q, SS * hp:SS * hp + 1152].rearrange("p (c n) -> p c n", n=144)[:, :, 0:SS]
                    i = cp(qv, aQT[q, :, TP + SS * b:TP + SS * b + SS])
                i.then_inc(S("qbd_ready"), 1)
                for hf in range(2):
                    dve.wait_ge(S("kt_mm"), 4 * b + 3 + hf)
                    cp(KTs[:, 4 * hf:4 * hf + 4, P:2 * P], bank(2 + hf).rearrange("p (c n) -> p c n", c=4)
                       ).then_inc(S("kts_d"), 1)
                dve.wait_ge(S("s_sc"), b + 1)
                st = st4[0]
                dve.tensor_reduce(st[:, 0:1], ps[:, 4, 0:320], AX, ALU.max)
                dve.drain()
                tsc(st[:, 0:1], st[:, 0:1], -0.125, None, ALU.mult).then_inc(S("s_nb"), 1)
                dve.wait_ge(S("s_exp"), b + 1)
                dve.reciprocal(st[:, 4:5], st[:, 2:3])
                dve.drain()
                tsc(PS, PS, st[:, 4:5], lams[:, 5:6], ALU.mult, ALU.mult).then_inc(S("s_am"), 1)
                dve.wait_ge(S("s_tr"), b + 1)
                for lo, hi, k in ((0, 2, P), (2, 3, TS)):
                    v = ps[0:k, 5, P * lo:P * hi].rearrange("p (k m q) -> p k m q", m=2, q=SS)
                    dve.tensor_reduce(ATs[0:k, lo:hi, :].rearrange("p k (h q) -> p (k h) q", q=SS),
                                      v.rearrange("p k m q -> p k q m"), AX, ALU.add).then_inc(S("s_at"), 1)
                dve.wait_ge(S("past_mm"), b + 1)
                cp(aOT[:, :, TP + SS * b:TP + SS * b + SS], ps[:, 6, 0:64].rearrange("p (h q) -> p h q", q=SS)
                   ).then_inc(S("s_oev"), 1)
            dve.wait_ge(S("sl_s"), after("sl_s", 8))
            dve.reciprocal(aSQ, aSQ)
            dve.drain()
            tt(aOT, aOT, aSQ, ALU.mult)
            dve.drain()
            for c in range(NC):
                tsc(aOT[:, c, :], aOT[:, c, :], subv, 1.0 - LI, ALU.mult, ALU.mult).then_inc(S("z2_ready"), 1)
            residual(32)
            layer_norm(2)
            experts(1)
            layer_norm(3)
            for t in range(3):
                n = P if t < 2 else TS
                dve.wait_ge(S("yo_mm"), 2 * t + 2)
                cp(OUTT[0:n, t, 512:1024], ps[0:n, 2 * t + 1, :]).then_inc(S("y_rows"), 1)


_INS = ["x_prompt", "x_sample", "cache_k", "cache_v", "page_table", "state_wkv", "state_shift", "meta_tokens",
        "rwkv_mix", "rwkv_w_rkv", "rwkv_decay_w0", "rwkv_decay_w1", "rwkv_decay_w2", "rwkv_a_w0", "rwkv_a_w1",
        "rwkv_a_w2", "rwkv_g_w1", "rwkv_g_w2", "rwkv_kk_ka", "rwkv_r_k", "rwkv_lnx", "rwkv_w_out", "w_kv_shared",
        "diff_w_q", "diff_lambda", "diff_subln", "diff_w_out", "router_w", "router_b", "moe_w_gate", "moe_w_up",
        "moe_w_down", "post_ln"]
_OUTS = [("y_prompt", (1, SEQ, D)), ("y_sample", (SB, SS, D)), ("new_k_prompt", (1, TP, 2 * NH, N)),
         ("new_v_prompt", (1, TP, NH, P)), ("new_wkv_prompt", (1, 1, H, N, N)), ("new_shift_prompt", (1, 1, D)),
         ("new_k_sample", (SB, SS, 2 * NH, N)), ("new_v_sample", (SB, SS, NH, P)),
         ("new_wkv_sample", (SB, 1, H, N, N)), ("new_shift_sample", (SB, 1, D))]


def kernel(**inputs):
    import numpy as _np
    import concourse.bacc as _bacc
    from concourse.bass_utils import run_bass_kernel_spmd as _run

    nc = _bacc.Bacc("TRN2", target_bir_lowering=False, num_devices=1)
    const, at = constants()
    arrays, I, O = {"in_const": const}, {}, {}
    for name in _INS:
        arrays["in_" + name] = _np.ascontiguousarray(inputs[name])
    for key, a in arrays.items():
        I[key[3:]] = nc.dram_tensor(key, a.shape, mybir.dt.from_np(a.dtype), kind="ExternalInput").ap()
    for name, shape in _OUTS:
        O[name] = nc.dram_tensor("out_" + name, shape, F32, kind="ExternalOutput").ap()
    build(nc, I, O, const, at)
    r = _run(nc, [arrays], core_ids=[0])
    return tuple(r.results[0]["out_" + name] for name, _ in _OUTS)
```

```python
from contextlib import ExitStack
import math

import numpy as np

import concourse.bass as bass
from concourse import mybir

ALU = mybir.AluOpType
ACT = mybir.ActivationFunctionType
AX = mybir.AxisListType.X
F32 = mybir.dt.float32
I32 = mybir.dt.int32
U32 = mybir.dt.uint32
FR = mybir.dt.float32r

P = 128
D = 1024
NC = D // P
N_META, SEQ = 16, 256
TP = N_META + SEQ
SB, SS = 8, 8
TS = SB * SS
T = TP + TS
H, N = 16, 64
C = 64
NFULL = TP // C
LEVELS = 6
NH = 8
PAGE, NPG = 128, 2
E_, G_, F_ = 16, 4, 512
NF = F_ // P
PAIRS = E_ // 2
CAP = 128
NBLK = -(-T // CAP)
NOV = E_ * (NBLK - 1)
QUARTER, NQ, NB = 1024, 12, 4
ALPHA = 4.0 ** 0.25
KAPPA = math.exp(-0.5)
LI = 0.8 - 0.6 * math.exp(-0.3)
BIG = 1e30
TOK = [(0, 128), (128, 128), (256, T - 256)]
KTILE = [(0, 128), (128, 128), (256, TP - 256), (TP, TS)]
ARENA = 53168
SLOT, NSLOT = 4096, 6
L_RKV, L_WO, L_MOE0, L_KV, L_Q, L_DO, L_MOE1 = 0, 6, 8, 56, 60, 62, 64


CHAINS = {
    "stage_mm": (("rkv_mm", 24), ("lora_mm", 3), ("lz_mm", 16), ("kks_mm", 8), ("nat_in_mm", 8), ("ss_mm", 16),
                 ("wkvp_mm", 2), ("wkvs_mm", 8), ("gn_mm", 8), ("gn_vm", 8), ("bn_mm", 8), ("g_mm", 8)),
    "stage_act": (("rkv_ev", 24), ("lora_ev", 3), ("lz_ev", 16), ("kksq_ready", 8), ("kks_ev", 8), ("nat_ev", 8),
                  ("wkvp_ready", 2), ("wkvs_ready", 8), ("gn_sq", 8), ("gn_s", 8)),
    "stage_dve": (("mix_ready", 48), ("kk_ready", 8), ("gn_c", 8), ("rkr_ready", 8), ("bn_ev", 8), ("z_ready", 8)),
    "kv_mm": (("ktr_mm", 8), ("vtr_mm", 8), ("sl_mm", 8)),
    "kv_dve": (("ktm_ready", 8), ("vtm_ready", 8), ("z2_ready", 8)),
    "sub_act": (("sl_sq", 8), ("sl_s", 8)),
}
SHARED = {stage: (name, sum(k for _, k in chain[:i])) for name, chain in CHAINS.items()
          for i, (stage, _) in enumerate(chain)}


CHUNK_PRIMED = {"pe": ("o_mm", "sa_mm"), "act": ("o_ready", "sa_ready"), "dve": ("u_ready", "ops_ready")}
OVER = {
    "pe": (("o_gather", 1), ("o_gate_up", 1), ("o_turn", 1), ("o_down", 1), ("o_scatter", 8)),
    "act": (("o_xg", 1), ("o_silu", 1), ("o_ht", 1), ("o_y", 1)),
    "dve": (("o_sel", 1), ("o_h", 1), ("o_add", 8)),
    "sp": (("o_weights", 48),),
}
PRIMED = {
    "pe": ("ga_mm", "gb_mm", "gate_mm", "up_mm", "sgt_mm", "down_mm", "yta_mm", "ytb_mm", "sc_mm"),
    "act": ("xga_ready", "hs_ready", "yt_ready", "ya_ready"),
    "dve": ("sel_ready", "xgb_ready", "h_ready", "sg_ready", "y_ready_", "add_done"),
}
PER_BLOCK = {"gate_mm": 2, "up_mm": 2, "down_mm": 2, "sc_mm": 8, "hs_ready": 2, "yt_ready": 2, "h_ready": 2,
             "add_done": 8}
PRIMED = {name for names in CHUNK_PRIMED.values() for name in names}


def after(stage, n):
    return n + (SHARED[stage][1] if stage in SHARED else 1 if stage in PRIMED else 0)


def constants():
    p = np.arange(P)[:, None]
    q = np.arange(P)[None, :]
    c64 = np.arange(64)[None, :]
    s, t = p % 64, c64
    parts = {}
    parts["ident"] = (p == q)
    parts["onesd"] = np.full((P, P), 1.0 / D)
    parts["ones"] = np.ones((P, P))
    parts["bones"] = (p // 64 == q // 64)
    parts["eps"] = np.concatenate([np.full((P, 1), 1e-5), np.full((P, 1), 64e-5)], 1)
    parts["maskp"] = np.concatenate([s <= t, s < t], 1)
    same = s // SS == t // SS
    parts["masks"] = np.concatenate([(s <= t) & same, (s < t) & same], 1)
    scan = np.ones(T)
    scan[0:TP:C] = 0
    scan[TP::SS] = 0
    parts["scan"] = np.tile(scan, (P, 1))
    parts["bm"] = (s // SS == np.arange(SB)[None, :])
    for name, a, b in (("low", p, q), ("up", q, p)):
        parts[name] = np.concatenate([(a // (2 * m) == b // (2 * m)) & (a % (2 * m) >= m) & (b % (2 * m) < m)
                                      for m in (1, 2, 4, 8, 16, 32)], 1)
    parts["ustrict"] = (p < q)
    parts["iota"] = np.tile(np.arange(CAP), (P, 1))
    parts["w16"] = np.tile(np.arange(E_, 0, -1), (P, 1))
    parts["w4"] = np.tile(np.arange(G_, 0, -1), (P, 1))
    parts["valid"] = np.concatenate([p < n for _, n in TOK], 1)
    parts["caus"] = np.where(q > p, -BIG, 0.0)
    win = np.arange(2 * TS - SS)[None, :] - (TS - SS)
    parts["win"] = np.where((win >= 0) & (win <= p % SS), 0.0, -BIG)
    parts["odd"] = (p // SS) % 2
    at, out = {}, []
    n = 0
    for k, v in parts.items():
        at[k] = (n, v.shape[1])
        n += v.shape[1]
        out.append(np.broadcast_to(v, v.shape).astype(np.float32))
    return np.ascontiguousarray(np.concatenate(out, 1)), at


def build(nc, I, O, const, at):
    ctx = ExitStack()
    with ctx:
        sems = {}

        def S(name):
            name = SHARED.get(name, (name, 0))[0]
            if name not in sems:
                sems[name] = ctx.enter_context(nc.semaphore(name))
            return sems[name]

        A = ctx.enter_context(nc.sbuf_tensor("arena", [P, ARENA], F32))
        ps = ctx.enter_context(nc.psum_tensor("ps", [P, 8, 512], F32))
        arena_at = nc.sbuf_base - 4 * ARENA
        cnt_i = ctx.enter_context(nc.sbuf_tensor("cnt_i", [1, E_ + 1], I32))
        pt_i = ctx.enter_context(nc.sbuf_tensor("pt_i", [1, SB * NPG], I32))

        top = [0]

        def cut(n, where=None):
            if where is not None:
                return A[:, where:where + n]
            v = A[:, top[0]:top[0] + n]
            top[0] += n
            assert top[0] <= ARENA, top
            return v

        cut(NSLOT * SLOT)

        def slot(n):
            return A[:, (n % NSLOT) * SLOT:(n % NSLOT + 1) * SLOT]

        def w_in(n):
            return slot(n).rearrange("p (k n) -> p k n", k=NC)

        def w_down(n):
            return slot(n).rearrange("p (k n) -> p k n", k=NF)

        def landed(n):
            return 16 * (n // NSLOT + 1)

        def chan(v):
            return v.rearrange("p (c t) -> p c t", c=NC)

        xT = chan(cut(NC * T))
        c0 = at["maskp"][0]
        common = cut(c0)
        par = cut(104 + 65)
        ssT = cut(64)
        oneka = cut(8)

        def cst(name, n=None):
            o, w = at[name]
            return common[:, o:o + w]

        ident, onesd, ones, bones = cst("ident"), cst("onesd"), cst("ones"), cst("bones")
        eps_ln, eps_lnx = common[:, at["eps"][0]:at["eps"][0] + 1], common[:, at["eps"][0] + 1:at["eps"][0] + 2]
        mixv = [par[:, 8 * i:8 * i + 8] for i in range(6)]
        dw0, aw0, kk0, ka, rkv_, lnx0, lnx1 = [par[:, 48 + 8 * i:56 + 8 * i] for i in range(7)]
        plv = [[[par[:, 104 + 8 * (4 * l + 2 * j + k):112 + 8 * (4 * l + 2 * j + k)] for k in range(2)]
                for j in range(2)] for l in range(2)]
        subv = par[:, 168:169]
        base = top[0]

        rT, kT_, vT_, sgT, T1, T2, T3 = [chan(cut(NC * T)) for _ in range(7)]
        lora0 = top[0]
        dw1 = cut(512).rearrange("p (k n) -> p k n", k=NC)
        aw1 = cut(512).rearrange("p (k n) -> p k n", k=NC)
        gw1 = cut(1024).rearrange("p (k n) -> p k n", k=NC)
        dw2, aw2 = cut(1024), cut(1024)
        gw2 = cut(1024)
        hg = cut(T)
        hw, ha = cut(T)[0:64, :], cut(T)[0:64, :]
        XI, XU, YI, LM = [cut(1024, lora0 + 1024 * i).rearrange("p (c s) -> p c s", c=NC) for i in range(4)]
        o = SLOT
        nR = at["ustrict"][0] - c0
        rconst = cut(nR, o)

        def rc(name):
            a, w = at[name]
            return rconst[:, a - c0:a - c0 + w]

        assert nR <= 3072
        STZ = cut(1024, 5 * SLOT + 3072).rearrange("p (c n) -> p c n", c=NC)
        QW = cut(1024, o + 3072).rearrange("p (c n) -> p c n", c=NC)
        RAV, BK, EX = [], [], []
        for o in (2 * SLOT, 0):
            RAV.append(cut(NC * 192, o).rearrange("p (c n) -> p c n", c=NC))
            BK.append(cut(NC * 128, o + 1536).rearrange("p (c n) -> p c n", c=NC))
            EX.append([cut(512, o + 2560 + 512 * i).rearrange("p (c n) -> p c n", c=NC) for i in range(3)])
        o = 3 * SLOT
        SAV = cut(1024, o).rearrange("p (h n) -> p h n", h=H)
        BKt = cut(1024, o + 1024).rearrange("p (c n) -> p c n", c=NC)
        GH = cut(2048, o + 2048).rearrange("p (h n) -> p h n", h=H)
        STS = cut(4096, 4 * SLOT).rearrange("p (c b n) -> p c b n", c=NC, b=SB)
        NAT = [cut(1024, 5 * SLOT + 1024 * i) for i in range(2)]
        U = cut(512, 5 * SLOT + 2048).rearrange("p (c n) -> p c n", c=NC)
        MV = cut(512, 5 * SLOT + 2560).rearrange("p (c n) -> p c n", c=NC)
        QS = NAT[0].rearrange("p (c w t) -> p c w t", c=NC, w=2)
        SAVB = [cut(512, 2 * SLOT + 512 * i).rearrange("p (b n) -> p b n", b=SB) for i in range(2)]

        top[0] = base
        YA = chan(cut(NC * T))
        CT = chan(cut(NC * T))
        SQ = chan(cut(NC * T))
        experts0 = base + NC * T
        top[0] = experts0
        XTM = cut(3 * D).rearrange("p (t n) -> p t n", t=3)
        SelM = [cut(3 * CAP).rearrange("p (t n) -> p t n", t=3) for _ in range(2)]
        HS = cut(F_)
        top[0] += (-top[0]) % 8

        def split(name, n):
            return [nc.alloc_sbuf_tensor_at(f"{name}_{part}", [P, n], FR, offset=arena_at + 4 * (top[0] + i * n))
                    for i, part in enumerate(("hi", "lo"))], cut(2 * n)

        WS = [split(f"w{i}", QUARTER)[0] for i in range(NB)]
        Xg, oXg = split("xg", D)
        Xg = [x[:, :].rearrange("p (c n) -> p c n", c=NC) for x in Xg]
        oXg = oXg[:, 0:D].rearrange("p (c n) -> p c n", c=NC)
        HT, oHT = split("ht", F_)
        YY, oYY = zip(*[split(f"y{e}", D) for e in range(2)])
        oYY = oYY[0][:, 0:D]
        SG = [nc.alloc_sbuf_tensor_at(f"sg{e}", [P, T], FR, offset=arena_at + 4 * (top[0] + e * T)) for e in range(2)]
        oSG = cut(2 * T)[:, 0:T]
        assert top[0] >= base + 3 * NC * T
        RS = cut(T)
        rw = cut(NC * E_).rearrange("p (c n) -> p c n", c=NC)
        rbB = cut(E_)
        mconst0 = at["ustrict"][0]
        nM = at["caus"][0] - mconst0
        mconst = cut(nM)

        def mc(name):
            a, w = at[name]
            return mconst[:, a - mconst0:a - mconst0 + w]

        rt = [cut(48) for _ in range(8)]
        pr6 = cut(72).rearrange("p (g n) -> p g n", g=12)
        gs = [cut(12) for _ in range(4)]
        rank3 = cut(48).rearrange("p (t n) -> p t n", t=3)
        gate3 = cut(48).rearrange("p (t n) -> p t n", t=3)
        cntf = cut(16)
        cntp = cut(8)
        rkp, gtp, gsl = [cut(3) for _ in range(2)], [cut(3) for _ in range(2)], [cut(1) for _ in range(2)]
        top[0] = base
        aKT, aQT, aOT = [chan(cut(NC * T)) for _ in range(3)]
        assert top[0] == base + 3 * NC * T
        aVT = aOT
        VTM = cut(4 * D).rearrange("p (t n) -> p t n", t=4)
        KTM0 = top[0]
        KTM = cut(4 * D).rearrange("p (t n) -> p t n", t=4)
        PGK = [cut(2048, KTM0), cut(2048)]
        PGV = [cut(2048, KTM0 + 2048), cut(2048)]
        PGK = [v.rearrange("p (g n) -> p g n", g=2) for v in PGK]
        PGV = [v.rearrange("p (g n) -> p g n", g=2) for v in PGV]
        k0_ = top[0]
        KTs = [cut(2048).rearrange("p (c n) -> p c n", c=NC), cut(2048, SLOT).rearrange("p (c n) -> p c n", c=NC)]
        PP = [cut(544, k0_ + 544 * i).rearrange("p (j n) -> p j n", j=2) for i in range(2)]
        AT = [cut(384, k0_ + 1088 + 384 * i).rearrange("p (k n) -> p k n", k=3) for i in range(2)]
        Qbd = [cut(1168), cut(1168, SLOT + 2048)]
        PS = [cut(320), cut(320, SLOT + 3216)]
        ATs = [v.rearrange("p (k n) -> p k n", k=3) for v in (cut(192), cut(192, SLOT + 3536))]
        SCB = (4, 7)
        aconst0 = at["caus"][0]
        aconst = cut(const.shape[1] - aconst0)

        def ac(name):
            a, w = at[name]
            return aconst[:, a - aconst0:a - aconst0 + w]

        lamt = cut(256)
        lamp = cut(128)
        lams = cut(8)
        st4 = [cut(8) for _ in range(2)]
        aRS = cut(T, k0_)
        aSQ = chan(cut(NC * T, KTM0))
        OUTT = A[:, base:base + 3 * D].rearrange("p (t n) -> p t n", t=3)

        def bank(b, n=512):
            return ps[:, b, 0:n]

        def heads(v):
            return v

        pw = [(0, 112), (112, 112), (224, 32)]

        block = ctx.enter_context(nc.Block())
        xp_rows = I["x_prompt"][0]
        xs_rows = I["x_sample"].rearrange("b s d -> (b s) d")

        def prime(eng, who):
            for name in CHUNK_PRIMED.get(who, ()):
                eng.sem_inc(S(name), 1)
            eng.sem_inc(S("o_" + who), 1)
            if who == "dve":
                eng.sem_inc(S("add_done"), 1)

        def apart(eng):
            eng.sem_inc(S("apart"), 1)

        def over(stage, n, k):
            for who, stages in OVER.items():
                at_ = 1
                for name, adds in stages:
                    if name == stage:
                        return S("o_" + who), sum(a for _, a in stages) * n + at_ + k
                    at_ += adds

        def overflow(eng, l, who, block, start=None):
            adds = sum(a for _, a in OVER[who])

            def skip(k, n):
                eng.wait_ge(S("o_" + who), adds * n + 1)
                eng.sem_inc(S("o_" + who), adds * k)

            more = NBLK - 1
            most = eng.value_load(cnt_i[0:1, E_:E_ + 1], min_val=0, max_val=T)
            with eng.If(most > CAP):
                with eng.Fori(0, E_) as i:
                    cnt = eng.value_load(cnt_i[0:1, bass.ds(i, 1)], min_val=0, max_val=T)
                    if start:
                        start(i)
                        eng.drain()
                    with eng.Fori(1, NBLK) as b:
                        n = NOV * l + more * i + b - 1
                        with eng.If(cnt > b * CAP):
                            block(i, b, n)
                        with eng.Else():
                            skip(1, n)
            with eng.Else():
                skip(NOV, NOV * l)

        def wait(eng, sem, value):
            if isinstance(value, int) and value <= 0:
                return
            eng.wait_ge(sem, value)

        @block.sync
        def _(sp):
            prime(sp, "sp")

            def load(n, src):
                sp.dma_start(w_in(n) if src.shape[0] == D else w_down(n),
                             src.rearrange("(k p) n -> p k n", p=P)).then_inc(S(f"w_full{n % NSLOT}"), 16)

            def ld(dst, src, name):
                sp.dma_start(dst, src).then_inc(S(name), 16)

            cd = I["const"]
            ld(common, cd[:, 0:c0], "in_common")
            rows = T3.rearrange("p c t -> p (c t)")
            xrow = A[:, base:base + 3 * D].rearrange("p (t n) -> p t n", t=3)
            prow = A[:, base + 3 * D:base + 3 * D + 128]
            prow2 = A[:, base + 3 * D + 128:base + 3 * D + 256]
            srow = A[:, base + 3 * D + 256:base + 3 * D + 384]
            ld(xrow[0:N_META, 0, :], I["meta_tokens"], "in_x")
            ld(xrow[N_META:P, 0, :], xp_rows[0:P - N_META, :], "in_x")
            ld(xrow[:, 1, :], xp_rows[P - N_META:2 * P - N_META, :], "in_x")
            ld(xrow[0:16, 2, :], xp_rows[2 * P - N_META:SEQ, :], "in_x")
            ld(xrow[16:80, 2, :], xs_rows, "in_x")
            ld(prow[0:48, :], I["rwkv_mix"][0].rearrange("i (c p) -> (i c) p", p=P), "in_par")
            ld(prow[48:56, :], I["rwkv_decay_w0"][0].rearrange("(c p) -> c p", p=P), "in_par")
            ld(prow[56:64, :], I["rwkv_a_w0"][0].rearrange("(c p) -> c p", p=P), "in_par")
            ld(prow[64:80, :], I["rwkv_kk_ka"][0].rearrange("i (c p) -> (i c) p", p=P), "in_par")
            ld(prow[80:88, :], I["rwkv_r_k"][0].rearrange("(c h) n -> c (h n)", h=2), "in_par")
            ld(prow[88:104, :], I["rwkv_lnx"][0].rearrange("i (c p) -> (i c) p", p=P), "in_par")
            ld(prow2[0:64, :], I["post_ln"].rearrange("l j k (c p) -> (l j k c) p", p=P), "in_par")
            ld(prow2[64:65, :], I["diff_subln"], "in_par")
            ld(srow[0:64, :], I["state_shift"].rearrange("b a (c p) -> (b a c) p", p=P), "in_par")
            wrkv = I["rwkv_w_rkv"][0]
            for i in range(3):
                for j in range(2):
                    load(L_RKV + 2 * i + j, wrkv[i][:, 512 * j:512 * j + 512])
            wout = I["rwkv_w_out"][0]
            sp.wait_ge(S("out_wkvp"), 32)
            sp.wait_ge(S("out_wkvs0"), 64)
            sp.wait_ge(S("out_wkvs1"), 64)
            load(L_WO, wout[:, 0:512])
            load(L_WO + 1, wout[:, 512:1024])

            def experts(layer, n0):
                wg, wu, wd = I["moe_w_gate"][layer], I["moe_w_up"][layer], I["moe_w_down"][layer]

                def fetch(n, j, expert, k, sem):
                    src = (wg, wu, wd)[k][bass.ds(expert, 1)].rearrange("a (k p) n -> p (a k) n", p=P)
                    sp.dma_start(w_in(n) if k < 2 else w_down(n), src).then_inc(sem, 16)

                def pair(j, first):
                    for e in range(2):
                        for k in range(3):
                            m = 3 * e + k
                            if first and e == 1 and k == 0:
                                more_blocks()
                            if first:
                                if layer == 0 and m >= 4:
                                    sp.wait_ge(S("proj_mm"), 4 * (m - 3))
                                if layer == 1 and m < 4:
                                    sp.wait_ge(S("proj_mm"), 8 + 4 * ((2, 3, 4, 5)[m] + 1))
                                if layer == 1 and m == 3:
                                    sp.wait_ge(S("past_mm"), SB)
                                if layer == 1 and m >= 4:
                                    sp.wait_ge(S("proj_mm"), 8 + 24 + 4 * (m - 3))
                            else:
                                sp.wait_ge(S("w_lo"), NQ * (E_ * layer + 2 * (j - 1) + e) + 4 * k + 4)
                            fetch(n0 + m, m, 2 * j + e, k, S(f"w_full{(n0 + m) % NSLOT}"))

                def more_blocks():
                    sp.wait_ge(S("proj_mm"), 8 if layer == 0 else 8 + 24 + 8)
                    sp.wait_ge(S("route_ready"), layer + 1)

                    def block(i, b, n):
                        sp.wait_ge(*over("o_sel", n, 0))
                        for k in range(3):
                            fetch(n0 + 3 + k, k, i, k, S("o_sp"))
                    overflow(sp, layer, "sp", block)
                    sp.wait_ge(*over("o_add", NOV * (layer + 1) - 1, 8))

                pair(0, True)
                with sp.Fori(1, PAIRS) as j:
                    pair(j, False)

            experts(0, L_MOE0)
            wkv = I["w_kv_shared"]
            for j in range(6):
                sp.wait_ge(S("w_lo"), NQ * (E_ - 2 + j // 3) + 4 * (j % 3) + 4)
                if j < 4:
                    load(L_KV + j, wkv[:, 512 * j:512 * j + 512])
                else:
                    load(L_Q + j - 4, I["diff_w_q"][0][:, 512 * (j - 4):512 * (j - 4) + 512])
            for j in range(2):
                sp.wait_ge(S("proj_mm"), 8 + 4 * (j + 1))
                load(L_DO + j, I["diff_w_out"][0][:, 512 * j:512 * j + 512])
            experts(1, L_MOE1)

        @block.gpsimd
        def _(pool):
            def ld(dst, src, name):
                pool.dma_start(dst, src).then_inc(S(name), 16)

            cd = I["const"]
            ld(dw1, I["rwkv_decay_w1"][0].rearrange("(k p) n -> p k n", p=P), "in_lora")
            ld(aw1, I["rwkv_a_w1"][0].rearrange("(k p) n -> p k n", p=P), "in_lora")
            ld(gw1, I["rwkv_g_w1"][0].rearrange("(k p) n -> p k n", p=P), "in_lora")
            ld(dw2[0:64, :], I["rwkv_decay_w2"][0], "in_lora")
            ld(aw2[0:64, :], I["rwkv_a_w2"][0], "in_lora")
            ld(gw2, I["rwkv_g_w2"][0], "in_lora")
            ld(O["new_shift_prompt"][0], I["x_prompt"][0, SEQ - 1:SEQ, :], "out")
            ld(O["new_shift_sample"].rearrange("b a d -> (b a) d"), I["x_sample"][:, SS - 1, :], "out")
            pool.wait_ge(S("rkv_mm"), after("rkv_mm", 8))
            ld(rconst, cd[:, c0:c0 + nR], "in_rconst")
            pool.wait_ge(S("rkv_mm"), after("rkv_mm", 24))
            sw = I["state_wkv"]
            for bp in range(4):
                if bp >= 2:
                    pool.wait_ge(S("nat_in_mm"), after("nat_in_mm", 2 * (bp - 1)))
                for e in range(2):
                    ld(NAT[bp % 2][64 * e:64 * e + 64, :].rearrange("p (h j) -> p h j", h=H),
                       sw[2 * bp + e, 0].rearrange("h i j -> i h j"), f"in_nat{bp % 2}")
            pool.wait_ge(S("wkvp_ready"), after("wkvp_ready", 2))
            for hp in range(2):
                pool.dma_start(O["new_wkv_prompt"][0, 0].rearrange("(c e) i j -> e i c j", e=2)[hp],
                               QW[64 * hp:64 * hp + 64, :, 64 * hp:64 * hp + 64]).then_inc(S("out_wkvp"), 16)
            for bp in range(4):
                pool.wait_ge(S("wkvs_ready"), after("wkvs_ready", 2 * (bp + 1)))
                for e in range(2):
                    pool.dma_start(O["new_wkv_sample"][2 * bp + e, 0].rearrange("h i j -> i h j"),
                                   NAT[bp % 2][64 * e:64 * e + 64, :].rearrange("p (h j) -> p h j", h=H)
                                   ).then_inc(S(f"out_wkvs{bp % 2}"), 16)
            pool.wait_ge(S("x_ready"), 8)
            ld(mconst, cd[:, mconst0:mconst0 + nM], "in_mconst")
            ld(rw, I["router_w"].rearrange("(c p) n -> p c n", p=P), "in_mconst")
            ld(rbB, I["router_b"].unsqueeze(0).to_broadcast([P, E_]), "in_mconst")
            pool.wait_ge(S("x_ready"), 16)
            ld(aconst, cd[:, aconst0:const.shape[1]], "in_aconst")
            ld(lamt, I["diff_lambda"][0].rearrange("i n -> (i n)").unsqueeze(0).to_broadcast([P, 256]), "in_aconst")
            ld(pt_i[:, :], I["page_table"].rearrange("b n -> (b n)").unsqueeze(0), "in_pt")
            for name, ready, tile in (("k", "ktm_ready", KTM), ("v", "vtm_ready", VTM)):
                op = O[f"new_{name}_prompt"][0].rearrange("t h n -> t (h n)")
                os_ = O[f"new_{name}_sample"].rearrange("b s h n -> (b s) (h n)")
                pool.wait_ge(S(ready), after(ready, 8))
                for t, (t0, n) in enumerate(KTILE):
                    dst = op[t0:t0 + n, :] if t < 3 else os_
                    pool.dma_start(dst, tile[0:n, t, :]).then_inc(S(f"out_{name}tm"), 16)
            pool.wait_ge(S("in_pt"), 16)
            pool.wait_ge(S("out_ktm"), 64)
            for b in range(SB):
                pages = [pool.value_load(pt_i[0:1, NPG * b + g:NPG * b + g + 1], min_val=0,
                                         max_val=I["cache_k"].shape[0] - 1) for g in range(NPG)]
                for cache, PG, name in (("cache_k", PGK, "in_pk"), ("cache_v", PGV, "in_pv")):
                    if b >= 2 and PG is PGK:
                        pool.wait_ge(S("kt_mm"), 4 * (b - 1))
                    if b >= 2 and PG is PGV:
                        pool.wait_ge(S("past_mm"), b - 1)
                    src = I[cache].rearrange("a p h n -> a p (h n)")
                    for g in range(NPG):
                        pool.dma_start(PG[b % 2][:, g, :], src[bass.ds(pages[g], 1)].rearrange("a p n -> p (a n)")
                                       ).then_inc(S(f"{name}{b % 2}"), 16)
            pool.wait_ge(S("x_ready"), 24)
            ld(mconst, cd[:, mconst0:mconst0 + nM], "in_mconst")
            ld(rw, I["router_w"].rearrange("(c p) n -> p c n", p=P), "in_mconst")
            ld(rbB, I["router_b"].unsqueeze(0).to_broadcast([P, E_]), "in_mconst")
            pool.wait_ge(S("y_rows"), 6)
            yp = O["y_prompt"][0]
            ld(yp[0:128, :], OUTT[:, 0, :], "out")
            ld(yp[128:256, :], OUTT[:, 1, :], "out")
            ld(O["y_sample"].rearrange("b s d -> (b s) d"), OUTT[0:64, 2, :], "out")
            pool.wait_ge(S("out"), 16 * 5)
            pool.wait_ge(S("out_wkvp"), 32)
            pool.wait_ge(S("out_wkvs0"), 64)
            pool.wait_ge(S("out_wkvs1"), 64)
            pool.wait_ge(S("out_ktm"), 64)
            pool.wait_ge(S("out_vtm"), 64)


        @block.tensor
        def _(pe):
            prime(pe, "pe")
            def mm(out, lhsT, rhs, start=True, stop=True):
                return pe.matmul(out, lhsT, rhs, start=start, stop=stop)

            def wait_w(n, more=0):
                pe.wait_ge(S(f"w_full{n % NSLOT}"), landed(n) + more)

            pe.wait_ge(S("in_common"), 16)
            pe.wait_ge(S("in_par"), 16 * 9)
            prow = A[:, base + 3 * D:base + 3 * D + 128]
            prow2 = A[:, base + 3 * D + 128:base + 3 * D + 256]
            srow = A[:, base + 3 * D + 256:base + 3 * D + 384]
            xrow = A[:, base:base + 3 * D].rearrange("p (t n) -> p t n", t=3)
            pe.transpose(ps[:, 0, 0:104], prow[0:104, :], ident[0:104, 0:104])
            pe.transpose(ps[:, 0, 128:193], prow2[0:65, :], ident[0:65, 0:65])
            pe.transpose(ps[:, 0, 256:320], srow[0:64, :], ident[0:64, 0:64]).then_inc(S("par_mm"), 1)
            pe.wait_ge(S("in_x"), 16 * 5)
            for t, (t0, n) in enumerate(TOK):
                for hf in range(2):
                    for c in range(4):
                        i = pe.transpose(ps[:, 1 + 2 * t + hf, n * c:n * c + n],
                                         xrow[0:n, t, P * (4 * hf + c):P * (4 * hf + c) + P], ident[0:n, 0:n])
                    i.then_inc(S("xt_mm"), 1)

            for i, X in enumerate((T1, T2, T3)):
                for co in range(NC):
                    n = 8 * i + co
                    w = w_in(L_RKV + 2 * i + co // 4)
                    wait_w(L_RKV + 2 * i + co // 4)
                    if n >= 4:
                        pe.wait_ge(S("rkv_ev"), after("rkv_ev", n - 3))
                    for k in range(NC):
                        if co == 0:
                            pe.wait_ge(S("mix_ready"), after("mix_ready", 8 * i + k + 1))
                        m = mm(bank(n % 4, T), w[:, k, P * (co % 4):P * (co % 4) + P], X[:, k, :], k == 0, k == NC - 1)
                    m.then_inc(S("rkv_mm"), 1)
            pe.wait_ge(S("in_lora"), 96)
            for i, (w, X, M) in enumerate(((dw1, T1, 64), (aw1, T2, 64), (gw1, T3, 128))):
                pe.wait_ge(S("mix_ready"), after("mix_ready", 8 * (i + 4)))
                for k in range(NC):
                    m = mm(ps[0:M, 4 + i, 0:T], w[:, k, :], X[:, k, :], k == 0, k == NC - 1)
                m.then_inc(S("lora_mm"), 1)
            pe.wait_ge(S("lora_ev"), after("lora_ev", 3))
            for i, (w, X) in enumerate(((dw2, hw), (aw2, ha))):
                for co in range(NC):
                    n = 8 * i + co
                    if n >= 4:
                        pe.wait_ge(S("lz_ev"), after("lz_ev", n - 3))
                    mm(bank(4 + n % 4, T), w[0:64, P * co:P * co + P], X).then_inc(S("lz_mm"), 1)
            pe.wait_ge(S("rkv_ev"), after("rkv_ev", 24))
            for c in range(NC):
                pe.wait_ge(S("kksq_ready"), after("kksq_ready", c + 1))
                if c >= 4:
                    pe.wait_ge(S("kks_ev"), after("kks_ev", c - 3))
                mm(bank(c % 4, T), bones, T2[:, c, :]).then_inc(S("kks_mm"), 1)
            pe.wait_ge(S("lz_ev"), after("lz_ev", 16))
            for bp in range(4):
                pe.wait_ge(S(f"in_nat{bp % 2}"), 32 * (bp // 2 + 1))
                for hf in range(2):
                    n = 2 * bp + hf
                    if n >= 4:
                        pe.wait_ge(S("nat_ev"), after("nat_ev", n - 3))
                    for c in range(4):
                        m = pe.transpose(ps[:, 4 + n % 4, P * c:P * c + P],
                                         NAT[bp % 2][:, P * (4 * hf + c):P * (4 * hf + c) + P], ident)
                    m.then_inc(S("nat_in_mm"), 1)
            pe.wait_ge(S("nat_ev"), after("nat_ev", 8))
            pe.wait_ge(S("kks_ev"), after("kks_ev", 8))

            def chunk(n, par, sample):
                rav, bk = RAV[par], BK[par]
                pe.wait_ge(S("ops_ready"), after("ops_ready", 1 * n + 1))
                pe.wait_ge(S("u_ready"), after("u_ready", 2 * n))
                for b, src, o0, name in ((0, bk, 0, "bkt_mm"), (2, rav, 64, "avt_mm")):
                    for hf in range(2):
                        for c in range(4):
                            m = pe.transpose(ps[:, b + hf, P * c:P * c + P], src[:, 4 * hf + c, o0:o0 + P], ident)
                        m.then_inc(S(name), 1)
                pe.wait_ge(S("sa_ready"), after("sa_ready", 2 * n))
                pe.wait_ge(S("o_ready"), after("o_ready", 1 * n))
                pe.wait_ge(S("st_ready"), 1 * n + 1)
                for hp in range(2):
                    q = slice(64 * hp, 64 * hp + 64)
                    for hf in range(2):
                        for c in range(4):
                            m = mm(ps[:, 4 + 2 * hp + hf, P * c:P * c + P], bk[q, 4 * hf + c, :], rav[q, 4 * hf + c, 0:128])
                        m.then_inc(S("gh_mm"), 1)
                pe.wait_ge(S("bkt_ready"), 2 * n + 2)
                apart(pe)
                for hp in range(2):
                    q = slice(64 * hp, 64 * hp + 64)
                    for c in range(NC):
                        o = P * (c % 4) + 64 * hp
                        m = mm(ps[q, c // 4, o:o + 64], rav[q, c, 64:128], bk[q, c, 0:64])
                    m.then_inc(S("l_mm"), 1)
                pe.wait_ge(S("sv_ready"), 2 * n + 2)
                apart(pe)
                for hf in range(2):
                    for hp in range(2):
                        q = slice(64 * hp, 64 * hp + 64)
                        for c in range(4 * hf, 4 * hf + 4):
                            o = P * (c % 4) + 64 * hp
                            m = mm(ps[q, 2 + hf, o:o + 64], bk[q, c, 0:64], rav[q, c, 64:128])
                    m.then_inc(S("lt_mm"), 1)
                pe.wait_ge(S("gh_ready"), 4 * n + 4)
                pe.wait_ge(S("lm_ready"), 2 * n + 2)
                levels = 2 if sample else LEVELS - 1
                for lv in range(1, levels + 1):
                    for hf in range(2):
                        if lv == 1:
                            pe.wait_ge(S("inv_ready"), 11 * n + 1)
                        else:
                            pe.wait_ge(S("inv_ready"), 11 * n + 1 + 2 * (lv - 2) + hf + 1)
                            pe.wait_ge(S("y_ready"), 10 * n + 2 * (lv - 2) + hf + 1)
                        for c in range(4):
                            m = mm(ps[:, 4 + hf, P * c:P * c + P], LM[:, 4 * hf + c, :], XU[:, 4 * hf + c, :])
                        m.then_inc(S("y_mm"), 1)
                    for hf in range(2):
                        pe.wait_ge(S("y_ready"), 10 * n + 2 * (lv - 1) + hf + 1)
                        bx = (6, 7) if hf == 0 else (0, 1)
                        if lv < levels:
                            for c in range(4):
                                mm(ps[:, bx[0], P * c:P * c + P], YI[:, 4 * hf + c, :], XI[:, 4 * hf + c, :])
                        for c in range(4):
                            m = mm(ps[:, bx[1], P * c:P * c + P], XI[:, 4 * hf + c, :], YI[:, 4 * hf + c, :])
                        m.then_inc(S("xu_mm"), 1)
                    if lv == 1:
                        for hf in range(2):
                            for c in range(4):
                                for hp in range(2):
                                    h = 2 * (4 * hf + c) + hp
                                    m = mm(ps[64 * hp:64 * hp + 64, 2 + hf, 64 * c:64 * c + 64],
                                           GH[64:128, h, 64:128], SAV[64:128, h, :])
                            m.then_inc(S("mv_mm"), 1)
                pe.wait_ge(S("mv_ready"), 2 * n + 2)
                pe.wait_ge(S("inv_ready"), 11 * n + 2 * levels + 1)
                apart(pe)
                if sample:
                    for hp in range(2):
                        q = slice(64 * hp, 64 * hp + 64)
                        for hf in range(2):
                            for c in range(4):
                                ov = ps[q, 2 * hp + hf, P * c:P * c + P].rearrange("p (w t) -> p w t", w=2)
                                rv = rav[q, 4 * hf + c, 0:128].rearrange("p (w t) -> p w t", w=2)
                                for b in range(SB):
                                    m = mm(ov[:, :, 8 * b:8 * b + 8], STS[q, 4 * hf + c, b, :], rv[:, :, 8 * b:8 * b + 8])
                            m.then_inc(S("qs_mm"), 1)
                    pe.wait_ge(S("qs_ready"), 4)
                for hf in range(2):
                    for c in range(4):
                        for hp in range(2):
                            q = slice(64 * hp, 64 * hp + 64)
                            out = ps[q, 2 + hf, 64 * c:64 * c + 64]
                            if sample:
                                m = mm(out, QS[q, 4 * hf + c, 1, :], ident[q, q])
                            else:
                                m = mm(out, rav[q, 4 * hf + c, 64:128], STZ[q, 4 * hf + c, q])
                    m.then_inc(S("u_mm"), 1)
                pe.wait_ge(S("u_ready"), after("u_ready", 2 * n + 2))
                apart(pe)
                for hp in range(2):
                    q = slice(64 * hp, 64 * hp + 64)
                    for c in range(NC):
                        m = mm(ps[0:64, 4 + hp, 64 * c:64 * c + 64], XU[q, c, q], U[q, c, :])
                    m.then_inc(S("sa_mm"), 1)
                pe.wait_ge(S("sa_ready"), after("sa_ready", 2 * n + 2))
                for c in range(NC):
                    if not sample:
                        mm(ps[:, 6, 64 * c:64 * c + 64], STZ[:, c, :], rav[:, c, 0:64], True, False)
                    for hp in range(2):
                        m = mm(ps[64 * hp:64 * hp + 64, 6, 64 * c:64 * c + 64], SAV[:, 2 * c + hp, :],
                               GH[:, 2 * c + hp, 0:64], sample, True)
                m.then_inc(S("o_mm"), 1)
                if not sample:
                    for c in range(NC):
                        for hp in range(2):
                            m = mm(ps[64 * hp:64 * hp + 64, 7, 64 * c:64 * c + 64], BKt[:, c, 64 * hp:64 * hp + 64],
                                   SAV[:, 2 * c + hp, :])
                    m.then_inc(S("st_mm"), 1)

            with pe.Fori(0, NFULL // 2) as i:
                for side in range(2):
                    chunk(2 * i + side, side, False)
            pe.wait_ge(S("tail_ready"), 1)
            chunk(NFULL, 0, False)
            chunk(NFULL + 1, 1, True)
            for h in range(H):
                c, hp = h // 2, h % 2
                pe.wait_ge(S("savb_ready"), h + 1)
                if c >= 2:
                    pe.wait_ge(S("sts_ready"), c - 1)
                if h == 0:
                    pe.wait_ge(S("o_ready"), after("o_ready", NFULL + 2))
                mm(ps[64 * hp:64 * hp + 64, 6 + c % 2, :], BKt[:, c, 64 * hp:64 * hp + 64],
                   SAVB[h % 2].rearrange("p b n -> p (b n)")).then_inc(S("ss_mm"), 1)
            for hf in range(2):
                for c in range(4):
                    m = pe.transpose(ps[:, 4 + hf, P * c:P * c + P], STZ[:, 4 * hf + c, :], ident)
                m.then_inc(S("wkvp_mm"), 1)
            pe.wait_ge(S("sts_ready"), 8)
            for bp in range(4):
                for hf in range(2):
                    n = 2 * bp + hf
                    if n >= 4:
                        pe.wait_ge(S("wkvs_ready"), after("wkvs_ready", n - 3))
                    for c in range(4):
                        m = pe.transpose(ps[:, n % 4, P * c:P * c + P],
                                         STS[:, 4 * hf + c, 2 * bp:2 * bp + 2, :].rearrange("p b n -> p (b n)"), ident)
                    m.then_inc(S("wkvs_mm"), 1)
            pe.wait_ge(S("wkvp_ready"), after("wkvp_ready", 2))
            for c in range(NC):
                if c >= 4:
                    pe.wait_ge(S("gn_c"), after("gn_c", c - 3))
                else:
                    pe.wait_ge(S("wkvs_ready"), after("wkvs_ready", 8))
                mm(bank(c % 4, T), bones, T3[:, c, :]).then_inc(S("gn_mm"), 1)
            for c in range(NC):
                pe.wait_ge(S("gn_sq"), after("gn_sq", c + 1))
                if c >= 4:
                    pe.wait_ge(S("gn_s"), after("gn_s", c - 3))
                mm(bank(4 + c % 4, T), bones, T1[:, c, :]).then_inc(S("gn_vm"), 1)
            for c in range(NC):
                pe.wait_ge(S("rkr_ready"), after("rkr_ready", c + 1))
                if c >= 4:
                    pe.wait_ge(S("bn_ev"), after("bn_ev", c - 3))
                mm(bank(c % 4, T), bones, rT[:, c, :]).then_inc(S("bn_mm"), 1)
            pe.wait_ge(S("gn_s"), after("gn_s", 8))
            for c in range(NC):
                if c >= 4:
                    pe.wait_ge(S("z_ready"), after("z_ready", c - 3))
                mm(bank(4 + c % 4, T), gw2[:, P * c:P * c + P], hg).then_inc(S("g_mm"), 1)
            pe.wait_ge(S("bn_ev"), after("bn_ev", 8))
            pe.wait_ge(S("z_ready"), after("z_ready", 8))

            def proj(n0, X, outs, freed, base_ev):
                for co in range(outs):
                    wait_w(n0 + co // 4)
                    w = w_in(n0 + co // 4)
                    if co >= 4:
                        pe.wait_ge(S(freed), base_ev + co - 3)
                    for k in range(NC):
                        m = mm(bank(co % 4, T), w[:, k, P * (co % 4):P * (co % 4) + P], X[:, k, :], k == 0, k == NC - 1)
                    m.then_inc(S("proj_mm"), 1)

            def layer_norm(i):
                for c in range(NC):
                    pe.wait_ge(S("ln_in"), 8 * i + c + 1)
                    m = mm(bank(6, T), onesd, YA[:, c, :], c == 0, c == NC - 1)
                m.then_inc(S("ln_mean"), 1)
                for c in range(NC):
                    pe.wait_ge(S("ln_sq"), 8 * i + c + 1)
                    m = mm(bank(7, T), onesd, SQ[:, c, :], c == 0, c == NC - 1)
                m.then_inc(S("ln_var"), 1)

            def gather(par, half):
                for c in range(4 * half, 4 * half + 4):
                    for t, (t0, k) in enumerate(TOK):
                        m = mm(ps[:, half, P * (c % 4):P * (c % 4) + P], XTM[0:k, t, P * c:P * c + P],
                               SelM[par][0:k, t, :], t == 0, t == 2)
                return m

            def turn_select(par):
                for t, (t0, k) in enumerate(TOK):
                    pe.transpose(ps[:, 3, t0:t0 + k], SelM[par][0:k, t, :], ident[0:k, 0:k])
                for t, (t0, k) in enumerate(TOK):
                    m = mm(ps[:, 3, 400:401], SelM[par][0:k, t, :], gtp[par][0:k, t:t + 1], t == 0, t == 2)
                return m

            def more_block(n0, n):
                pe.wait_ge(*over("o_sel", n, 1))
                gather(0, 0)
                gather(0, 1).then_inc(S("o_pe"), 1)
                pe.wait_ge(*over("o_xg", n, 1))
                pe.wait_ge(*over("o_weights", n, 48))
                for k in range(2):
                    w = w_in(n0 + 3 + k)
                    for c in range(NC):
                        m = mm(bank(2 + k), oXg[:, c, :], w[:, c, :], c == 0, c == NC - 1)
                m.then_inc(S("o_pe"), 1)
                pe.wait_ge(*over("o_h", n, 1))
                for f in range(NF):
                    pe.transpose(ps[:, 2, P * f:P * f + P], HS[:, P * f:P * f + P], ident)
                turn_select(0).then_inc(S("o_pe"), 1)
                pe.wait_ge(*over("o_ht", n, 1))
                w = w_down(n0 + 5)
                for hf in range(2):
                    for f in range(NF):
                        m = mm(bank(4 + hf), oHT[:, P * f:P * f + P], w[:, f, 512 * hf:512 * hf + 512], f == 0, f == NF - 1)
                m.then_inc(S("o_pe"), 1)
                pe.wait_ge(*over("o_y", n, 1))
                for c in range(NC):
                    if c >= 2:
                        pe.wait_ge(*over("o_add", n, c - 1))
                    mm(bank(6 + c % 2, T), oYY[:, P * c:P * c + P], oSG).then_inc(S("o_pe"), 1)

            def three(out, x, w, start, stop):
                mm(out, x[0], w[0], start, False)
                mm(out, x[1], w[0], False, False)
                return mm(out, x[0], w[1], False, stop)

            def quarter(n):
                pe.wait_ge(S("w_hi"), n + 1)
                pe.wait_ge(S("w_lo"), n + 1)

            def scatter(s):
                for c in range(NC):
                    pe.wait_ge(S("add_done"), 8 * s + 1 + max(c - 1, 0))
                    for e in range(2):
                        for h in range(2):
                            m = mm(bank(6 + c % 2, T), YY[e][h][:, P * c:P * c + P], SG[e][:, :], e + h == 0, e + h == 2)
                    m.then_inc(S("sc_mm"), 1)

            def expert(l, n0, j, e, first, last):
                G = E_ * l + 2 * j + e
                pe.wait_ge(S("xg_hi"), 2 * G + 2)
                pe.wait_ge(S("xg_lo"), 2 * G + 2)
                for k in range(2):
                    wait(pe, S("ht_lo") if k == 0 else S("sg_ready"), G)
                    for q in range(4):
                        quarter(NQ * G + 4 * k + q)
                        b = (4 * k + q) % NB
                        for c in (2 * q, 2 * q + 1):
                            m = three(bank(2 + k), [Xg[h][:, c, :] for h in range(2)],
                                      [WS[b][h][:, 512 * (c % 2):512 * (c % 2) + 512] for h in range(2)], c == 0, c == NC - 1)
                        m.then_inc(S("w_used"), 1)
                more = not (last and e == 1)
                if more:
                    pe.wait_ge(S("sel_ready"), G + 2)
                    gather(1 - e, 0).then_inc(S("ga_mm"), 1)
                pe.wait_ge(S("h_ready"), G + 1)
                for f in range(NF):
                    m = pe.transpose(ps[:, 2, P * f:P * f + P], HS[:, P * f:P * f + P], ident)
                m.then_inc(S("turn_mm"), 1)
                if more:
                    gather(1 - e, 1).then_inc(S("gb_mm"), 1)
                if e == 0 and not first:
                    pe.wait_ge(S("y_lo"), 2 * G)
                    pe.wait_ge(S("sg_ready"), G)
                    scatter(PAIRS * l + j - 1)
                turn_select(e).then_inc(S("sgt_mm"), 1)
                pe.wait_ge(S("ht_hi"), G + 1)
                pe.wait_ge(S("ht_lo"), G + 1)
                wait(pe, S("y_lo"), 2 * G)
                for f in range(NF):
                    quarter(NQ * G + 8 + f)
                    b = (8 + f) % NB
                    for hf in range(2):
                        m = three(bank(4 + hf), [HT[h][:, P * f:P * f + P] for h in range(2)],
                                  [WS[b][h][:, 512 * hf:512 * hf + 512] for h in range(2)], f == 0, f == NF - 1)
                    m.then_inc(S("w_used"), 1)

            def experts(l, n0):
                pe.wait_ge(S("x_ready"), 16 * l + 8)
                for t, (t0, n) in enumerate(TOK):
                    for hf in range(2):
                        for c in range(4):
                            m = pe.transpose(ps[0:n, 2 * t + hf, P * c:P * c + P], xT[:, 4 * hf + c, t0:t0 + n], ident)
                        m.then_inc(S("xtm_mm"), 1)
                pe.wait_ge(S("in_mconst"), 48 * (l + 1))
                for t, (t0, n) in enumerate(TOK):
                    for c in range(NC):
                        m = mm(ps[0:n, 6, E_ * t:E_ * t + E_], xT[:, c, t0:t0 + n], rw[:, c, :], c == 0, c == NC - 1)
                m.then_inc(S("rt_mm"), 1)
                pe.wait_ge(S("msk_ready"), l + 1)
                for t in range(3):
                    for u in range(t + 1):
                        mm(ps[:, 7, E_ * t:E_ * t + E_], mc("ustrict") if u == t else ones, rt[6][:, E_ * u:E_ * u + E_],
                           u == 0, u == t)
                for u in range(3):
                    m = mm(ps[:, 7, 64:64 + E_], ones, rt[6][:, E_ * u:E_ * u + E_], u == 0, u == 2)
                m.then_inc(S("rk_mm"), 1)
                pe.wait_ge(S("xtm_a"), 3 * (l + 1))
                pe.wait_ge(S("xtm_d"), 3 * (l + 1))
                pe.wait_ge(S("route_ready"), l + 1)
                overflow(pe, l, "pe", lambda i, b, n: more_block(n0, n))
                pe.wait_ge(*over("o_y", NOV * (l + 1) - 1, 1))
                pe.wait_ge(*over("o_add", NOV * (l + 1) - 1, 8))
                pe.wait_ge(S("sel_ready"), E_ * l + 1)
                gather(0, 0).then_inc(S("ga_mm"), 1)
                gather(0, 1).then_inc(S("gb_mm"), 1)
                for e in range(2):
                    expert(l, n0, 0, e, True, False)
                with pe.Fori(1, PAIRS - 1) as j:
                    for e in range(2):
                        expert(l, n0, j, e, False, False)
                for e in range(2):
                    expert(l, n0, PAIRS - 1, e, False, True)
                pe.wait_ge(S("y_lo"), 2 * E_ * (l + 1))
                pe.wait_ge(S("sg_ready"), E_ * (l + 1))
                scatter(PAIRS * (l + 1) - 1)

            proj(L_WO, T3, NC, "ln_in", 0)
            layer_norm(0)
            experts(0, L_MOE0)
            layer_norm(1)
            pe.wait_ge(S("x_ready"), 16)
            proj(L_KV, xT, 16, "kvq_ev", 0)
            for i, (X, name) in enumerate(((aKT, "ktr_mm"), (aVT, "vtr_mm"))):
                pe.wait_ge(S("kvq_ev"), 8 * (i + 1))
                for t, (t0, n) in enumerate(KTILE):
                    for hf in range(2):
                        j = 8 * i + 2 * t + hf
                        if j >= 4:
                            if j < 12:
                                pe.wait_ge(S("ktm_ready"), after("ktm_ready", min(j - 3, 8)))
                            else:
                                pe.wait_ge(S("vtm_ready"), after("vtm_ready", j - 11))
                        for c in range(4):
                            m = pe.transpose(ps[0:n, 4 + j % 4, P * c:P * c + P], X[:, 4 * hf + c, t0:t0 + n], ident)
                        m.then_inc(S(name), 1)
            pe.wait_ge(S("kvq_ev"), 16)
            proj(L_Q, xT, NC, "kvq_ev", 16)
            pe.wait_ge(S("kvq_ev"), 24)
            pe.wait_ge(S("vtm_ready"), after("vtm_ready", 8))
            pe.wait_ge(S("in_aconst"), 32)

            units = [(t, h) for t in range(3) for h in range(NH)]

            def scores(u):
                t, h = units[u]
                q0, nq = KTILE[t]
                nk = q0 + nq
                if u >= 2:
                    pe.wait_ge(S("p_exp"), 2 * (u - 1))
                for j in range(2):
                    q = slice(64 * j, 64 * j + 64)
                    b = 2 * (u % 2) + j
                    mm(ps[0:nq, b, 0:nk], aQT[q, h, q0:q0 + nq], aKT[q, h, 0:nk], True, False)
                    m = mm(ps[0:nq, b, q0:nk], ident[:, 0:nq], ac("caus")[:, 0:nq], False, True)
                m.then_inc(S("p_sc"), 1)

            def turn(u):
                t, h = units[u]
                q0, nq = KTILE[t]
                pe.wait_ge(S("p_am"), u + 1)
                if u >= 2:
                    pe.wait_ge(S("p_at"), u - 1)
                for kt in range(t + 1):
                    k0, n = KTILE[kt]
                    m = pe.transpose(ps[0:n, 4 + u % 2, P * kt:P * kt + nq], PP[u % 2][0:nq, 0, k0:k0 + n], ident[0:nq, 0:nq])
                m.then_inc(S("p_tr"), 1)

            def values(u):
                t, h = units[u]
                q0, nq = KTILE[t]
                pe.wait_ge(S("p_at"), u + 1)
                if u >= 2:
                    pe.wait_ge(S("p_oev"), u - 1)
                for kt in range(t + 1):
                    k0, n = KTILE[kt]
                    m = mm(ps[:, 6 + u % 2, 0:nq], VTM[0:n, kt, P * h:P * h + P], AT[u % 2][0:n, kt, 0:nq], kt == 0, kt == t)
                m.then_inc(S("p_av"), 1)

            NU = len(units)
            for i in range(NU + 2):
                if i < NU:
                    scores(i)
                if 1 <= i <= NU:
                    turn(i - 1)
                if i >= 2:
                    values(i - 2)
            pe.wait_ge(S("p_exp"), 2 * NU)
            pe.wait_ge(S("p_oev"), NU)
            def sample_scores(b):
                pe.wait_ge(S(f"in_pk{b % 2}"), 32 * (b // 2 + 1))
                if b:
                    pe.wait_ge(S("kts_a"), 2 * b)
                    pe.wait_ge(S("kts_d"), 2 * b)
                for g in range(NPG):
                    for hf in range(2):
                        for c in range(4):
                            m = pe.transpose(ps[:, 2 * g + hf, P * c:P * c + P],
                                             PGK[b % 2][:, g, P * (4 * hf + c):P * (4 * hf + c) + P], ident)
                        m.then_inc(S("kt_mm"), 1)
                pe.wait_ge(S("qbd_ready"), b + 1)
                if b >= 2:
                    pe.wait_ge(S("s_exp"), b - 1)
                qb = Qbd[b % 2][:, 0:1024].rearrange("p (c n) -> p c n", c=NC)
                sc = ps[:, SCB[b % 2], :]
                for c in range(NC):
                    mm(sc[:, 256:320], qb[:, c, :], aKT[:, c, TP:T], c == 0, False)
                w0 = TS - SS - 8 * b
                mm(sc[:, 256:320], ident, ac("win")[:, w0:w0 + TS], False, True)
                pe.wait_ge(S("kts_a"), 2 * b + 2)
                pe.wait_ge(S("kts_d"), 2 * b + 2)
                for c in range(NC):
                    m = mm(sc[:, 0:256], qb[:, c, :], KTs[b % 2][:, c, :], c == 0, c == NC - 1)
                m.then_inc(S("s_sc"), 1)

            def sample_values(b):
                pe.wait_ge(S("s_am"), b + 1)
                if b:
                    pe.wait_ge(S("s_at"), 2 * b)
                for kt in range(3):
                    n = P if kt < 2 else TS
                    m = pe.transpose(ps[0:n, 5, P * kt:P * kt + P], PS[b % 2][:, P * kt:P * kt + n], ident)
                m.then_inc(S("s_tr"), 1)
                pe.wait_ge(S(f"in_pv{b % 2}"), 32 * (b // 2 + 1))
                pe.wait_ge(S("s_at"), 2 * b + 2)
                if b:
                    pe.wait_ge(S("s_oev"), b)
                at_ = ATs[b % 2]
                for h in range(NH):
                    o = ps[:, 6, SS * h:SS * h + SS]
                    for g in range(2):
                        mm(o, PGV[b % 2][:, g, P * h:P * h + P], at_[:, g, SS * h:SS * h + SS], g == 0, False)
                    m = mm(o, VTM[0:TS, 3, P * h:P * h + P], at_[0:TS, 2, SS * h:SS * h + SS], False, True)
                m.then_inc(S("past_mm"), 1)

            sample_scores(0)
            for b in range(SB):
                if b + 1 < SB:
                    sample_scores(b + 1)
                sample_values(b)
            for c in range(NC):
                pe.wait_ge(S("sl_sq"), after("sl_sq", c + 1))
                if c >= 4:
                    pe.wait_ge(S("sl_s"), after("sl_s", c - 3))
                mm(bank(c % 4, T), ones, aSQ[:, c, :]).then_inc(S("sl_mm"), 1)
            pe.wait_ge(S("z2_ready"), after("z2_ready", 8))
            proj(L_DO, aOT, NC, "ln_in", 16)
            layer_norm(2)
            experts(1, L_MOE1)
            layer_norm(3)
            pe.wait_ge(S("x_ready"), 32)
            for t, (t0, n) in enumerate(((N_META, P), (N_META + P, P), (TP, TS))):
                for hf in range(2):
                    for c in range(4):
                        m = pe.transpose(ps[0:n, 2 * t + hf, P * c:P * c + P], xT[:, 4 * hf + c, t0:t0 + n], ident)
                    m.then_inc(S("yo_mm"), 1)

        @block.scalar
        def _(act):
            prime(act, "act")
            def f(out, in_, func, **k):
                return act.activation(out, in_, func, **k)

            def copy(out, in_):
                return act.copy(out, in_)

            for i, X in enumerate((rT, kT_, vT_)):
                for c in range(NC):
                    n = 8 * i + c
                    act.wait_ge(S("rkv_mm"), after("rkv_mm", n + 1))
                    copy(X[:, c, :], bank(n % 4, T)).then_inc(S("rkv_ev"), 1)
            act.wait_ge(S("lora_mm"), after("lora_mm", 1))
            f(hw, ps[0:64, 4, 0:T], ACT.Tanh).then_inc(S("lora_ev"), 1)
            act.wait_ge(S("lora_mm"), after("lora_mm", 2))
            copy(ha, ps[0:64, 5, 0:T]).then_inc(S("lora_ev"), 1)
            act.wait_ge(S("lora_mm"), after("lora_mm", 3))
            f(hg, ps[:, 6, 0:T], ACT.Sigmoid).then_inc(S("lora_ev"), 1)
            act.wait_ge(S("mix_ready"), after("mix_ready", 48))
            for i, (X, w0) in enumerate(((sgT, dw0), (T3, aw0))):
                for c in range(NC):
                    act.wait_ge(S("lz_mm"), after("lz_mm", 8 * i + c + 1))
                    f(X[:, c, :], bank(4 + c % 4, T), ACT.Sigmoid, bias=w0[:, c:c + 1]).then_inc(S("lz_ev"), 1)
            for c in range(NC):
                act.wait_ge(S("kk_ready"), after("kk_ready", c + 1))
                f(T2[:, c, :], T1[:, c, :], ACT.Square).then_inc(S("kksq_ready"), 1)
            for c in range(NC):
                act.wait_ge(S("kks_mm"), after("kks_mm", c + 1))
                f(T2[:, c, :], bank(c % 4, T), ACT.Sqrt).then_inc(S("kks_ev"), 1)
            for n in range(8):
                bp, hf = n // 2, n % 2
                act.wait_ge(S("nat_in_mm"), after("nat_in_mm", n + 1))
                copy(STS[:, 4 * hf:4 * hf + 4, 2 * bp:2 * bp + 2, :].rearrange("p c b n -> p c (b n)"),
                     bank(4 + n % 4).rearrange("p (c n) -> p c n", c=4)).then_inc(S("nat_ev"), 1)
            act.wait_ge(S("prep_ready"), 1)

            def factors(n, par, t0, w, part):
                cols, ex = bass.ds(t0, w), EX[par]
                if part == 0:
                    act.wait_ge(S("st_ready"), n)
                    f(ex[0][:, :, 0:w], T3[:, :, cols], ACT.Exp, scale=-KAPPA).then_inc(S("ex_ready"), 1)
                    f(ex[1][:, :, 0:w], T3[:, :, cols], ACT.Exp, scale=KAPPA).then_inc(S("ex_ready"), 1)
                else:
                    act.wait_ge(S("lx_ready"), n + 1)
                    f(ex[2][:, :, 0:w], ex[2][:, :, 0:w], ACT.Exp, scale=-KAPPA).then_inc(S("ex_ready"), 1)

            def chunk(n, par, t0, w, sample, nxt):
                cols = bass.ds(t0, w)
                for hf in range(2):
                    act.wait_ge(S("bkt_mm"), 2 * n + hf + 1)
                    copy(BKt[:, 4 * hf:4 * hf + 4, :].rearrange("p c n -> p (c n)"), bank(hf)).then_inc(S("bkt_ready"), 1)
                for hp in range(2):
                    q = slice(64 * hp, 64 * hp + 64)
                    act.wait_ge(S("l_mm"), 2 * n + hp + 1)
                    copy(LM[q, :, q], ps[q, 0:2, :].rearrange("p b (c n) -> p (b c) n", c=4)[:, :, q]).then_inc(S("lm_ready"), 1)
                levels = 2 if sample else LEVELS - 1
                for lv in range(1, levels + 1):
                    for hf in range(2):
                        act.wait_ge(S("y_mm"), 10 * n + 2 * (lv - 1) + hf + 1)
                        copy(YI[:, 4 * hf:4 * hf + 4, :].rearrange("p c n -> p (c n)"), bank(4 + hf)).then_inc(S("y_ready"), 1)
                    if lv == 1:
                        for hf in range(2):
                            act.wait_ge(S("mv_mm"), 2 * n + hf + 1)
                            act.wait_ge(S("u_ready"), after("u_ready", 2 * n))
                            copy(MV[:, 4 * hf:4 * hf + 4, :].rearrange("p c n -> p (c n)"), bank(2 + hf, 256)
                                 ).then_inc(S("mv_ready"), 1)
                    if nxt and lv <= 2:
                        factors(n + 1, 1 - par, *nxt, lv - 1)
                if sample:
                    for hp in range(2):
                        for hf in range(2):
                            q = slice(64 * hp, 64 * hp + 64)
                            act.wait_ge(S("qs_mm"), 2 * hp + hf + 1)
                            copy(QS[q, 4 * hf:4 * hf + 4, :, :].rearrange("p c w t -> p (c w t)"), ps[q, 2 * hp + hf, :]
                                 ).then_inc(S("qs_ready"), 1)
                for hp in range(2):
                    act.wait_ge(S("sa_mm"), after("sa_mm", 2 * n + hp + 1))
                    copy(SAV.rearrange("p (c e) n -> p e c n", e=2)[0:64, hp], ps[0:64, 4 + hp, :].rearrange("p (c n) -> p c n", c=NC)
                         ).then_inc(S("sa_ready"), 1)
                if not sample:
                    act.wait_ge(S("o_mm"), after("o_mm", 1 * n + 1))
                    apart(act)
                    copy(T3[:, :, cols], bank(6).rearrange("p (c t) -> p c t", c=NC)[:, :, 0:w]).then_inc(S("o_ready"), 1)

            act.wait_ge(S("st_ready"), 1)
            for part in range(2):
                factors(0, 0, 0, C, part)
            with act.Fori(0, NFULL // 2) as i:
                for side in range(2):
                    t0 = (2 * i + side) * C
                    chunk(2 * i + side, side, t0, C, False, (t0 + C, C))
            chunk(NFULL, 0, NFULL * C, TP - NFULL * C, False, (TP, TS))
            chunk(NFULL + 1, 1, TP, TS, True, None)
            for hf in range(2):
                act.wait_ge(S("wkvp_mm"), after("wkvp_mm", hf + 1))
                copy(QW[:, 4 * hf:4 * hf + 4, :].rearrange("p c n -> p (c n)"), bank(4 + hf)).then_inc(S("wkvp_ready"), 1)
            for n in range(8):
                bp, hf = n // 2, n % 2
                act.wait_ge(S("wkvs_mm"), after("wkvs_mm", n + 1))
                if n == 0:
                    act.wait_ge(S("o_ready"), after("o_ready", NFULL + 2))
                if bp >= 2 and hf == 0:
                    act.wait_ge(S(f"out_wkvs{bp % 2}"), 32)
                copy(NAT[bp % 2][:, 512 * hf:512 * hf + 512], bank(n % 4)).then_inc(S("wkvs_ready"), 1)
            for c in range(NC):
                act.wait_ge(S("gn_c"), after("gn_c", c + 1))
                f(T1[:, c, :], sgT[:, c, :], ACT.Square).then_inc(S("gn_sq"), 1)
            for c in range(NC):
                act.wait_ge(S("gn_vm"), after("gn_vm", c + 1))
                f(T1[:, c, :], bank(4 + c % 4, T), ACT.Sqrt, scale=1.0 / N, bias=eps_lnx).then_inc(S("gn_s"), 1)

            def layer_norm(i, l, j):
                for c in range(NC):
                    act.wait_ge(S("ln_c"), 8 * i + c + 1)
                    f(SQ[:, c, :], CT[:, c, :], ACT.Square).then_inc(S("ln_sq"), 1)
                act.wait_ge(S("ln_var"), i + 1)
                f(RS, bank(7, T), ACT.Sqrt, bias=eps_ln).then_inc(S("ln_rs"), 1)
                for c in range(NC):
                    act.wait_ge(S("ln_n"), 8 * i + c + 1)
                    f(xT[:, c, :], CT[:, c, :], ACT.Identity, scale=plv[l][j][0][:, c:c + 1],
                      bias=plv[l][j][1][:, c:c + 1]).then_inc(S("x_ready"), 1)

            def more_block(n):
                act.wait_ge(*over("o_gather", n, 1))
                f(oXg, ps[:, 0:2, :].rearrange("p b (c n) -> p (b c) n", c=4), ACT.Copy).then_inc(S("o_act"), 1)
                act.wait_ge(*over("o_gate_up", n, 1))
                f(HS, bank(2), ACT.Silu).then_inc(S("o_act"), 1)
                act.wait_ge(*over("o_turn", n, 1))
                f(oHT[:, 0:F_], bank(2), ACT.Copy)
                f(oSG, bank(3, T), ACT.Copy)
                f(gsl[0], ps[:, 3, 400:401], ACT.Copy).then_inc(S("o_act"), 1)
                act.wait_ge(*over("o_down", n, 1))
                act.wait_ge(*over("o_ht", n, 1))
                f(oYY, ps[:, 4:6, :].rearrange("p b n -> p (b n)"), ACT.Identity, scale=gsl[0]).then_inc(S("o_act"), 1)

            def w_hi(l, n0, j, e, q):
                G = E_ * l + 2 * j + e
                n = n0 + 3 * e + q // 4
                if q % 4 == 0:
                    act.wait_ge(S(f"w_full{n % NSLOT}"), landed(n) + 16 * j)
                wait(act, S("w_used"), NQ * G + q + 1 - NB)
                f(WS[q % NB][0][:, :], slot(n)[:, QUARTER * (q % 4):QUARTER * (q % 4 + 1)], ACT.Copy).then_inc(S("w_hi"), 1)

            def xg_hi(G, half):
                act.wait_ge(S("gb_mm" if half else "ga_mm"), G + 1)
                f(Xg[0][:, 4 * half:4 * half + 4, :].rearrange("p c n -> p (c n)"), bank(half), ACT.Copy).then_inc(S("xg_hi"), 1)

            def expert(l, n0, j, e, first, last):
                G = E_ * l + 2 * j + e
                more = not (last and e == 1)
                for q in range(NB, 8):
                    w_hi(l, n0, j, e, q)
                act.wait_ge(S("w_used"), NQ * G + 4)
                f(HS, bank(2), ACT.Silu).then_inc(S("hs_ready"), 1)
                for q in range(8, NQ):
                    w_hi(l, n0, j, e, q)
                if more:
                    xg_hi(G + 1, 0)
                act.wait_ge(S("turn_mm"), G + 1)
                f(HT[0][:, :], bank(2), ACT.Copy).then_inc(S("ht_hi"), 1)
                if more:
                    xg_hi(G + 1, 1)
                act.wait_ge(S("sgt_mm"), G + 1)
                f(SG[e][:, :], bank(3, T), ACT.Copy)
                f(gsl[e], ps[:, 3, 400:401], ACT.Copy).then_inc(S("sg_ready"), 1)
                if more:
                    for q in range(NB):
                        w_hi(l, n0, j + e, 1 - e, q)
                act.wait_ge(S("w_used"), NQ * G + NQ)
                act.wait_ge(S("sg_ready"), G + 1)
                for hf in range(2):
                    f(YY[e][0][:, 512 * hf:512 * hf + 512], bank(4 + hf), ACT.Identity, scale=gsl[e]).then_inc(S("y_hi"), 1)

            def experts(l, n0):
                for t, (t0, n) in enumerate(TOK):
                    act.wait_ge(S("xtm_mm"), 6 * l + 2 * t + 1)
                    copy(XTM[0:n, t, 0:512], ps[0:n, 2 * t, :]).then_inc(S("xtm_a"), 1)
                act.wait_ge(S("rt_mm"), l + 1)
                act.wait_ge(S("rt_zero"), l + 1)
                f(rt[0][:, 0:32], ps[:, 6, 0:32], ACT.Sigmoid)
                f(rt[0][0:TOK[2][1], 32:48], ps[0:TOK[2][1], 6, 32:48], ACT.Sigmoid).then_inc(S("s_ready"), 1)
                act.wait_ge(S("route_ready"), l + 1)
                overflow(act, l, "act", lambda i, b, n: more_block(n))
                for q in range(NB):
                    w_hi(l, n0, 0, 0, q)
                xg_hi(E_ * l, 0)
                xg_hi(E_ * l, 1)
                for e in range(2):
                    expert(l, n0, 0, e, True, False)
                with act.Fori(1, PAIRS - 1) as j:
                    for e in range(2):
                        expert(l, n0, j, e, False, False)
                for e in range(2):
                    expert(l, n0, PAIRS - 1, e, False, True)

            layer_norm(0, 0, 0)
            experts(0, L_MOE0)
            layer_norm(1, 0, 1)
            for i, X in enumerate((aKT, aVT, aQT)):
                for c in range(NC):
                    act.wait_ge(S("proj_mm"), 8 + 8 * i + c + 1)
                    copy(X[:, c, :], bank(c % 4, T)).then_inc(S("kvq_ev"), 1)
            act.wait_ge(S("lam_s"), 1)
            f(lams[:, 2:4], lams[:, 0:2], ACT.Exp).then_inc(S("lam_e"), 1)
            units = [(t, h) for t in range(3) for h in range(NH)]

            def weights_out(u):
                t, h = units[u]
                nq = KTILE[t][1]
                act.wait_ge(S("p_tr"), u + 1)
                if u >= 2:
                    act.wait_ge(S("p_av"), u - 1)
                for lo, hi in ((0, min(t + 1, 2)), (2, t + 1)):
                    if lo < hi:
                        k = KTILE[lo][1]
                        i = copy(AT[u % 2][0:k, lo:hi, 0:nq],
                                 ps[0:k, 4 + u % 2, P * lo:P * hi].rearrange("p (k n) -> p k n", n=P)[:, :, 0:nq])
                i.then_inc(S("p_at"), 1)

            NU = len(units)
            for u in range(NU + 1):
                if u < NU:
                    t, h = units[u]
                    nq = KTILE[t][1]
                    nk = KTILE[t][0] + nq
                    act.wait_ge(S("p_nb"), u + 1)
                    if u >= 2:
                        act.wait_ge(S("p_tr"), u - 1)
                    for j in range(2):
                        f(PP[u % 2][0:nq, j, 0:nk], ps[0:nq, 2 * (u % 2) + j, 0:nk], ACT.Exp, scale=0.125,
                          bias=st4[u % 2][0:nq, j:j + 1], accum_out=st4[u % 2][0:nq, 2 + j:3 + j]).then_inc(S("p_exp"), 1)
                if u >= 1:
                    weights_out(u - 1)
            for b in range(SB):
                for hf in range(2):
                    act.wait_ge(S("kt_mm"), 4 * b + hf + 1)
                    copy(KTs[b % 2][:, 4 * hf:4 * hf + 4, 0:P], bank(hf).rearrange("p (c n) -> p c n", c=4)).then_inc(S("kts_a"), 1)
                act.wait_ge(S("s_nb"), b + 1)
                if b >= 2:
                    act.wait_ge(S("s_tr"), b - 1)
                st = st4[b % 2]
                f(PS[b % 2], ps[:, SCB[b % 2], 0:320], ACT.Exp, scale=0.125, bias=st[:, 0:1],
                  accum_out=st[:, 2:3]).then_inc(S("s_exp"), 1)
            act.wait_ge(S("s_oev"), SB)
            for c in range(NC):
                f(aSQ[:, c, :], aOT[:, c, :], ACT.Square).then_inc(S("sl_sq"), 1)
            for c in range(NC):
                act.wait_ge(S("sl_mm"), after("sl_mm", c + 1))
                f(aSQ[:, c, :], bank(c % 4, T), ACT.Sqrt, scale=1.0 / P, bias=eps_ln).then_inc(S("sl_s"), 1)
            layer_norm(2, 1, 0)
            experts(1, L_MOE1)
            layer_norm(3, 1, 1)
            for t in range(3):
                n = P if t < 2 else TS
                act.wait_ge(S("yo_mm"), 2 * t + 1)
                copy(OUTT[0:n, t, 0:512], ps[0:n, 2 * t, :]).then_inc(S("y_rows"), 1)

        @block.vector
        def _(dve):
            prime(dve, "dve")
            tt, tsc, stt, cp = dve.tensor_tensor, dve.tensor_scalar, dve.scalar_tensor_tensor, dve.tensor_copy
            dve.wait_ge(S("par_mm"), 1)
            cp(par[:, 0:104], ps[:, 0, 0:104])
            cp(par[:, 104:169], ps[:, 0, 128:193])
            cp(ssT, ps[:, 0, 256:320])
            dve.drain()
            tsc(oneka, ka, -1.0, 1.0, ALU.mult, ALU.add)
            for t, (t0, n) in enumerate(TOK):
                for hf in range(2):
                    dve.wait_ge(S("xt_mm"), 2 * t + hf + 1)
                    cp(xT[:, 4 * hf:4 * hf + 4, t0:t0 + n], ps[:, 1 + 2 * t + hf, 0:4 * n].rearrange("p (c n) -> p c n", c=4))
            dve.drain()
            tt(sgT[:, :, 1:T], xT[:, :, 0:T - 1], xT[:, :, 1:T], ALU.subtract)
            dve.drain()
            tsc(sgT[:, :, 0:1], xT[:, :, 0:1], -1.0, None, ALU.mult)
            tt(sgT[:, :, TP:T:SS], ssT.rearrange("p (b c) -> p c b", c=NC), xT[:, :, TP:T:SS], ALU.subtract)
            dve.drain()
            for i, (m, X) in enumerate(((0, T1), (2, T2), (3, T3), (1, T1), (4, T2), (5, T3))):
                if i >= 3:
                    dve.wait_ge(S("rkv_mm"), after("rkv_mm", 8 * (i - 2)))
                for c in range(NC):
                    stt(X[:, c, :], sgT[:, c, :], mixv[m][:, c:c + 1], xT[:, c, :], ALU.mult, ALU.add
                        ).then_inc(S("mix_ready"), 1)
            dve.wait_ge(S("lora_mm"), after("lora_mm", 1))
            dve.wait_ge(S("rkv_ev"), after("rkv_ev", 16))
            for c in range(NC):
                tsc(T1[:, c, :], kT_[:, c, :], kk0[:, c:c + 1], None, ALU.mult).then_inc(S("kk_ready"), 1)
            dve.wait_ge(S("kks_ev"), after("kks_ev", 8))
            tsc(T2, T2, 1e-12, None, ALU.max)
            dve.drain()
            dve.reciprocal(T2, T2)
            dve.drain()
            stt(T1, T1, -1.0, T2, ALU.mult, ALU.mult)
            dve.wait_ge(S("lz_ev"), after("lz_ev", 16))
            dve.drain()
            stt(T2, T1, -1.0, T3, ALU.mult, ALU.mult)
            dve.drain()
            for c in range(NC):
                tsc(T3[:, c, :], T3[:, c, :], ka[:, c:c + 1], oneka[:, c:c + 1], ALU.mult, ALU.add)
            dve.drain()
            tt(kT_, kT_, T3, ALU.mult)
            dve.drain()
            dve.wait_ge(S("in_rconst"), 16)
            for c in range(NC):
                dve.tensor_tensor_scan(T3[:, c, :], rc("scan"), sgT[:, c, :], 0.0, ALU.mult, ALU.add)
            dve.memset(STZ, 0.0)
            dve.memset(LM, 0.0)
            dve.drain().then_inc(S("prep_ready"), 1)
            dve.wait_ge(S("nat_ev"), after("nat_ev", 8))
            dve.nop().then_inc(S("st_ready"), 1)
            dve.wait_ge(S("prep_ready"), 1)

            def operands(n, par, t0, w, part):
                cols, rav, bk, ex = bass.ds(t0, w), RAV[par], BK[par], EX[par]
                if part == 0:
                    tt(ex[2][:, :, 0:w], T3[:, :, cols], sgT[:, :, cols], ALU.subtract).then_inc(S("lx_ready"), 1)
                if part == 1:
                    if not isinstance(n, int) or n > 0:
                        dve.wait_ge(S("o_mm"), after("o_mm", 1 * n - 1))
                    dve.wait_ge(S("ex_ready"), 3 * n + 3)
                    tt(rav[:, :, 0:w], rT[:, :, cols], ex[0][:, :, 0:w], ALU.mult)
                    tt(rav[:, :, 64:64 + w], T1[:, :, cols], ex[2][:, :, 0:w], ALU.mult)
                if part == 2:
                    cp(rav[:, :, 128:128 + w], vT_[:, :, cols])
                    tt(bk[:, :, 0:w], T2[:, :, cols], ex[1][:, :, 0:w], ALU.mult)
                if part == 3:
                    tt(bk[:, :, 64:64 + w], kT_[:, :, cols], ex[1][:, :, 0:w], ALU.mult).then_inc(S("ops_ready"), 1)

            def chunk(n, par, t0, w, sample, nxt):
                cols = bass.ds(t0, w)
                dve.wait_ge(S("sa_mm"), after("sa_mm", 2 * n))
                cp(XI, ident.unsqueeze(1).to_broadcast([P, NC, P]))
                cp(XU, ident.unsqueeze(1).to_broadcast([P, NC, P]))
                for hf in range(2):
                    dve.wait_ge(S("avt_mm"), 2 * n + hf + 1)
                    cp(SAV[64:128, 8 * hf:8 * hf + 8, :].rearrange("p h n -> p (h n)"), ps[64:128, 2 + hf, :]
                       ).then_inc(S("sv_ready"), 1)
                mask = rc("masks" if sample else "maskp").unsqueeze(1).to_broadcast([P, 4, P])
                gv = GH.rearrange("p (c e) n -> p e c n", e=2)
                for hp in range(2):
                    for hf in range(2):
                        dve.wait_ge(S("gh_mm"), 4 * n + 2 * hp + hf + 1)
                        tt(gv[:, hp, 4 * hf:4 * hf + 4, :], bank(4 + 2 * hp + hf).rearrange("p (c n) -> p c n", c=4),
                           mask, ALU.mult).then_inc(S("gh_ready"), 1)

                def level(name, m):
                    return rc(name)[:, P * m:P * m + P].bitcast(U32).unsqueeze(1).to_broadcast([P, 4, P])

                def c4(b):
                    return bank(b).rearrange("p (c n) -> p c n", c=4)

                dve.drain()
                dve.wait_ge(S("lm_ready"), 2 * n + 2)
                apart(dve)
                for hf in range(2):
                    dve.copy_predicated(XI[:, 4 * hf:4 * hf + 4, :], level("low", 0), LM[:, 4 * hf:4 * hf + 4, :])
                for hf in range(2):
                    dve.wait_ge(S("lt_mm"), 2 * n + hf + 1)
                    apart(dve)
                    i = dve.copy_predicated(XU[:, 4 * hf:4 * hf + 4, :], level("up", 0), c4(2 + hf))
                i.then_inc(S("inv_ready"), 1)
                levels = 2 if sample else LEVELS - 1
                for lv in range(1, levels + 1):
                    for hf in range(2):
                        h4 = slice(4 * hf, 4 * hf + 4)
                        bx = (6, 7) if hf == 0 else (0, 1)
                        dve.wait_ge(S("xu_mm"), 10 * n + 2 * (lv - 1) + hf + 1)
                        apart(dve)
                        if lv < levels:
                            dve.copy_predicated(XI[:, h4, :], level("low", lv), c4(bx[0]))
                        dve.copy_predicated(XU[:, h4, :], level("up", lv), c4(bx[1])).then_inc(S("inv_ready"), 1)
                    if nxt and lv != 2:
                        operands(n + 1, 1 - par, *nxt, max(lv - 2, 0))
                for hf in range(2):
                    h4 = slice(4 * hf, 4 * hf + 4)
                    dve.wait_ge(S("u_mm"), 2 * n + hf + 1)
                    dve.wait_ge(S("mv_ready"), 2 * n + hf + 1)
                    tt(U[:, h4, :].rearrange("p c n -> p (c n)"), bank(2 + hf, 256),
                       MV[:, h4, :].rearrange("p c n -> p (c n)"), ALU.add).then_inc(S("u_ready"), 1)
                if sample:
                    dve.wait_ge(S("o_mm"), after("o_mm", 1 * n + 1))
                    tt(T3[:, :, cols], bank(6).rearrange("p (c t) -> p c t", c=NC), QS[:, :, 0, :], ALU.add
                       ).then_inc(S("o_ready"), 1)
                else:
                    dve.wait_ge(S("st_mm"), 1 * n + 1)
                    for hp in range(2):
                        q = slice(64 * hp, 64 * hp + 64)
                        tt(STZ[q, :, q], bank(7).rearrange("p (c n) -> p c n", c=NC)[q], STZ[q, :, q], ALU.add)
                    dve.drain()
                    for hp in range(2):
                        q = slice(64 * hp, 64 * hp + 64)
                        i = tt(STZ[q, :, q], STZ[q, :, q], EX[par][0][q, :, w - 1:w].to_broadcast([64, NC, 64]), ALU.mult)
                    i.then_inc(S("st_ready"), 1)

            for part in range(4):
                operands(0, 0, 0, C, part)
            with dve.Fori(0, NFULL // 2) as i:
                for side in range(2):
                    t0 = (2 * i + side) * C
                    chunk(2 * i + side, side, t0, C, False, (t0 + C, C))
            for v in (RAV[0], BK[0]):
                dve.memset(v.rearrange("p c (w t) -> p (c w) t", t=C)[:, :, TP % C:C], 0.0)
            dve.drain().then_inc(S("tail_ready"), 1)
            chunk(NFULL, 0, NFULL * C, TP - NFULL * C, False, (TP, TS))
            chunk(NFULL + 1, 1, TP, TS, True, None)

            def state_update(dve, c):
                dve.wait_ge(S("ss_mm"), after("ss_mm", 2 * c + 2))
                v = STS[:, c, :, :]
                tt(v, bank(6 + c % 2).rearrange("p (b n) -> p b n", b=SB), v, ALU.add)
                dve.drain()
                tt(v, v, EX[1][0][:, c, SS - 1:TS:SS].unsqueeze(2).to_broadcast([P, SB, N]), ALU.mult
                   ).then_inc(S("sts_ready"), 1)

            for h in range(H):
                c, hp = h // 2, h % 2
                if h >= 2:
                    dve.wait_ge(S("ss_mm"), after("ss_mm", h - 1))
                if h == 0:
                    dve.wait_ge(S("sa_ready"), after("sa_ready", 2 * (NFULL + 2)))
                tt(SAVB[h % 2], SAV[:, h, :].unsqueeze(1).to_broadcast([P, SB, N]),
                   rc("bm").unsqueeze(2).to_broadcast([P, SB, N]), ALU.mult).then_inc(S("savb_ready"), 1)
                if hp and c >= 1:
                    state_update(dve, c - 1)
            state_update(dve, NC - 1)

            for c in range(NC):
                dve.wait_ge(S("gn_mm"), after("gn_mm", c + 1))
                stt(sgT[:, c, :], bank(c % 4, T), -1.0 / N, T3[:, c, :], ALU.mult, ALU.add).then_inc(S("gn_c"), 1)
            tt(rT, rT, kT_, ALU.mult)
            dve.drain()
            for c in range(NC):
                tsc(rT[:, c, :], rT[:, c, :], rkv_[:, c:c + 1], None, ALU.mult).then_inc(S("rkr_ready"), 1)
            dve.wait_ge(S("gn_s"), after("gn_s", 8))
            dve.reciprocal(T1, T1)
            dve.drain()
            tt(sgT, sgT, T1, ALU.mult)
            dve.drain()
            for c in range(NC):
                tsc(sgT[:, c, :], sgT[:, c, :], lnx0[:, c:c + 1], lnx1[:, c:c + 1], ALU.mult, ALU.add)
            for c in range(NC):
                dve.wait_ge(S("bn_mm"), after("bn_mm", c + 1))
                tt(T2[:, c, :], bank(c % 4, T), vT_[:, c, :], ALU.mult).then_inc(S("bn_ev"), 1)
            dve.drain()
            tt(sgT, sgT, T2, ALU.add)
            dve.drain()
            for c in range(NC):
                dve.wait_ge(S("g_mm"), after("g_mm", c + 1))
                tt(T3[:, c, :], sgT[:, c, :], bank(4 + c % 4, T), ALU.mult).then_inc(S("z_ready"), 1)

            def residual(base_mm):
                for c in range(NC):
                    dve.wait_ge(S("proj_mm"), base_mm + c + 1)
                    stt(YA[:, c, :], xT[:, c, :], ALPHA, bank(c % 4, T), ALU.mult, ALU.add).then_inc(S("ln_in"), 1)

            def layer_norm(i):
                dve.wait_ge(S("ln_mean"), i + 1)
                for c in range(NC):
                    tt(CT[:, c, :], YA[:, c, :], bank(6, T), ALU.subtract).then_inc(S("ln_c"), 1)
                dve.wait_ge(S("ln_rs"), i + 1)
                dve.reciprocal(RS, RS)
                dve.drain()
                for c in range(NC):
                    tt(CT[:, c, :], CT[:, c, :], RS, ALU.mult).then_inc(S("ln_n"), 1)

            def select(par):
                dve.drain()
                return tt(SelM[par], mc("iota").unsqueeze(1).to_broadcast([P, 3, CAP]),
                          rkp[par].unsqueeze(2).to_broadcast([P, 3, CAP]), ALU.is_equal)

            def pick(par, i):
                cp(rkp[par].unsqueeze(2), rank3[:, :, bass.ds(i, 1)])
                cp(gtp[par].unsqueeze(2), gate3[:, :, bass.ds(i, 1)])

            def more_block(i, b, n):
                tsc(rkp[0], rkp[0], -float(CAP), None, ALU.add)
                select(0).then_inc(S("o_dve"), 1)
                dve.wait_ge(*over("o_silu", n, 1))
                tt(HS, HS, bank(3), ALU.mult).then_inc(S("o_dve"), 1)
                for c in range(NC):
                    dve.wait_ge(*over("o_scatter", n, c + 1))
                    tt(YA[:, c, :], YA[:, c, :], bank(6 + c % 2, T), ALU.add).then_inc(S("o_dve"), 1)

            def w_lo(l, n0, j, e, q):
                G = E_ * l + 2 * j + e
                dve.wait_ge(S("w_hi"), NQ * G + q + 1)
                tt(WS[q % NB][1][:, :], slot(n0 + 3 * e + q // 4)[:, QUARTER * (q % 4):QUARTER * (q % 4 + 1)],
                   WS[q % NB][0][:, :].bitcast(F32), ALU.subtract).then_inc(S("w_lo"), 1)

            def xg_lo(G, half):
                dve.wait_ge(S("xg_hi"), 2 * G + half + 1)
                h, lo = [x[:, 4 * half:4 * half + 4, :].rearrange("p c n -> p (c n)") for x in Xg]
                tt(lo, bank(half), h.bitcast(F32), ALU.subtract).then_inc(S("xg_lo"), 1)

            def adds(s_):
                for c in range(NC):
                    dve.wait_ge(S("sc_mm"), 8 * s_ + c + 1)
                    tt(YA[:, c, :], YA[:, c, :], bank(6 + c % 2, T), ALU.add).then_inc(S("add_done"), 1)

            def expert(l, n0, j, e, first, last):
                G = E_ * l + 2 * j + e
                more = not (last and e == 1)
                for q in range(NB, NQ - 1):
                    w_lo(l, n0, j, e, q)
                dve.wait_ge(S("hs_ready"), G + 1)
                dve.wait_ge(S("w_used"), NQ * G + 8)
                tt(HS, HS, bank(3), ALU.mult).then_inc(S("h_ready"), 1)
                w_lo(l, n0, j, e, NQ - 1)
                if more:
                    xg_lo(G + 1, 0)
                dve.wait_ge(S("ht_hi"), G + 1)
                tt(HT[1][:, :], bank(2), HT[0][:, :].bitcast(F32), ALU.subtract).then_inc(S("ht_lo"), 1)
                if more:
                    xg_lo(G + 1, 1)
                if e == 0 and not first:
                    adds(PAIRS * l + j - 1)
                if not last:
                    dve.wait_ge(S("sgt_mm"), G + 1)
                    pick(e, 2 * j + e + 2)
                    select(e).then_inc(S("sel_ready"), 1)
                if more:
                    for q in range(NB):
                        w_lo(l, n0, j + e, 1 - e, q)
                for hf in range(2):
                    dve.wait_ge(S("y_hi"), 2 * G + hf + 1)
                    v = slice(512 * hf, 512 * hf + 512)
                    stt(YY[e][1][:, v], bank(4 + hf), gsl[e], YY[e][0][:, v].bitcast(F32), ALU.mult, ALU.subtract
                        ).then_inc(S("y_lo"), 1)

            def experts(l, n0):
                dve.memset(rt[0], 0.0).then_inc(S("rt_zero"), 1)
                dve.wait_ge(S("x_ready"), 16 * l + 8)
                dve.memset(YA, 0.0)
                for t, (t0, n) in enumerate(TOK):
                    dve.wait_ge(S("xtm_mm"), 6 * l + 2 * t + 2)
                    cp(XTM[0:n, t, 512:1024], ps[0:n, 2 * t + 1, :]).then_inc(S("xtm_d"), 1)
                dve.wait_ge(S("in_mconst"), 48 * (l + 1))
                dve.wait_ge(S("s_ready"), l + 1)

                def v3(x):
                    return x.rearrange("p (t n) -> p t n", t=3)

                def g12(x):
                    return x.rearrange("p (g n) -> p g n", n=4)

                score, sel, a1, a2, oh, msk0, msk, _ = rt
                gm, ga, gb, gc = gs
                m12 = ga[:, 0:12]
                tt(v3(sel), v3(score), rbB.unsqueeze(1).to_broadcast([P, 3, E_]), ALU.add)
                dve.drain()
                for d, o, k in ((1, 0, 3), (2, 3, 2), (3, 5, 1)):
                    tt(pr6[:, :, o:o + k], g12(sel)[:, :, 0:k], g12(sel)[:, :, d:d + k], ALU.add)
                dve.drain()
                dve.tensor_reduce(gm, pr6, AX, ALU.max)
                dve.drain()
                top1 = cntf[:, 0:3]

                def first_best(dst, val, tmp, width, weight):
                    dve.tensor_reduce(top1, v3(val), AX, ALU.max)
                    dve.drain()
                    tt(v3(tmp), v3(val), top1.unsqueeze(2).to_broadcast([P, 3, width]), ALU.is_equal)
                    dve.drain()
                    tt(v3(tmp), v3(tmp), weight.unsqueeze(1).to_broadcast([P, 3, width]), ALU.mult)
                    dve.drain()
                    dve.tensor_reduce(top1, v3(tmp), AX, ALU.max)
                    dve.drain()
                    tt(v3(dst), top1.unsqueeze(2).to_broadcast([P, 3, width]),
                       weight.unsqueeze(1).to_broadcast([P, 3, width]), ALU.is_equal)
                    dve.drain()

                first_best(gb, gm, ga, G_, mc("w4"))
                gmask = gb.unsqueeze(2).to_broadcast([P, 12, 4])
                tsc(gc, gb, BIG, -BIG, ALU.mult, ALU.add)
                tt(g12(a1), g12(sel), gmask, ALU.mult)
                dve.drain()
                tt(g12(a1), g12(a1), gc.unsqueeze(2).to_broadcast([P, 12, 4]), ALU.add)
                dve.drain()
                first_best(msk0, a1, a2, E_, mc("w16"))
                stt(a1, msk0, -2 * BIG, a1, ALU.mult, ALU.add)
                dve.drain()
                first_best(oh, a1, a2, E_, mc("w16"))
                tt(msk, msk0, oh, ALU.add)
                dve.drain()
                tt(v3(msk), v3(msk), mc("valid").unsqueeze(2).to_broadcast([P, 3, E_]), ALU.mult).then_inc(S("msk_ready"), 1)
                dve.drain()
                tt(a1, score, msk, ALU.mult)
                dve.drain()
                dve.tensor_reduce(top1, v3(a1), AX, ALU.add)
                dve.drain()
                tsc(top1, top1, 1e-37, None, ALU.max)
                dve.drain()
                dve.reciprocal(top1, top1)
                dve.drain()
                tt(gate3, v3(a1), top1.unsqueeze(2).to_broadcast([P, 3, E_]), ALU.mult)
                tsc(a2, msk, -1e6, 1e6, ALU.mult, ALU.add)
                dve.wait_ge(S("rk_mm"), l + 1)
                dve.drain()
                tt(rank3.rearrange("p t n -> p (t n)"), a2, ps[:, 7, 0:48], ALU.add)
                dve.tensor_reduce(cntp[:, 0:1], ps[:, 7, 64:80], AX, ALU.max)
                cp(cnt_i[0:1, 0:E_], ps[0:1, 7, 64:80])
                dve.drain()
                cp(cnt_i[0:1, E_:E_ + 1], cntp[0:1, 0:1])
                dve.drain().then_inc(S("route_ready"), 1)
                dve.wait_ge(S("route_ready"), l + 1)
                overflow(dve, l, "dve", more_block, lambda i: pick(0, i))
                dve.drain()
                for e in range(2):
                    pick(e, e)
                    select(e).then_inc(S("sel_ready"), 1)
                for q in range(NB):
                    w_lo(l, n0, 0, 0, q)
                xg_lo(E_ * l, 0)
                xg_lo(E_ * l, 1)
                for e in range(2):
                    expert(l, n0, 0, e, True, False)
                with dve.Fori(1, PAIRS - 1) as j:
                    for e in range(2):
                        expert(l, n0, j, e, False, False)
                for e in range(2):
                    expert(l, n0, PAIRS - 1, e, False, True)
                adds(PAIRS * (l + 1) - 1)
                dve.drain()
                for c in range(NC):
                    stt(YA[:, c, :], xT[:, c, :], ALPHA, YA[:, c, :], ALU.mult, ALU.add).then_inc(S("ln_in"), 1)

            residual(0)
            layer_norm(0)
            experts(0, L_MOE0)
            layer_norm(1)
            dve.wait_ge(S("in_aconst"), 32)
            lt4 = lamt.rearrange("p (a b n) -> p a b n", a=2, b=2)
            tt(lamp.rearrange("p (a n) -> p a n", a=2), lt4[:, :, 0, :], lt4[:, :, 1, :], ALU.mult)
            dve.drain()
            dve.tensor_reduce(lams[:, 0:2], lamp.rearrange("p (a n) -> p a n", a=2), AX, ALU.add).then_inc(S("lam_s"), 1)
            for i, (X, name) in enumerate(((KTM, "k"), (VTM, "v"))):
                for t, (t0, n) in enumerate(KTILE):
                    for hf in range(2):
                        j = 2 * t + hf
                        dve.wait_ge(S(f"{name}tr_mm"), after(f"{name}tr_mm", j + 1))
                        cp(X[0:n, t, 512 * hf:512 * hf + 512], ps[0:n, 4 + j % 4, :]).then_inc(S(f"{name}tm_ready"), 1)
            dve.wait_ge(S("lam_e"), 1)
            tt(lams[:, 4:5], lams[:, 3:4], lams[:, 2:3], ALU.subtract)
            dve.drain()
            tsc(lams[:, 4:5], lams[:, 4:5], -LI, None, ALU.add)
            dve.drain()
            tsc(lams[:, 6:7], lams[:, 4:5], -1.0, None, ALU.add)
            dve.drain()
            tt(lams[:, 5:6], lams[:, 6:7], ac("odd"), ALU.mult)
            dve.drain()
            tsc(lams[:, 5:6], lams[:, 5:6], 1.0, None, ALU.add)
            dve.wait_ge(S("kvq_ev"), 24)
            for v in Qbd:
                dve.memset(v, 0.0)
            dve.drain()
            units = [(t, h) for t in range(3) for h in range(NH)]
            NU = len(units)
            for u in range(NU + 2):
                if u < NU:
                    t, h = units[u]
                    nq = KTILE[t][1]
                    nk = KTILE[t][0] + nq
                    st = st4[u % 2]
                    dve.wait_ge(S("p_sc"), u + 1)
                    b = 2 * (u % 2)
                    dve.tensor_reduce(st[0:nq, 0:2], ps[0:nq, b:b + 2, 0:nk], AX, ALU.max)
                    dve.drain()
                    tsc(st[0:nq, 0:2], st[0:nq, 0:2], -0.125, None, ALU.mult).then_inc(S("p_nb"), 1)
                if 1 <= u <= NU:
                    t, h = units[u - 1]
                    nq = KTILE[t][1]
                    nk = KTILE[t][0] + nq
                    st, p = st4[(u - 1) % 2], PP[(u - 1) % 2]
                    dve.wait_ge(S("p_exp"), 2 * u)
                    dve.reciprocal(st[0:nq, 4:6], st[0:nq, 2:4])
                    dve.drain()
                    tt(st[0:nq, 5:6], st[0:nq, 5:6], lams[0:nq, 4:5], ALU.mult)
                    tsc(p[0:nq, 0, 0:nk], p[0:nq, 0, 0:nk], st[0:nq, 4:5], None, ALU.mult)
                    dve.drain()
                    stt(p[0:nq, 0, 0:nk], p[0:nq, 1, 0:nk], st[0:nq, 5:6], p[0:nq, 0, 0:nk], ALU.mult, ALU.add
                        ).then_inc(S("p_am"), 1)
                if u >= 2:
                    t, h = units[u - 2]
                    q0, nq = KTILE[t]
                    dve.wait_ge(S("p_av"), u - 1)
                    cp(aOT[:, h, q0:q0 + nq], ps[:, 6 + u % 2, 0:nq]).then_inc(S("p_oev"), 1)
            def sample_queries(b):
                if b >= 2:
                    dve.wait_ge(S("s_sc"), b - 1)
                for hp in range(2):
                    q = slice(64 * hp, 64 * hp + 64)
                    qv = Qbd[b % 2][q, SS * hp:SS * hp + 1152].rearrange("p (c n) -> p c n", n=144)[:, :, 0:SS]
                    i = cp(qv, aQT[q, :, TP + SS * b:TP + SS * b + SS])
                i.then_inc(S("qbd_ready"), 1)

            def sample_keys(b):
                for hf in range(2):
                    dve.wait_ge(S("kt_mm"), 4 * b + 3 + hf)
                    cp(KTs[b % 2][:, 4 * hf:4 * hf + 4, P:2 * P], bank(2 + hf).rearrange("p (c n) -> p c n", c=4)
                       ).then_inc(S("kts_d"), 1)
                dve.wait_ge(S("s_sc"), b + 1)
                st = st4[b % 2]
                dve.tensor_reduce(st[:, 0:1], ps[:, SCB[b % 2], 0:320], AX, ALU.max)
                dve.drain()
                tsc(st[:, 0:1], st[:, 0:1], -0.125, None, ALU.mult).then_inc(S("s_nb"), 1)

            dve.wait_ge(S("kvq_ev"), 24)
            sample_queries(0)
            sample_keys(0)
            for b in range(SB):
                if b + 1 < SB:
                    sample_queries(b + 1)
                st = st4[b % 2]
                dve.wait_ge(S("s_exp"), b + 1)
                dve.reciprocal(st[:, 4:5], st[:, 2:3])
                dve.drain()
                tsc(PS[b % 2], PS[b % 2], st[:, 4:5], lams[:, 5:6], ALU.mult, ALU.mult).then_inc(S("s_am"), 1)
                if b + 1 < SB:
                    sample_keys(b + 1)
                dve.wait_ge(S("s_tr"), b + 1)
                for lo, hi, k in ((0, 2, P), (2, 3, TS)):
                    v = ps[0:k, 5, P * lo:P * hi].rearrange("p (k m q) -> p k m q", m=2, q=SS)
                    dve.tensor_reduce(ATs[b % 2][0:k, lo:hi, :].rearrange("p k (h q) -> p (k h) q", q=SS),
                                      v.rearrange("p k m q -> p k q m"), AX, ALU.add).then_inc(S("s_at"), 1)
                dve.wait_ge(S("past_mm"), b + 1)
                cp(aOT[:, :, TP + SS * b:TP + SS * b + SS], ps[:, 6, 0:64].rearrange("p (h q) -> p h q", q=SS)
                   ).then_inc(S("s_oev"), 1)
            dve.wait_ge(S("sl_s"), after("sl_s", 8))
            dve.reciprocal(aSQ, aSQ)
            dve.drain()
            tt(aOT, aOT, aSQ, ALU.mult)
            dve.drain()
            for c in range(NC):
                tsc(aOT[:, c, :], aOT[:, c, :], subv, 1.0 - LI, ALU.mult, ALU.mult).then_inc(S("z2_ready"), 1)
            residual(32)
            layer_norm(2)
            experts(1, L_MOE1)
            layer_norm(3)
            for t in range(3):
                n = P if t < 2 else TS
                dve.wait_ge(S("yo_mm"), 2 * t + 2)
                cp(OUTT[0:n, t, 512:1024], ps[0:n, 2 * t + 1, :]).then_inc(S("y_rows"), 1)


_INS = ["x_prompt", "x_sample", "cache_k", "cache_v", "page_table", "state_wkv", "state_shift", "meta_tokens",
        "rwkv_mix", "rwkv_w_rkv", "rwkv_decay_w0", "rwkv_decay_w1", "rwkv_decay_w2", "rwkv_a_w0", "rwkv_a_w1",
        "rwkv_a_w2", "rwkv_g_w1", "rwkv_g_w2", "rwkv_kk_ka", "rwkv_r_k", "rwkv_lnx", "rwkv_w_out", "w_kv_shared",
        "diff_w_q", "diff_lambda", "diff_subln", "diff_w_out", "router_w", "router_b", "moe_w_gate", "moe_w_up",
        "moe_w_down", "post_ln"]
_OUTS = [("y_prompt", (1, SEQ, D)), ("y_sample", (SB, SS, D)), ("new_k_prompt", (1, TP, 2 * NH, N)),
         ("new_v_prompt", (1, TP, NH, P)), ("new_wkv_prompt", (1, 1, H, N, N)), ("new_shift_prompt", (1, 1, D)),
         ("new_k_sample", (SB, SS, 2 * NH, N)), ("new_v_sample", (SB, SS, NH, P)),
         ("new_wkv_sample", (SB, 1, H, N, N)), ("new_shift_sample", (SB, 1, D))]


def kernel(**inputs):
    import numpy as _np
    import concourse.bacc as _bacc
    from concourse.bass_utils import run_bass_kernel_spmd as _run

    nc = _bacc.Bacc("TRN2", target_bir_lowering=False, num_devices=1)
    const, at = constants()
    arrays, I, O = {"in_const": const}, {}, {}
    for name in _INS:
        arrays["in_" + name] = _np.ascontiguousarray(inputs[name])
    for key, a in arrays.items():
        I[key[3:]] = nc.dram_tensor(key, a.shape, mybir.dt.from_np(a.dtype), kind="ExternalInput").ap()
    for name, shape in _OUTS:
        O[name] = nc.dram_tensor("out_" + name, shape, F32, kind="ExternalOutput").ap()
    build(nc, I, O, const, at)
    r = _run(nc, [arrays], core_ids=[0])
    return tuple(r.results[0]["out_" + name] for name, _ in _OUTS)
```

```python
from contextlib import ExitStack
import math

import numpy as np

import concourse.bass as bass
from concourse import mybir

ALU = mybir.AluOpType
ACT = mybir.ActivationFunctionType
AX = mybir.AxisListType.X
F32 = mybir.dt.float32
I32 = mybir.dt.int32
U32 = mybir.dt.uint32
FR = mybir.dt.float32r

P = 128
D = 1024
NC = D // P
N_META, SEQ = 16, 256
TP = N_META + SEQ
SB, SS = 8, 8
TS = SB * SS
T = TP + TS
H, N = 16, 64
C = 64
NFULL = TP // C
LEVELS = 6
NH = 8
PAGE, NPG = 128, 2
E_, G_, F_ = 16, 4, 512
NF = F_ // P
PAIRS = E_ // 2
CAP = 128
NBLK = -(-T // CAP)
NOV = E_ * (NBLK - 1)
QUARTER, NQ, NB = 1024, 12, 4
ALPHA = 4.0 ** 0.25
KAPPA = math.exp(-0.5)
LI = 0.8 - 0.6 * math.exp(-0.3)
BIG = 1e30
TOK = [(0, 128), (128, 128), (256, T - 256)]
KTILE = [(0, 128), (128, 128), (256, TP - 256), (TP, TS)]
ARENA = 53168
SLOT, NSLOT = 4096, 6
L_RKV, L_WO, L_MOE0, L_KV, L_Q, L_DO, L_MOE1 = 0, 6, 8, 56, 60, 62, 64


CHAINS = {
    "stage_mm": (("rkv_mm", 24), ("kks_mm", 8), ("lora_mm", 3), ("lz_mm", 16), ("nat_in_mm", 8), ("ss_mm", 16),
                 ("wkvp_mm", 2), ("wkvs_mm", 8), ("gn_mm", 8), ("gn_vm", 1), ("bn_mm", 8), ("gr_mm", 8), ("g_mm", 8)),
    "stage_act": (("rkv_ev", 24), ("kks_ev", 8), ("lora_ev", 3), ("lz_ev", 16), ("nat_ev", 8),
                  ("wkvp_ready", 2), ("wkvs_ready", 8), ("gn_sq", 8), ("gn_s", 1)),
    "stage_dve": (("mix_ready", 48), ("rkr_ready", 8), ("gn_c", 8), ("gr_ready", 1), ("bn_ev", 8), ("gr_ev", 8),
                  ("z_ready", 8)),
    "kv_mm": (("ktr_mm", 8), ("vtr_mm", 8), ("sl_mm", 1), ("sr_mm", 8)),
    "kv_dve": (("ktm_ready", 8), ("vtm_ready", 8), ("sr_ready", 1), ("z2_ready", 8)),
    "sub_act": (("sl_sq", 8), ("sl_s", 1)),
}
SHARED = {stage: (name, sum(k for _, k in chain[:i])) for name, chain in CHAINS.items()
          for i, (stage, _) in enumerate(chain)}


CHUNK_PRIMED = {"pe": ("o_mm", "sa_mm"), "act": ("o_ready", "sa_ready"), "dve": ("u_ready", "ops_ready")}
OVER = {
    "pe": (("o_gather", 1), ("o_gate_up", 1), ("o_turn", 1), ("o_down", 1), ("o_scatter", 8)),
    "act": (("o_xg", 1), ("o_silu", 1), ("o_ht", 1), ("o_y", 1)),
    "dve": (("o_sel", 1), ("o_h", 1), ("o_add", 8)),
    "sp": (("o_weights", 48),),
}
PRIMED = {name for names in CHUNK_PRIMED.values() for name in names}


def after(stage, n):
    return n + (SHARED[stage][1] if stage in SHARED else 1 if stage in PRIMED else 0)


def constants():
    p = np.arange(P)[:, None]
    q = np.arange(P)[None, :]
    c64 = np.arange(64)[None, :]
    s, t = p % 64, c64
    parts = {}
    parts["ident"] = (p == q)
    parts["onesd"] = np.full((P, P), 1.0 / D)
    parts["ones"] = np.ones((P, P))
    parts["bones"] = (p // 64 == q // 64)
    parts["eps"] = np.concatenate([np.full((P, 1), 1e-5), np.full((P, 1), 64e-5)], 1)
    parts["maskp"] = np.concatenate([s <= t, s < t], 1)
    same = s // SS == t // SS
    parts["masks"] = np.concatenate([(s <= t) & same, (s < t) & same], 1)
    scan = np.ones(T)
    scan[0:TP:C] = 0
    scan[TP::SS] = 0
    parts["scan"] = np.tile(scan, (P, 1))
    parts["bm"] = (s // SS == np.arange(SB)[None, :])
    for name, a, b in (("low", p, q), ("up", q, p)):
        parts[name] = np.concatenate([(a // (2 * m) == b // (2 * m)) & (a % (2 * m) >= m) & (b % (2 * m) < m)
                                      for m in (1, 2, 4, 8, 16, 32)], 1)
    parts["ustrict"] = (p < q)
    parts["iota"] = np.tile(np.arange(CAP), (P, 1))
    parts["w16"] = np.tile(np.arange(E_, 0, -1), (P, 1))
    parts["w4"] = np.tile(np.arange(G_, 0, -1), (P, 1))
    parts["valid"] = np.concatenate([p < n for _, n in TOK], 1)
    parts["caus"] = np.where(q > p, -BIG, 0.0)
    win = np.arange(2 * TS - SS)[None, :] - (TS - SS)
    parts["win"] = np.where((win >= 0) & (win <= p % SS), 0.0, -BIG)
    parts["odd"] = (p // SS) % 2
    j = np.arange(H)[None, :]
    parts["rows"] = np.concatenate([j == 2 * c + p // 64 for c in range(NC)], 1)
    parts["rows2"] = np.concatenate([np.broadcast_to(j // 2 == c, (P, H)) for c in range(NC)], 1)
    parts["spread"] = np.concatenate([p == 2 * c + q // 64 for c in range(NC)], 1)
    at, out = {}, []
    n = 0
    for k, v in parts.items():
        at[k] = (n, v.shape[1])
        n += v.shape[1]
        out.append(np.broadcast_to(v, v.shape).astype(np.float32))
    return np.ascontiguousarray(np.concatenate(out, 1)), at


def build(nc, I, O, const, at):
    ctx = ExitStack()
    with ctx:
        sems = {}

        def S(name):
            name = SHARED.get(name, (name, 0))[0]
            if name not in sems:
                sems[name] = ctx.enter_context(nc.semaphore(name))
            return sems[name]

        A = ctx.enter_context(nc.sbuf_tensor("arena", [P, ARENA], F32))
        ps = ctx.enter_context(nc.psum_tensor("ps", [P, 8, 512], F32))
        arena_at = nc.sbuf_base - 4 * ARENA
        cnt_i = ctx.enter_context(nc.sbuf_tensor("cnt_i", [1, E_ + 1], I32))
        pt_i = ctx.enter_context(nc.sbuf_tensor("pt_i", [1, SB * NPG], I32))

        top = [0]

        def cut(n, where=None):
            if where is not None:
                return A[:, where:where + n]
            v = A[:, top[0]:top[0] + n]
            top[0] += n
            assert top[0] <= ARENA, top
            return v

        cut(NSLOT * SLOT)

        def slot_no(n):
            return 0 if n == 5 else n % NSLOT

        def slot(n):
            return A[:, slot_no(n) * SLOT:(slot_no(n) + 1) * SLOT]

        def w_in(n):
            return slot(n).rearrange("p (k n) -> p k n", k=NC)

        def w_down(n):
            return slot(n).rearrange("p (k n) -> p k n", k=NF)

        def landed(n):
            before = 1 if n == 5 or (n % NSLOT == 0 and n > 5) else -1 if n % NSLOT == 5 else 0
            return 16 * (n // NSLOT + 1 + before)

        def chan(v):
            return v.rearrange("p (c t) -> p c t", c=NC)

        xT = chan(cut(NC * T))
        c0 = at["maskp"][0]
        common = cut(c0)
        par = cut(104 + 65)
        ssT = cut(64)
        oneka = cut(8)

        def cst(name):
            o, w = at[name]
            return common[:, o:o + w]

        ident, onesd, ones, bones = cst("ident"), cst("onesd"), cst("ones"), cst("bones")
        eps_ln, eps_lnx = common[:, at["eps"][0]:at["eps"][0] + 1], common[:, at["eps"][0] + 1:at["eps"][0] + 2]
        mixv = [par[:, 8 * i:8 * i + 8] for i in range(6)]
        dw0, aw0, kk0, ka, rkv_, lnx0, lnx1 = [par[:, 48 + 8 * i:56 + 8 * i] for i in range(7)]
        plv = [[[par[:, 104 + 8 * (4 * l + 2 * j + k):112 + 8 * (4 * l + 2 * j + k)] for k in range(2)]
                for j in range(2)] for l in range(2)]
        subv = par[:, 168:169]
        top[0] += (-top[0]) % 8
        base = top[0]

        rT, kT_, vT_, sgT, T1, T2, T3 = [chan(cut(NC * T)) for _ in range(7)]
        lora0 = top[0]
        dw1 = cut(512).rearrange("p (k n) -> p k n", k=NC)
        aw1 = cut(512).rearrange("p (k n) -> p k n", k=NC)
        gw1 = cut(1024).rearrange("p (k n) -> p k n", k=NC)
        dw2, aw2 = cut(1024), cut(1024)
        gw2 = cut(1024)
        hg = cut(T)
        hw, ha = cut(T)[0:64, :], cut(T)[0:64, :]
        XI, XU, YI, LM = [cut(1024, lora0 + 1024 * i).rearrange("p (c s) -> p c s", c=NC) for i in range(4)]
        o = SLOT
        nR = at["ustrict"][0] - c0
        rconst = cut(nR, o)

        def rc(name):
            a, w = at[name]
            return rconst[:, a - c0:a - c0 + w]

        assert nR <= 3072
        STZ = cut(1024, 5 * SLOT + 3072).rearrange("p (c n) -> p c n", c=NC)
        QW = cut(1024, o + 3072).rearrange("p (c n) -> p c n", c=NC)
        RAV, BK, EX = [], [], []
        for o in (2 * SLOT, 0):
            RAV.append(cut(NC * 192, o).rearrange("p (c n) -> p c n", c=NC))
            BK.append(cut(NC * 128, o + 1536).rearrange("p (c n) -> p c n", c=NC))
            EX.append([cut(512, o + 2560 + 512 * i).rearrange("p (c n) -> p c n", c=NC) for i in range(3)])
        o = 3 * SLOT
        SAV = cut(1024, o).rearrange("p (h n) -> p h n", h=H)
        BKt = cut(1024, o + 1024).rearrange("p (c n) -> p c n", c=NC)
        GH = cut(2048, o + 2048).rearrange("p (h n) -> p h n", h=H)
        STS = cut(4096, 4 * SLOT).rearrange("p (c b n) -> p c b n", c=NC, b=SB)
        NAT = [cut(1024, 5 * SLOT + 1024 * i) for i in range(2)]
        U = cut(512, 5 * SLOT + 2048).rearrange("p (c n) -> p c n", c=NC)
        MV = cut(512, 5 * SLOT + 2560).rearrange("p (c n) -> p c n", c=NC)
        OUTS = NAT + [cut(1024, 1024 * i) for i in range(2)]
        QS = NAT[0].rearrange("p (c w t) -> p c w t", c=NC, w=2)
        SAVB = [cut(512, 2 * SLOT + 512 * i).rearrange("p (b n) -> p b n", b=SB) for i in range(2)]

        top[0] = base
        YA = chan(cut(NC * T))
        CT = chan(cut(NC * T))
        SQ = chan(cut(NC * T))
        experts0 = base + NC * T
        top[0] = experts0
        XTM = cut(3 * D).rearrange("p (t n) -> p t n", t=3)
        SelM = [cut(3 * CAP).rearrange("p (t n) -> p t n", t=3) for _ in range(2)]
        HS = cut(F_)
        top[0] += (-top[0]) % 8

        def split(name, n):
            return [nc.alloc_sbuf_tensor_at(f"{name}_{part}", [P, n], FR, offset=arena_at + 4 * (top[0] + i * n))
                    for i, part in enumerate(("hi", "lo"))], cut(2 * n)

        WS = [split(f"w{i}", QUARTER)[0] for i in range(NB)]
        Xg, oXg = split("xg", D)
        Xg = [x[:, :].rearrange("p (c n) -> p c n", c=NC) for x in Xg]
        oXg = oXg[:, 0:D].rearrange("p (c n) -> p c n", c=NC)
        HT, oHT = split("ht", F_)
        YY, oYY = zip(*[split(f"y{e}", D) for e in range(2)])
        oYY = oYY[0][:, 0:D]
        SG = [nc.alloc_sbuf_tensor_at(f"sg{e}", [P, T], FR, offset=arena_at + 4 * (top[0] + e * T)) for e in range(2)]
        oSG = cut(2 * T)[:, 0:T]
        assert top[0] >= base + 3 * NC * T
        RS = cut(T)
        rw = cut(NC * E_).rearrange("p (c n) -> p c n", c=NC)
        rbB = cut(E_)
        mconst0 = at["ustrict"][0]
        nM = at["caus"][0] - mconst0
        mconst = cut(nM)

        def mc(name):
            a, w = at[name]
            return mconst[:, a - mconst0:a - mconst0 + w]

        rt = [cut(48) for _ in range(8)]
        pr6 = cut(72).rearrange("p (g n) -> p g n", g=12)
        gs = [cut(12) for _ in range(4)]
        rank3 = cut(48).rearrange("p (t n) -> p t n", t=3)
        gate3 = cut(48).rearrange("p (t n) -> p t n", t=3)
        cntf = cut(16)
        cntp = cut(8)
        rkp, gtp, gsl = [cut(3) for _ in range(2)], [cut(3) for _ in range(2)], [cut(1) for _ in range(2)]
        top[0] = base
        aKT, aQT, aOT = [chan(cut(NC * T)) for _ in range(3)]
        assert top[0] == base + 3 * NC * T
        aVT = aOT
        VTM = cut(4 * D).rearrange("p (t n) -> p t n", t=4)
        KTM0 = top[0]
        KTM = cut(4 * D).rearrange("p (t n) -> p t n", t=4)
        PGK = [cut(2048, KTM0), cut(2048)]
        PGV = [cut(2048, KTM0 + 2048), cut(2048)]
        PGK = [v.rearrange("p (g n) -> p g n", g=2) for v in PGK]
        PGV = [v.rearrange("p (g n) -> p g n", g=2) for v in PGV]
        k0_ = top[0]
        KTs = [cut(2048).rearrange("p (c n) -> p c n", c=NC), cut(2048, SLOT).rearrange("p (c n) -> p c n", c=NC)]
        PP = [cut(544, k0_ + 544 * i).rearrange("p (j n) -> p j n", j=2) for i in range(2)]
        AT = [cut(384, k0_ + 1088 + 384 * i).rearrange("p (k n) -> p k n", k=3) for i in range(2)]
        Qbd = [cut(1168), cut(1168, SLOT + 2048)]
        PS = [cut(320), cut(320, SLOT + 3216)]
        ATs = [v.rearrange("p (k n) -> p k n", k=3) for v in (cut(192), cut(192, SLOT + 3536))]
        SCB = (4, 7)
        aconst0 = at["caus"][0]
        nA = at["rows"][0] - aconst0
        aconst = cut(nA)

        def ac(name):
            a, w = at[name]
            return aconst[:, a - aconst0:a - aconst0 + w]

        lamt = cut(256)
        lamp = cut(128)
        lams = cut(8)
        st4 = [cut(8) for _ in range(2)]
        aRS = cut(T, k0_)
        aSQ = chan(cut(NC * T, KTM0))
        OUTT = A[:, base:base + 3 * D].rearrange("p (t n) -> p t n", t=3)

        rows0 = at["rows"][0]
        nN = const.shape[1] - rows0
        nconst = [cut(nN, o) for o in (2 * SLOT + 1024, 0)]
        norm16 = [cut(T, o + nN)[0:H, :] for o in (2 * SLOT + 1024, 0)]
        kkn = chan(cut(NC * T, 2 * SLOT))

        def split_at(name, n, where):
            assert where % 8 == 0
            return [nc.alloc_sbuf_tensor_at(f"{name}_{part}", [P, n], FR, offset=arena_at + 4 * (where + i * n))
                    for i, part in enumerate(("hi", "lo"))]

        lora_at = base + 7 * NC * T
        half = NC * T // 2
        PW = [[split_at(f"pw{j}_{i}", D, o + 2 * D * i) for i in range(2)]
              for j, o in enumerate((lora_at, base + 5 * NC * T))]
        PX = [[split_at(f"px{j}_{i}", half, o + 2 * half * i) for i in range(2)]
              for j, o in enumerate((base + 4 * NC * T, base + 3 * NC * T))]

        PWR = [split_at(f"pwr_{i}", D, 5 * SLOT + 2 * D * i) for i in range(2)]
        rx_hi_ = split_at("rx_hi", half, lora_at + 2048)
        rx_lo_ = [split_at(f"rx_lo{i}", half, base + (4 + i) * NC * T) for i in range(3)]

        def rx_part(i, h, c):
            return (rx_lo_[i] if h else rx_hi_)[c // 4][:, T * (c % 4):T * (c % 4) + T]

        def x_part(place, h, c):
            return PX[place][c // 4][h][:, T * (c % 4):T * (c % 4) + T]

        def sum_rows(i, name, c):
            o = at[name][0] - rows0 + H * c
            return nconst[i][:, o:o + H]

        def spread(i, c):
            o = at["spread"][0] - rows0 + P * c
            return nconst[i][0:H, o:o + P]

        def bank(b, n=512):
            return ps[:, b, 0:n]

        block = ctx.enter_context(nc.Block())
        xp_rows = I["x_prompt"][0]
        xs_rows = I["x_sample"].rearrange("b s d -> (b s) d")

        def prime(eng, who):
            for name in CHUNK_PRIMED.get(who, ()):
                eng.sem_inc(S(name), 1)
            eng.sem_inc(S("o_" + who), 1)
            if who == "dve":
                eng.sem_inc(S("add_done"), 1)

        def apart(eng):
            eng.sem_inc(S("apart"), 1)

        def over(stage, n, k):
            for who, stages in OVER.items():
                at_ = 1
                for name, adds in stages:
                    if name == stage:
                        return S("o_" + who), sum(a for _, a in stages) * n + at_ + k
                    at_ += adds

        def overflow(eng, l, who, block, start=None):
            adds = sum(a for _, a in OVER[who])

            def skip(k, n):
                eng.wait_ge(S("o_" + who), adds * n + 1)
                eng.sem_inc(S("o_" + who), adds * k)

            more = NBLK - 1
            most = eng.value_load(cnt_i[0:1, E_:E_ + 1], min_val=0, max_val=T)
            with eng.If(most > CAP):
                with eng.Fori(0, E_) as i:
                    cnt = eng.value_load(cnt_i[0:1, bass.ds(i, 1)], min_val=0, max_val=T)
                    if start:
                        start(i)
                        eng.drain()
                    with eng.Fori(1, NBLK) as b:
                        n = NOV * l + more * i + b - 1
                        with eng.If(cnt > b * CAP):
                            block(i, b, n)
                        with eng.Else():
                            skip(1, n)
            with eng.Else():
                skip(NOV, NOV * l)

        def wait(eng, sem, value):
            if isinstance(value, int) and value <= 0:
                return
            eng.wait_ge(sem, value)

        @block.sync
        def _(sp):
            prime(sp, "sp")

            def load(n, src):
                sp.dma_start(w_in(n) if src.shape[0] == D else w_down(n),
                             src.rearrange("(k p) n -> p k n", p=P)).then_inc(S(f"w_full{slot_no(n)}"), 16)

            def ld(dst, src, name):
                sp.dma_start(dst, src).then_inc(S(name), 16)

            cd = I["const"]
            ld(common, cd[:, 0:c0], "in_common")
            xrow = A[:, base:base + 3 * D].rearrange("p (t n) -> p t n", t=3)
            prow = A[:, base + 3 * D:base + 3 * D + 128]
            prow2 = A[:, base + 3 * D + 128:base + 3 * D + 256]
            srow = A[:, base + 3 * D + 256:base + 3 * D + 384]
            ld(xrow[0:N_META, 0, :], I["meta_tokens"], "in_x")
            ld(xrow[N_META:P, 0, :], xp_rows[0:P - N_META, :], "in_x")
            ld(xrow[:, 1, :], xp_rows[P - N_META:2 * P - N_META, :], "in_x")
            ld(xrow[0:16, 2, :], xp_rows[2 * P - N_META:SEQ, :], "in_x")
            ld(xrow[16:80, 2, :], xs_rows, "in_x")
            ld(prow[0:48, :], I["rwkv_mix"][0].rearrange("i (c p) -> (i c) p", p=P), "in_par")
            ld(prow[48:56, :], I["rwkv_decay_w0"][0].rearrange("(c p) -> c p", p=P), "in_par")
            ld(prow[56:64, :], I["rwkv_a_w0"][0].rearrange("(c p) -> c p", p=P), "in_par")
            ld(prow[64:80, :], I["rwkv_kk_ka"][0].rearrange("i (c p) -> (i c) p", p=P), "in_par")
            ld(prow[80:88, :], I["rwkv_r_k"][0].rearrange("(c h) n -> c (h n)", h=2), "in_par")
            ld(prow[88:104, :], I["rwkv_lnx"][0].rearrange("i (c p) -> (i c) p", p=P), "in_par")
            ld(prow2[0:64, :], I["post_ln"].rearrange("l j k (c p) -> (l j k c) p", p=P), "in_par")
            ld(prow2[64:65, :], I["diff_subln"], "in_par")
            ld(srow[0:64, :], I["state_shift"].rearrange("b a (c p) -> (b a c) p", p=P), "in_par")
            wrkv = I["rwkv_w_rkv"][0]
            for i in range(3):
                for j in range(2):
                    if 2 * i + j == 5:
                        sp.wait_ge(S("rkv_mm"), after("rkv_mm", 4))
                    load(L_RKV + 2 * i + j, wrkv[i][:, 512 * j:512 * j + 512])
            wout = I["rwkv_w_out"][0]
            sp.wait_ge(S("out_wkvp"), 32)
            sp.wait_ge(S("out_wkvs0"), 64)
            sp.wait_ge(S("out_wkvs1"), 64)
            load(L_WO, wout[:, 0:512])
            load(L_WO + 1, wout[:, 512:1024])

            def experts(layer, n0):
                wg, wu, wd = I["moe_w_gate"][layer], I["moe_w_up"][layer], I["moe_w_down"][layer]

                def fetch(n, j, expert, k, sem):
                    src = (wg, wu, wd)[k][bass.ds(expert, 1)].rearrange("a (k p) n -> p (a k) n", p=P)
                    sp.dma_start(w_in(n) if k < 2 else w_down(n), src).then_inc(sem, 16)

                def pair(j, first):
                    for e in range(2):
                        for k in range(3):
                            m = 3 * e + k
                            if first and e == 1 and k == 0:
                                more_blocks()
                            if first:
                                if layer == 0 and m == 0:
                                    sp.wait_ge(S("z_ready"), after("z_ready", 8))
                                if layer == 0 and m >= 4:
                                    sp.wait_ge(S("proj_mm"), 4 * (m - 3))
                                if layer == 1 and m < 4:
                                    sp.wait_ge(S("proj_mm"), 8 + 4 * ((2, 3, 4, 5)[m] + 1))
                                if layer == 1 and m == 2:
                                    sp.wait_ge(S("z2_ready"), after("z2_ready", 8))
                                if layer == 1 and m == 3:
                                    sp.wait_ge(S("past_mm"), SB)
                                if layer == 1 and m >= 4:
                                    sp.wait_ge(S("proj_mm"), 8 + 24 + 4 * (m - 3))
                            else:
                                sp.wait_ge(S("w_lo"), NQ * (E_ * layer + 2 * (j - 1) + e) + 4 * k + 4)
                            fetch(n0 + m, m, 2 * j + e, k, S(f"w_full{(n0 + m) % NSLOT}"))

                def more_blocks():
                    sp.wait_ge(S("proj_mm"), 8 if layer == 0 else 8 + 24 + 8)
                    sp.wait_ge(S("route_ready"), layer + 1)

                    def block(i, b, n):
                        sp.wait_ge(*over("o_sel", n, 0))
                        for k in range(3):
                            fetch(n0 + 3 + k, k, i, k, S("o_sp"))
                    overflow(sp, layer, "sp", block)
                    sp.wait_ge(*over("o_add", NOV * (layer + 1) - 1, 8))

                pair(0, True)
                with sp.Fori(1, PAIRS) as j:
                    pair(j, False)

            experts(0, L_MOE0)
            wkv = I["w_kv_shared"]
            for j in range(6):
                sp.wait_ge(S("w_lo"), NQ * (E_ - 2 + j // 3) + 4 * (j % 3) + 4)
                if j < 4:
                    load(L_KV + j, wkv[:, 512 * j:512 * j + 512])
                else:
                    load(L_Q + j - 4, I["diff_w_q"][0][:, 512 * (j - 4):512 * (j - 4) + 512])
            for j in range(2):
                sp.wait_ge(S("proj_mm"), 8 + 4 * (j + 1))
                load(L_DO + j, I["diff_w_out"][0][:, 512 * j:512 * j + 512])
            experts(1, L_MOE1)

        @block.gpsimd
        def _(pool):
            def ld(dst, src, name):
                pool.dma_start(dst, src).then_inc(S(name), 16)

            cd = I["const"]
            ld(dw1, I["rwkv_decay_w1"][0].rearrange("(k p) n -> p k n", p=P), "in_lora")
            ld(aw1, I["rwkv_a_w1"][0].rearrange("(k p) n -> p k n", p=P), "in_lora")
            ld(gw1, I["rwkv_g_w1"][0].rearrange("(k p) n -> p k n", p=P), "in_lora")
            ld(O["new_shift_prompt"][0], I["x_prompt"][0, SEQ - 1:SEQ, :], "out")
            ld(O["new_shift_sample"].rearrange("b a d -> (b a) d"), I["x_sample"][:, SS - 1, :], "out")
            pool.wait_ge(S("rkv_mm"), after("rkv_mm", 8))
            ld(rconst, cd[:, c0:c0 + nR], "in_rconst")
            pool.wait_ge(S("rkv_mm"), after("rkv_mm", 24))
            ld(dw2[0:64, :], I["rwkv_decay_w2"][0], "in_lora2")
            ld(aw2[0:64, :], I["rwkv_a_w2"][0], "in_lora2")
            ld(gw2, I["rwkv_g_w2"][0], "in_lora2")
            pool.wait_ge(S("rkv_mm"), after("rkv_mm", 24))
            sw = I["state_wkv"]
            for bp in range(4):
                if bp >= 2:
                    pool.wait_ge(S("nat_in_mm"), after("nat_in_mm", 2 * (bp - 1)))
                for e in range(2):
                    ld(NAT[bp % 2][64 * e:64 * e + 64, :].rearrange("p (h j) -> p h j", h=H),
                       sw[2 * bp + e, 0].rearrange("h i j -> i h j"), f"in_nat{bp % 2}")
            pool.wait_ge(S("st_ready"), NFULL + 2)
            ld(nconst[0], cd[:, rows0:rows0 + nN], "in_rows")
            pool.wait_ge(S("wkvp_ready"), after("wkvp_ready", 2))
            for hp in range(2):
                pool.dma_start(O["new_wkv_prompt"][0, 0].rearrange("(c e) i j -> e i c j", e=2)[hp],
                               QW[64 * hp:64 * hp + 64, :, 64 * hp:64 * hp + 64]).then_inc(S("out_wkvp"), 16)
            for bp in range(4):
                pool.wait_ge(S("wkvs_ready"), after("wkvs_ready", 2 * (bp + 1)))
                for e in range(2):
                    pool.dma_start(O["new_wkv_sample"][2 * bp + e, 0].rearrange("h i j -> i h j"),
                                   OUTS[bp][64 * e:64 * e + 64, :].rearrange("p (h j) -> p h j", h=H)
                                   ).then_inc(S(f"out_wkvs{bp % 2}"), 16)
            pool.wait_ge(S("z_ready"), after("z_ready", 8))
            ld(mconst, cd[:, mconst0:mconst0 + nM], "in_mconst")
            ld(rw, I["router_w"].rearrange("(c p) n -> p c n", p=P), "in_mconst")
            ld(rbB, I["router_b"].unsqueeze(0).to_broadcast([P, E_]), "in_mconst")
            pool.wait_ge(S("x_ready"), 16)
            ld(aconst, cd[:, aconst0:aconst0 + nA], "in_aconst")
            ld(lamt, I["diff_lambda"][0].rearrange("i n -> (i n)").unsqueeze(0).to_broadcast([P, 256]), "in_aconst")
            ld(pt_i[:, :], I["page_table"].rearrange("b n -> (b n)").unsqueeze(0), "in_pt")
            for name, ready, tile in (("k", "ktm_ready", KTM), ("v", "vtm_ready", VTM)):
                op = O[f"new_{name}_prompt"][0].rearrange("t h n -> t (h n)")
                os_ = O[f"new_{name}_sample"].rearrange("b s h n -> (b s) (h n)")
                pool.wait_ge(S(ready), after(ready, 8))
                for t, (t0, n) in enumerate(KTILE):
                    dst = op[t0:t0 + n, :] if t < 3 else os_
                    pool.dma_start(dst, tile[0:n, t, :]).then_inc(S(f"out_{name}tm"), 16)
            pool.wait_ge(S("in_pt"), 16)
            pool.wait_ge(S("out_ktm"), 64)
            for b in range(SB):
                pages = [pool.value_load(pt_i[0:1, NPG * b + g:NPG * b + g + 1], min_val=0,
                                         max_val=I["cache_k"].shape[0] - 1) for g in range(NPG)]
                for cache, PG, name in (("cache_k", PGK, "in_pk"), ("cache_v", PGV, "in_pv")):
                    if b >= 2 and PG is PGK:
                        pool.wait_ge(S("kt_mm"), 4 * (b - 1))
                    if b >= 2 and PG is PGV:
                        pool.wait_ge(S("past_mm"), b - 1)
                    src = I[cache].rearrange("a p h n -> a p (h n)")
                    for g in range(NPG):
                        pool.dma_start(PG[b % 2][:, g, :], src[bass.ds(pages[g], 1)].rearrange("a p n -> p (a n)")
                                       ).then_inc(S(f"{name}{b % 2}"), 16)
            pool.wait_ge(S("proj_mm"), 8 + 24)
            ld(nconst[1], cd[:, rows0:rows0 + nN], "in_rows")
            pool.wait_ge(S("z2_ready"), after("z2_ready", 8))
            ld(mconst, cd[:, mconst0:mconst0 + nM], "in_mconst")
            ld(rw, I["router_w"].rearrange("(c p) n -> p c n", p=P), "in_mconst")
            ld(rbB, I["router_b"].unsqueeze(0).to_broadcast([P, E_]), "in_mconst")
            pool.wait_ge(S("y_rows"), 6)
            yp = O["y_prompt"][0]
            ld(yp[0:128, :], OUTT[:, 0, :], "out")
            ld(yp[128:256, :], OUTT[:, 1, :], "out")
            ld(O["y_sample"].rearrange("b s d -> (b s) d"), OUTT[0:64, 2, :], "out")
            pool.wait_ge(S("out"), 16 * 5)
            pool.wait_ge(S("out_wkvp"), 32)
            pool.wait_ge(S("out_wkvs0"), 64)
            pool.wait_ge(S("out_wkvs1"), 64)
            pool.wait_ge(S("out_ktm"), 64)
            pool.wait_ge(S("out_vtm"), 64)


        @block.tensor
        def _(pe):
            prime(pe, "pe")
            def mm(out, lhsT, rhs, start=True, stop=True):
                return pe.matmul(out, lhsT, rhs, start=start, stop=stop)

            def three(out, x, w, start, stop):
                mm(out, x[0], w[0], start, False)
                mm(out, x[1], w[0], False, False)
                return mm(out, x[0], w[1], False, stop)

            pe.wait_ge(S("in_common"), 16)
            prow = A[:, base + 3 * D:base + 3 * D + 128]
            prow2 = A[:, base + 3 * D + 128:base + 3 * D + 256]
            srow = A[:, base + 3 * D + 256:base + 3 * D + 384]
            xrow = A[:, base:base + 3 * D].rearrange("p (t n) -> p t n", t=3)
            pe.wait_ge(S("in_x"), 16 * 5)
            for t, (t0, n) in enumerate(TOK):
                for hf in range(2):
                    for c in range(4):
                        i = pe.transpose(ps[:, 1 + 2 * t + hf, n * c:n * c + n],
                                         xrow[0:n, t, P * (4 * hf + c):P * (4 * hf + c) + P], ident[0:n, 0:n])
                    i.then_inc(S("xt_mm"), 1)
            pe.wait_ge(S("in_par"), 16 * 9)
            pe.transpose(ps[:, 0, 0:104], prow[0:104, :], ident[0:104, 0:104])
            pe.transpose(ps[:, 0, 128:193], prow2[0:65, :], ident[0:65, 0:65])
            pe.transpose(ps[:, 0, 256:320], srow[0:64, :], ident[0:64, 0:64]).then_inc(S("par_mm"), 1)

            for i in range(3):
                for co in range(NC):
                    n = 8 * i + co
                    pe.wait_ge(S("rw_hi"), n + 1)
                    pe.wait_ge(S("rw_lo"), n + 1)
                    if n >= 4:
                        pe.wait_ge(S("rkv_ev"), after("rkv_ev", n - 3))
                    for k in range(NC):
                        if co == 0:
                            pe.wait_ge(S("rx_hi"), 8 * i + k + 1)
                            pe.wait_ge(S("rx_lo"), 8 * i + k + 1)
                        m = three(bank(n % 4, T), [PWR[n % 2][h][:, P * k:P * k + P] for h in range(2)],
                                  [rx_part(i, h, k) for h in range(2)], k == 0, k == NC - 1)
                    m.then_inc(S("rkv_mm"), 1)
            for c in range(NC):
                pe.wait_ge(S("kksq_ready"), c + 1)
                if c >= 4:
                    pe.wait_ge(S("kks_ev"), after("kks_ev", c - 3))
                mm(bank(4 + c % 4, T), bones, kkn[:, c, :]).then_inc(S("kks_mm"), 1)
            pe.wait_ge(S("kks_ev"), after("kks_ev", 8))
            pe.wait_ge(S("in_lora"), 48)
            for i, (w, X, M) in enumerate(((dw1, T1, 64), (aw1, T2, 64), (gw1, T3, 128))):
                pe.wait_ge(S("mix_ready"), after("mix_ready", 8 * (i + 4)))
                for k in range(NC):
                    m = mm(ps[0:M, 4 + i, 0:T], w[:, k, :], X[:, k, :], k == 0, k == NC - 1)
                m.then_inc(S("lora_mm"), 1)
            pe.wait_ge(S("lora_ev"), after("lora_ev", 3))
            pe.wait_ge(S("in_lora2"), 48)
            for i, (w, X) in enumerate(((dw2, hw), (aw2, ha))):
                for co in range(NC):
                    n = 8 * i + co
                    if n >= 4:
                        pe.wait_ge(S("lz_ev"), after("lz_ev", n - 3))
                    mm(bank(4 + n % 4, T), w[0:64, P * co:P * co + P], X).then_inc(S("lz_mm"), 1)
            pe.wait_ge(S("lz_ev"), after("lz_ev", 16))
            for bp in range(4):
                pe.wait_ge(S(f"in_nat{bp % 2}"), 32 * (bp // 2 + 1))
                for hf in range(2):
                    n = 2 * bp + hf
                    if n >= 4:
                        pe.wait_ge(S("nat_ev"), after("nat_ev", n - 3))
                    for c in range(4):
                        m = pe.transpose(ps[:, 4 + n % 4, P * c:P * c + P],
                                         NAT[bp % 2][:, P * (4 * hf + c):P * (4 * hf + c) + P], ident)
                    m.then_inc(S("nat_in_mm"), 1)
            pe.wait_ge(S("nat_ev"), after("nat_ev", 8))

            def chunk(n, par, sample):
                rav, bk = RAV[par], BK[par]
                pe.wait_ge(S("ops_ready"), after("ops_ready", 1 * n + 1))
                pe.wait_ge(S("u_ready"), after("u_ready", 2 * n))
                for b, src, o0, name in ((0, bk, 0, "bkt_mm"), (2, rav, 64, "avt_mm")):
                    for hf in range(2):
                        for c in range(4):
                            m = pe.transpose(ps[:, b + hf, P * c:P * c + P], src[:, 4 * hf + c, o0:o0 + P], ident)
                        m.then_inc(S(name), 1)
                pe.wait_ge(S("sa_ready"), after("sa_ready", 2 * n))
                pe.wait_ge(S("o_ready"), after("o_ready", 1 * n))
                pe.wait_ge(S("st_ready"), 1 * n + 1)
                for hp in range(2):
                    q = slice(64 * hp, 64 * hp + 64)
                    for hf in range(2):
                        for c in range(4):
                            m = mm(ps[:, 4 + 2 * hp + hf, P * c:P * c + P], bk[q, 4 * hf + c, :], rav[q, 4 * hf + c, 0:128])
                        m.then_inc(S("gh_mm"), 1)
                pe.wait_ge(S("bkt_ready"), 2 * n + 2)
                apart(pe)
                for hp in range(2):
                    q = slice(64 * hp, 64 * hp + 64)
                    for c in range(NC):
                        o = P * (c % 4) + 64 * hp
                        m = mm(ps[q, c // 4, o:o + 64], rav[q, c, 64:128], bk[q, c, 0:64])
                    m.then_inc(S("l_mm"), 1)
                pe.wait_ge(S("sv_ready"), 2 * n + 2)
                apart(pe)
                for hf in range(2):
                    for hp in range(2):
                        q = slice(64 * hp, 64 * hp + 64)
                        for c in range(4 * hf, 4 * hf + 4):
                            o = P * (c % 4) + 64 * hp
                            m = mm(ps[q, 2 + hf, o:o + 64], bk[q, c, 0:64], rav[q, c, 64:128])
                    m.then_inc(S("lt_mm"), 1)
                pe.wait_ge(S("gh_ready"), 4 * n + 4)
                pe.wait_ge(S("lm_ready"), 2 * n + 2)
                levels = 2 if sample else LEVELS - 1
                for lv in range(1, levels + 1):
                    for hf in range(2):
                        if lv == 1:
                            pe.wait_ge(S("inv_ready"), 11 * n + 1)
                        else:
                            pe.wait_ge(S("inv_ready"), 11 * n + 1 + 2 * (lv - 2) + hf + 1)
                            pe.wait_ge(S("y_ready"), 10 * n + 2 * (lv - 2) + hf + 1)
                        for c in range(4):
                            m = mm(ps[:, 4 + hf, P * c:P * c + P], LM[:, 4 * hf + c, :], XU[:, 4 * hf + c, :])
                        m.then_inc(S("y_mm"), 1)
                    for hf in range(2):
                        pe.wait_ge(S("y_ready"), 10 * n + 2 * (lv - 1) + hf + 1)
                        bx = (6, 7) if hf == 0 else (0, 1)
                        if lv < levels:
                            for c in range(4):
                                mm(ps[:, bx[0], P * c:P * c + P], YI[:, 4 * hf + c, :], XI[:, 4 * hf + c, :])
                        for c in range(4):
                            m = mm(ps[:, bx[1], P * c:P * c + P], XI[:, 4 * hf + c, :], YI[:, 4 * hf + c, :])
                        m.then_inc(S("xu_mm"), 1)
                    if lv == 1:
                        for hf in range(2):
                            for c in range(4):
                                for hp in range(2):
                                    h = 2 * (4 * hf + c) + hp
                                    m = mm(ps[64 * hp:64 * hp + 64, 2 + hf, 64 * c:64 * c + 64],
                                           GH[64:128, h, 64:128], SAV[64:128, h, :])
                            m.then_inc(S("mv_mm"), 1)
                pe.wait_ge(S("mv_ready"), 2 * n + 2)
                pe.wait_ge(S("inv_ready"), 11 * n + 2 * levels + 1)
                apart(pe)
                if sample:
                    for hp in range(2):
                        q = slice(64 * hp, 64 * hp + 64)
                        for hf in range(2):
                            for c in range(4):
                                ov = ps[q, 2 * hp + hf, P * c:P * c + P].rearrange("p (w t) -> p w t", w=2)
                                rv = rav[q, 4 * hf + c, 0:128].rearrange("p (w t) -> p w t", w=2)
                                for b in range(SB):
                                    m = mm(ov[:, :, 8 * b:8 * b + 8], STS[q, 4 * hf + c, b, :], rv[:, :, 8 * b:8 * b + 8])
                            m.then_inc(S("qs_mm"), 1)
                    pe.wait_ge(S("qs_ready"), 4)
                for hf in range(2):
                    for c in range(4):
                        for hp in range(2):
                            q = slice(64 * hp, 64 * hp + 64)
                            out = ps[q, 2 + hf, 64 * c:64 * c + 64]
                            if sample:
                                m = mm(out, QS[q, 4 * hf + c, 1, :], ident[q, q])
                            else:
                                m = mm(out, rav[q, 4 * hf + c, 64:128], STZ[q, 4 * hf + c, q])
                    m.then_inc(S("u_mm"), 1)
                pe.wait_ge(S("u_ready"), after("u_ready", 2 * n + 2))
                apart(pe)
                for hp in range(2):
                    q = slice(64 * hp, 64 * hp + 64)
                    for c in range(NC):
                        m = mm(ps[0:64, 4 + hp, 64 * c:64 * c + 64], XU[q, c, q], U[q, c, :])
                    m.then_inc(S("sa_mm"), 1)
                pe.wait_ge(S("sa_ready"), after("sa_ready", 2 * n + 2))
                for c in range(NC):
                    if not sample:
                        mm(ps[:, 6, 64 * c:64 * c + 64], STZ[:, c, :], rav[:, c, 0:64], True, False)
                    for hp in range(2):
                        m = mm(ps[64 * hp:64 * hp + 64, 6, 64 * c:64 * c + 64], SAV[:, 2 * c + hp, :],
                               GH[:, 2 * c + hp, 0:64], sample, True)
                m.then_inc(S("o_mm"), 1)
                if not sample:
                    for c in range(NC):
                        for hp in range(2):
                            m = mm(ps[64 * hp:64 * hp + 64, 7, 64 * c:64 * c + 64], BKt[:, c, 64 * hp:64 * hp + 64],
                                   SAV[:, 2 * c + hp, :])
                    m.then_inc(S("st_mm"), 1)

            with pe.Fori(0, NFULL // 2) as i:
                for side in range(2):
                    chunk(2 * i + side, side, False)
            pe.wait_ge(S("tail_ready"), 1)
            chunk(NFULL, 0, False)
            chunk(NFULL + 1, 1, True)
            for h in range(H):
                c, hp = h // 2, h % 2
                pe.wait_ge(S("savb_ready"), h + 1)
                if c >= 2:
                    pe.wait_ge(S("sts_ready"), c - 1)
                if h == 0:
                    pe.wait_ge(S("o_ready"), after("o_ready", NFULL + 2))
                mm(ps[64 * hp:64 * hp + 64, 6 + c % 2, :], BKt[:, c, 64 * hp:64 * hp + 64],
                   SAVB[h % 2].rearrange("p b n -> p (b n)")).then_inc(S("ss_mm"), 1)
            for hf in range(2):
                for c in range(4):
                    m = pe.transpose(ps[:, 4 + hf, P * c:P * c + P], STZ[:, 4 * hf + c, :], ident)
                m.then_inc(S("wkvp_mm"), 1)
            pe.wait_ge(S("sts_ready"), 8)
            for bp in range(4):
                for hf in range(2):
                    n = 2 * bp + hf
                    if n >= 4:
                        pe.wait_ge(S("wkvs_ready"), after("wkvs_ready", n - 3))
                    for c in range(4):
                        m = pe.transpose(ps[:, n % 4, P * c:P * c + P],
                                         STS[:, 4 * hf + c, 2 * bp:2 * bp + 2, :].rearrange("p b n -> p (b n)"), ident)
                    m.then_inc(S("wkvs_mm"), 1)
            pe.wait_ge(S("wkvp_ready"), after("wkvp_ready", 2))
            for c in range(NC):
                if c >= 4:
                    pe.wait_ge(S("gn_c"), after("gn_c", c - 3))
                else:
                    pe.wait_ge(S("wkvs_ready"), after("wkvs_ready", 8))
                mm(bank(c % 4, T), bones, T3[:, c, :]).then_inc(S("gn_mm"), 1)
            pe.wait_ge(S("in_rows"), 16)
            for c in range(NC):
                pe.wait_ge(S("gn_sq"), after("gn_sq", c + 1))
                m = mm(ps[0:H, 4, 0:T], sum_rows(0, "rows", c), T1[:, c, :], c == 0, c == NC - 1)
            m.then_inc(S("gn_vm"), 1)
            for c in range(NC):
                pe.wait_ge(S("rkr_ready"), after("rkr_ready", c + 1))
                pe.wait_ge(*((S("gn_c"), after("gn_c", c + 5)) if c < 4 else (S("bn_ev"), after("bn_ev", c - 3))))
                mm(bank(c % 4, T), bones, rT[:, c, :]).then_inc(S("bn_mm"), 1)
            pe.wait_ge(S("gr_ready"), after("gr_ready", 1))
            for c in range(NC):
                if c >= 4:
                    pe.wait_ge(S("gr_ev"), after("gr_ev", c - 3))
                mm(bank(4 + c % 4, T), spread(0, c), norm16[0]).then_inc(S("gr_mm"), 1)
            for c in range(NC):
                pe.wait_ge(*((S("bn_ev"), after("bn_ev", c + 5)) if c < 4 else (S("z_ready"), after("z_ready", c - 3))))
                mm(bank(c % 4, T), gw2[:, P * c:P * c + P], hg).then_inc(S("g_mm"), 1)
            pe.wait_ge(S("z_ready"), after("z_ready", 8))

            def proj(place, m0, x0, outs, freed, base_ev):
                for co in range(outs):
                    pe.wait_ge(S("pw_hi"), m0 + co + 1)
                    pe.wait_ge(S("pw_lo"), m0 + co + 1)
                    if co >= 4:
                        pe.wait_ge(S(freed), base_ev + co - 3)
                    for k in range(NC):
                        if co == 0:
                            pe.wait_ge(S("px_hi"), x0 + k + 1)
                            pe.wait_ge(S("px_lo"), x0 + k + 1)
                        m = three(bank(co % 4, T), [PW[place][(m0 + co) % 2][h][:, P * k:P * k + P] for h in range(2)],
                                  [x_part(place, h, k) for h in range(2)], k == 0, k == NC - 1)
                    m.then_inc(S("proj_mm"), 1)

            def layer_norm(i):
                for c in range(NC):
                    pe.wait_ge(S("ln_in"), 8 * i + c + 1)
                    m = mm(bank(6, T), onesd, YA[:, c, :], c == 0, c == NC - 1)
                m.then_inc(S("ln_mean"), 1)
                for c in range(NC):
                    pe.wait_ge(S("ln_sq"), 8 * i + c + 1)
                    m = mm(bank(7, T), onesd, SQ[:, c, :], c == 0, c == NC - 1)
                m.then_inc(S("ln_var"), 1)

            def gather(par, half):
                for c in range(4 * half, 4 * half + 4):
                    for t, (t0, k) in enumerate(TOK):
                        m = mm(ps[:, half, P * (c % 4):P * (c % 4) + P], XTM[0:k, t, P * c:P * c + P],
                               SelM[par][0:k, t, :], t == 0, t == 2)
                return m

            def turn_select(par):
                for t, (t0, k) in enumerate(TOK):
                    pe.transpose(ps[:, 3, t0:t0 + k], SelM[par][0:k, t, :], ident[0:k, 0:k])
                for t, (t0, k) in enumerate(TOK):
                    m = mm(ps[:, 3, 400:401], SelM[par][0:k, t, :], gtp[par][0:k, t:t + 1], t == 0, t == 2)
                return m

            def more_block(n0, n):
                pe.wait_ge(*over("o_sel", n, 1))
                gather(0, 0)
                gather(0, 1).then_inc(S("o_pe"), 1)
                pe.wait_ge(*over("o_xg", n, 1))
                pe.wait_ge(*over("o_weights", n, 48))
                for k in range(2):
                    w = w_in(n0 + 3 + k)
                    for c in range(NC):
                        m = mm(bank(2 + k), oXg[:, c, :], w[:, c, :], c == 0, c == NC - 1)
                m.then_inc(S("o_pe"), 1)
                pe.wait_ge(*over("o_h", n, 1))
                for f in range(NF):
                    pe.transpose(ps[:, 2, P * f:P * f + P], HS[:, P * f:P * f + P], ident)
                turn_select(0).then_inc(S("o_pe"), 1)
                pe.wait_ge(*over("o_ht", n, 1))
                w = w_down(n0 + 5)
                for hf in range(2):
                    for f in range(NF):
                        m = mm(bank(4 + hf), oHT[:, P * f:P * f + P], w[:, f, 512 * hf:512 * hf + 512], f == 0, f == NF - 1)
                m.then_inc(S("o_pe"), 1)
                pe.wait_ge(*over("o_y", n, 1))
                for c in range(NC):
                    if c >= 2:
                        pe.wait_ge(*over("o_add", n, c - 1))
                    mm(bank(6 + c % 2, T), oYY[:, P * c:P * c + P], oSG).then_inc(S("o_pe"), 1)

            def quarter(n):
                pe.wait_ge(S("w_hi"), n + 1)
                pe.wait_ge(S("w_lo"), n + 1)

            def scatter(s):
                for c in range(NC):
                    pe.wait_ge(S("add_done"), 8 * s + 1 + max(c - 1, 0))
                    for e in range(2):
                        for h in range(2):
                            m = mm(bank(6 + c % 2, T), YY[e][h][:, P * c:P * c + P], SG[e][:, :], e + h == 0, e + h == 2)
                    m.then_inc(S("sc_mm"), 1)

            def expert(l, n0, j, e, first, last):
                G = E_ * l + 2 * j + e
                pe.wait_ge(S("xg_hi"), 2 * G + 2)
                pe.wait_ge(S("xg_lo"), 2 * G + 2)
                for k in range(2):
                    wait(pe, S("ht_lo") if k == 0 else S("sg_ready"), G)
                    for q in range(4):
                        quarter(NQ * G + 4 * k + q)
                        b = (4 * k + q) % NB
                        for c in (2 * q, 2 * q + 1):
                            m = three(bank(2 + k), [Xg[h][:, c, :] for h in range(2)],
                                      [WS[b][h][:, 512 * (c % 2):512 * (c % 2) + 512] for h in range(2)], c == 0, c == NC - 1)
                        m.then_inc(S("w_used"), 1)
                more = not (last and e == 1)
                if more:
                    pe.wait_ge(S("sel_ready"), G + 2)
                    gather(1 - e, 0).then_inc(S("ga_mm"), 1)
                pe.wait_ge(S("h_ready"), G + 1)
                for f in range(NF):
                    m = pe.transpose(ps[:, 2, P * f:P * f + P], HS[:, P * f:P * f + P], ident)
                m.then_inc(S("turn_mm"), 1)
                if more:
                    gather(1 - e, 1).then_inc(S("gb_mm"), 1)
                if e == 0 and not first:
                    pe.wait_ge(S("y_lo"), 2 * G)
                    pe.wait_ge(S("sg_ready"), G)
                    scatter(PAIRS * l + j - 1)
                turn_select(e).then_inc(S("sgt_mm"), 1)
                pe.wait_ge(S("ht_hi"), G + 1)
                pe.wait_ge(S("ht_lo"), G + 1)
                wait(pe, S("y_lo"), 2 * G)
                for f in range(NF):
                    quarter(NQ * G + 8 + f)
                    b = (8 + f) % NB
                    for hf in range(2):
                        m = three(bank(4 + hf), [HT[h][:, P * f:P * f + P] for h in range(2)],
                                  [WS[b][h][:, 512 * hf:512 * hf + 512] for h in range(2)], f == 0, f == NF - 1)
                    m.then_inc(S("w_used"), 1)

            def experts(l, n0):
                pe.wait_ge(S("in_mconst"), 48 * (l + 1))
                for t, (t0, n) in enumerate(TOK):
                    for c in range(NC):
                        if t == 0:
                            pe.wait_ge(S("x_ready"), 16 * l + c + 1)
                        m = mm(ps[0:n, 6, E_ * t:E_ * t + E_], xT[:, c, t0:t0 + n], rw[:, c, :], c == 0, c == NC - 1)
                m.then_inc(S("rt_mm"), 1)
                for t, (t0, n) in enumerate(TOK):
                    for hf in range(2):
                        for c in range(4):
                            m = pe.transpose(ps[0:n, 2 * t + hf, P * c:P * c + P], xT[:, 4 * hf + c, t0:t0 + n], ident)
                        m.then_inc(S("xtm_mm"), 1)
                pe.wait_ge(S("msk_ready"), l + 1)
                for t in range(3):
                    for u in range(t + 1):
                        mm(ps[:, 7, E_ * t:E_ * t + E_], mc("ustrict") if u == t else ones, rt[6][:, E_ * u:E_ * u + E_],
                           u == 0, u == t)
                for u in range(3):
                    m = mm(ps[:, 7, 64:64 + E_], ones, rt[6][:, E_ * u:E_ * u + E_], u == 0, u == 2)
                m.then_inc(S("rk_mm"), 1)
                pe.wait_ge(S("xtm_ready"), 6 * (l + 1))
                pe.wait_ge(S("route_ready"), l + 1)
                overflow(pe, l, "pe", lambda i, b, n: more_block(n0, n))
                pe.wait_ge(*over("o_y", NOV * (l + 1) - 1, 1))
                pe.wait_ge(*over("o_add", NOV * (l + 1) - 1, 8))
                pe.wait_ge(S("sel_ready"), E_ * l + 1)
                gather(0, 0).then_inc(S("ga_mm"), 1)
                gather(0, 1).then_inc(S("gb_mm"), 1)
                for e in range(2):
                    expert(l, n0, 0, e, True, False)
                with pe.Fori(1, PAIRS - 1) as j:
                    for e in range(2):
                        expert(l, n0, j, e, False, False)
                for e in range(2):
                    expert(l, n0, PAIRS - 1, e, False, True)
                pe.wait_ge(S("y_lo"), 2 * E_ * (l + 1))
                pe.wait_ge(S("sg_ready"), E_ * (l + 1))
                scatter(PAIRS * (l + 1) - 1)

            proj(0, 0, 0, NC, "ln_in", 0)
            layer_norm(0)
            experts(0, L_MOE0)
            layer_norm(1)
            proj(1, 8, 8, 24, "kvq_ev", 0)
            for i, (X, name) in enumerate(((aKT, "ktr_mm"), (aVT, "vtr_mm"))):
                pe.wait_ge(S("kvq_ev"), 8 * (i + 1))
                for t, (t0, n) in enumerate(KTILE):
                    for hf in range(2):
                        j = 8 * i + 2 * t + hf
                        if j >= 4:
                            if j < 12:
                                pe.wait_ge(S("ktm_ready"), after("ktm_ready", min(j - 3, 8)))
                            else:
                                pe.wait_ge(S("vtm_ready"), after("vtm_ready", j - 11))
                        for c in range(4):
                            m = pe.transpose(ps[0:n, 4 + j % 4, P * c:P * c + P], X[:, 4 * hf + c, t0:t0 + n], ident)
                        m.then_inc(S(name), 1)
            pe.wait_ge(S("kvq_ev"), 24)
            pe.wait_ge(S("vtm_ready"), after("vtm_ready", 8))
            pe.wait_ge(S("in_aconst"), 32)

            units = [(t, h) for t in range(3) for h in range(NH)]

            def scores(u):
                t, h = units[u]
                q0, nq = KTILE[t]
                nk = q0 + nq
                if u >= 2:
                    pe.wait_ge(S("p_exp"), 2 * (u - 1))
                for j in range(2):
                    q = slice(64 * j, 64 * j + 64)
                    b = 2 * (u % 2) + j
                    mm(ps[0:nq, b, 0:nk], aQT[q, h, q0:q0 + nq], aKT[q, h, 0:nk], True, False)
                    m = mm(ps[0:nq, b, q0:nk], ident[:, 0:nq], ac("caus")[:, 0:nq], False, True)
                m.then_inc(S("p_sc"), 1)

            def turn(u):
                t, h = units[u]
                q0, nq = KTILE[t]
                pe.wait_ge(S("p_am"), u + 1)
                if u >= 2:
                    pe.wait_ge(S("p_at"), u - 1)
                for kt in range(t + 1):
                    k0, n = KTILE[kt]
                    m = pe.transpose(ps[0:n, 4 + u % 2, P * kt:P * kt + nq], PP[u % 2][0:nq, 0, k0:k0 + n], ident[0:nq, 0:nq])
                m.then_inc(S("p_tr"), 1)

            def values(u):
                t, h = units[u]
                q0, nq = KTILE[t]
                pe.wait_ge(S("p_at"), u + 1)
                if u >= 2:
                    pe.wait_ge(S("p_oev"), u - 1)
                for kt in range(t + 1):
                    k0, n = KTILE[kt]
                    m = mm(ps[:, 6 + u % 2, 0:nq], VTM[0:n, kt, P * h:P * h + P], AT[u % 2][0:n, kt, 0:nq], kt == 0, kt == t)
                m.then_inc(S("p_av"), 1)

            NU = len(units)
            for i in range(NU + 2):
                if i < NU:
                    scores(i)
                if 1 <= i <= NU:
                    turn(i - 1)
                if i >= 2:
                    values(i - 2)
            pe.wait_ge(S("p_exp"), 2 * NU)
            pe.wait_ge(S("p_oev"), NU)
            def turn_keys(b):
                pe.wait_ge(S(f"in_pk{b % 2}"), 32 * (b // 2 + 1))
                if b:
                    pe.wait_ge(S("kts_a"), 2 * b)
                    pe.wait_ge(S("kts_d"), 2 * b)
                for g in range(NPG):
                    for hf in range(2):
                        for c in range(4):
                            m = pe.transpose(ps[:, 2 * g + hf, P * c:P * c + P],
                                             PGK[b % 2][:, g, P * (4 * hf + c):P * (4 * hf + c) + P], ident)
                        m.then_inc(S("kt_mm"), 1)

            def new_scores(b):
                pe.wait_ge(S("qbd_ready"), b + 1)
                if b >= 2:
                    pe.wait_ge(S("s_exp"), b - 1)
                qb = Qbd[b % 2][:, 0:1024].rearrange("p (c n) -> p c n", c=NC)
                sc = ps[:, SCB[b % 2], :]
                for c in range(NC):
                    mm(sc[:, 256:320], qb[:, c, :], aKT[:, c, TP:T], c == 0, False)
                w0 = TS - SS - 8 * b
                mm(sc[:, 256:320], ident, ac("win")[:, w0:w0 + TS], False, True)

            def past_scores(b, c):
                if c == 0:
                    pe.wait_ge(S("kts_a"), 2 * b + 2)
                    pe.wait_ge(S("kts_d"), 2 * b + 2)
                m = mm(ps[:, SCB[b % 2], 0:256], Qbd[b % 2][:, P * c:P * c + P], KTs[b % 2][:, c, :], c == 0, c == NC - 1)
                if c == NC - 1:
                    m.then_inc(S("s_sc"), 1)

            def turn_weights(b):
                pe.wait_ge(S("s_am"), b + 1)
                if b:
                    pe.wait_ge(S("s_at"), 2 * b)
                for kt in range(3):
                    n = P if kt < 2 else TS
                    m = pe.transpose(ps[0:n, 5, P * kt:P * kt + P], PS[b % 2][:, P * kt:P * kt + n], ident)
                m.then_inc(S("s_tr"), 1)

            def values_of(b, h):
                if h == 0:
                    pe.wait_ge(S(f"in_pv{b % 2}"), 32 * (b // 2 + 1))
                    pe.wait_ge(S("s_at"), 2 * b + 2)
                    if b:
                        pe.wait_ge(S("s_oev"), b)
                at_ = ATs[b % 2]
                o = ps[:, 6, SS * h:SS * h + SS]
                for g in range(2):
                    mm(o, PGV[b % 2][:, g, P * h:P * h + P], at_[:, g, SS * h:SS * h + SS], g == 0, False)
                m = mm(o, VTM[0:TS, 3, P * h:P * h + P], at_[0:TS, 2, SS * h:SS * h + SS], False, True)
                if h == NH - 1:
                    m.then_inc(S("past_mm"), 1)

            turn_keys(0)
            new_scores(0)
            for c in range(NC):
                past_scores(0, c)
            for b in range(SB):
                more = b + 1 < SB
                if more:
                    turn_keys(b + 1)
                turn_weights(b)
                if more:
                    new_scores(b + 1)
                for h in range(NH):
                    if more:
                        past_scores(b + 1, h)
                    values_of(b, h)
            pe.wait_ge(S("in_rows"), 32)
            for c in range(NC):
                pe.wait_ge(S("sl_sq"), after("sl_sq", c + 1))
                m = mm(ps[0:H, 0, 0:T], sum_rows(1, "rows2", c), aSQ[:, c, :], c == 0, c == NC - 1)
            m.then_inc(S("sl_mm"), 1)
            pe.wait_ge(S("sr_ready"), after("sr_ready", 1))
            for c in range(NC):
                if c >= 4:
                    pe.wait_ge(S("z2_ready"), after("z2_ready", c - 3))
                mm(bank(4 + c % 4, T), spread(1, c), norm16[1]).then_inc(S("sr_mm"), 1)
            proj(1, 32, 16, NC, "ln_in", 16)
            layer_norm(2)
            experts(1, L_MOE1)
            layer_norm(3)
            pe.wait_ge(S("x_ready"), 32)
            for t, (t0, n) in enumerate(((N_META, P), (N_META + P, P), (TP, TS))):
                for hf in range(2):
                    for c in range(4):
                        m = pe.transpose(ps[0:n, 2 * t + hf, P * c:P * c + P], xT[:, 4 * hf + c, t0:t0 + n], ident)
                    m.then_inc(S("yo_mm"), 1)

        @block.scalar
        def _(act):
            prime(act, "act")
            def f(out, in_, func, **k):
                return act.activation(out, in_, func, **k)

            def copy(out, in_):
                return act.copy(out, in_)

            def rw_hi(n):
                b = L_RKV + n // 4
                if n % 4 == 0:
                    act.wait_ge(S(f"w_full{slot_no(b)}"), landed(b))
                if n >= 2:
                    act.wait_ge(S("rkv_mm"), after("rkv_mm", n - 1))
                f(PWR[n % 2][0][:, :].rearrange("p (k n) -> p k n", k=NC), w_in(b)[:, :, P * (n % 4):P * (n % 4) + P],
                  ACT.Copy).then_inc(S("rw_hi"), 1)

            rw_hi(0)
            for n in range(24):
                i, c = n // 8, n % 8
                if c == 0:
                    if i:
                        act.wait_ge(S("rkv_mm"), after("rkv_mm", 8 * i))
                    for k in range(NC):
                        act.wait_ge(S("mix_ready"), after("mix_ready", 8 * i + k + 1))
                        f(rx_part(i, 0, k), (T1, T2, T3)[i][:, k, :], ACT.Copy).then_inc(S("rx_hi"), 1)
                if n + 1 < 24:
                    rw_hi(n + 1)
                if n == 16:
                    act.wait_ge(S("rkv_ev"), after("rkv_ev", 16))
                    for k in range(NC):
                        f(kkn[:, k, :], kT_[:, k, :], ACT.Square, scale=kk0[:, k:k + 1]).then_inc(S("kksq_ready"), 1)
                act.wait_ge(S("rkv_mm"), after("rkv_mm", n + 1))
                copy((rT, kT_, vT_)[i][:, c, :], bank(n % 4, T)).then_inc(S("rkv_ev"), 1)
            for c in range(NC):
                act.wait_ge(S("kks_mm"), after("kks_mm", c + 1))
                f(kkn[:, c, :], bank(4 + c % 4, T), ACT.Sqrt).then_inc(S("kks_ev"), 1)
            act.wait_ge(S("lora_mm"), after("lora_mm", 1))
            f(hw, ps[0:64, 4, 0:T], ACT.Tanh).then_inc(S("lora_ev"), 1)
            act.wait_ge(S("lora_mm"), after("lora_mm", 2))
            copy(ha, ps[0:64, 5, 0:T]).then_inc(S("lora_ev"), 1)
            act.wait_ge(S("lora_mm"), after("lora_mm", 3))
            f(hg, ps[:, 6, 0:T], ACT.Sigmoid).then_inc(S("lora_ev"), 1)
            act.wait_ge(S("mix_ready"), after("mix_ready", 48))
            for i, (X, w0) in enumerate(((sgT, dw0), (T3, aw0))):
                for c in range(NC):
                    act.wait_ge(S("lz_mm"), after("lz_mm", 8 * i + c + 1))
                    f(X[:, c, :], bank(4 + c % 4, T), ACT.Sigmoid, bias=w0[:, c:c + 1]).then_inc(S("lz_ev"), 1)
            for n in range(8):
                bp, hf = n // 2, n % 2
                act.wait_ge(S("nat_in_mm"), after("nat_in_mm", n + 1))
                copy(STS[:, 4 * hf:4 * hf + 4, 2 * bp:2 * bp + 2, :].rearrange("p c b n -> p c (b n)"),
                     bank(4 + n % 4).rearrange("p (c n) -> p c n", c=4)).then_inc(S("nat_ev"), 1)
            act.wait_ge(S("prep_ready"), 1)

            def factors(n, par, t0, w, part):
                cols, ex = bass.ds(t0, w), EX[par]
                if part == 0:
                    act.wait_ge(S("st_ready"), n)
                    f(ex[0][:, :, 0:w], T3[:, :, cols], ACT.Exp, scale=-KAPPA).then_inc(S("ex_ready"), 1)
                    f(ex[1][:, :, 0:w], T3[:, :, cols], ACT.Exp, scale=KAPPA).then_inc(S("ex_ready"), 1)
                else:
                    act.wait_ge(S("lx_ready"), n + 1)
                    f(ex[2][:, :, 0:w], ex[2][:, :, 0:w], ACT.Exp, scale=-KAPPA).then_inc(S("ex_ready"), 1)

            def chunk(n, par, t0, w, sample, nxt):
                cols = bass.ds(t0, w)
                for hf in range(2):
                    act.wait_ge(S("bkt_mm"), 2 * n + hf + 1)
                    copy(BKt[:, 4 * hf:4 * hf + 4, :].rearrange("p c n -> p (c n)"), bank(hf)).then_inc(S("bkt_ready"), 1)
                for hp in range(2):
                    q = slice(64 * hp, 64 * hp + 64)
                    act.wait_ge(S("l_mm"), 2 * n + hp + 1)
                    copy(LM[q, :, q], ps[q, 0:2, :].rearrange("p b (c n) -> p (b c) n", c=4)[:, :, q]).then_inc(S("lm_ready"), 1)
                levels = 2 if sample else LEVELS - 1
                for lv in range(1, levels + 1):
                    for hf in range(2):
                        act.wait_ge(S("y_mm"), 10 * n + 2 * (lv - 1) + hf + 1)
                        copy(YI[:, 4 * hf:4 * hf + 4, :].rearrange("p c n -> p (c n)"), bank(4 + hf)).then_inc(S("y_ready"), 1)
                    if lv == 1:
                        for hf in range(2):
                            act.wait_ge(S("mv_mm"), 2 * n + hf + 1)
                            act.wait_ge(S("u_ready"), after("u_ready", 2 * n))
                            copy(MV[:, 4 * hf:4 * hf + 4, :].rearrange("p c n -> p (c n)"), bank(2 + hf, 256)
                                 ).then_inc(S("mv_ready"), 1)
                    if nxt and lv <= 2:
                        factors(n + 1, 1 - par, *nxt, lv - 1)
                if sample:
                    for hp in range(2):
                        for hf in range(2):
                            q = slice(64 * hp, 64 * hp + 64)
                            act.wait_ge(S("qs_mm"), 2 * hp + hf + 1)
                            copy(QS[q, 4 * hf:4 * hf + 4, :, :].rearrange("p c w t -> p (c w t)"), ps[q, 2 * hp + hf, :]
                                 ).then_inc(S("qs_ready"), 1)
                for hp in range(2):
                    act.wait_ge(S("sa_mm"), after("sa_mm", 2 * n + hp + 1))
                    copy(SAV.rearrange("p (c e) n -> p e c n", e=2)[0:64, hp], ps[0:64, 4 + hp, :].rearrange("p (c n) -> p c n", c=NC)
                         ).then_inc(S("sa_ready"), 1)
                if not sample:
                    act.wait_ge(S("o_mm"), after("o_mm", 1 * n + 1))
                    apart(act)
                    copy(T3[:, :, cols], bank(6).rearrange("p (c t) -> p c t", c=NC)[:, :, 0:w]).then_inc(S("o_ready"), 1)

            act.wait_ge(S("st_ready"), 1)
            for part in range(2):
                factors(0, 0, 0, C, part)
            with act.Fori(0, NFULL // 2) as i:
                for side in range(2):
                    t0 = (2 * i + side) * C
                    chunk(2 * i + side, side, t0, C, False, (t0 + C, C))
            chunk(NFULL, 0, NFULL * C, TP - NFULL * C, False, (TP, TS))
            chunk(NFULL + 1, 1, TP, TS, True, None)
            for hf in range(2):
                act.wait_ge(S("wkvp_mm"), after("wkvp_mm", hf + 1))
                copy(QW[:, 4 * hf:4 * hf + 4, :].rearrange("p c n -> p (c n)"), bank(4 + hf)).then_inc(S("wkvp_ready"), 1)
            for n in range(8):
                bp, hf = n // 2, n % 2
                act.wait_ge(S("wkvs_mm"), after("wkvs_mm", n + 1))
                if n == 0:
                    act.wait_ge(S("o_ready"), after("o_ready", NFULL + 2))
                copy(OUTS[bp][:, 512 * hf:512 * hf + 512], bank(n % 4)).then_inc(S("wkvs_ready"), 1)
            for c in range(NC):
                act.wait_ge(S("gn_c"), after("gn_c", c + 1))
                f(T1[:, c, :], sgT[:, c, :], ACT.Square).then_inc(S("gn_sq"), 1)
            act.wait_ge(S("gn_vm"), after("gn_vm", 1))
            f(norm16[0], ps[0:H, 4, 0:T], ACT.Sqrt, scale=1.0 / N, bias=eps_lnx[0:H]).then_inc(S("gn_s"), 1)

            def layer_norm(i, l, j, meanwhile=None):
                for c in range(NC):
                    act.wait_ge(S("ln_c"), 8 * i + c + 1)
                    f(SQ[:, c, :], CT[:, c, :], ACT.Square).then_inc(S("ln_sq"), 1)
                if meanwhile:
                    meanwhile()
                act.wait_ge(S("ln_var"), i + 1)
                f(RS, bank(7, T), ACT.Sqrt, bias=eps_ln).then_inc(S("ln_rs"), 1)
                for c in range(NC):
                    act.wait_ge(S("ln_n"), 8 * i + c + 1)
                    f(xT[:, c, :], CT[:, c, :], ACT.Identity, scale=plv[l][j][0][:, c:c + 1],
                      bias=plv[l][j][1][:, c:c + 1]).then_inc(S("x_ready"), 1)

            def more_block(n):
                act.wait_ge(*over("o_gather", n, 1))
                f(oXg, ps[:, 0:2, :].rearrange("p b (c n) -> p (b c) n", c=4), ACT.Copy).then_inc(S("o_act"), 1)
                act.wait_ge(*over("o_gate_up", n, 1))
                f(HS, bank(2), ACT.Silu).then_inc(S("o_act"), 1)
                act.wait_ge(*over("o_turn", n, 1))
                f(oHT[:, 0:F_], bank(2), ACT.Copy)
                f(oSG, bank(3, T), ACT.Copy)
                f(gsl[0], ps[:, 3, 400:401], ACT.Copy).then_inc(S("o_act"), 1)
                act.wait_ge(*over("o_down", n, 1))
                act.wait_ge(*over("o_ht", n, 1))
                f(oYY, ps[:, 4:6, :].rearrange("p b n -> p (b n)"), ACT.Identity, scale=gsl[0]).then_inc(S("o_act"), 1)

            def w_hi(l, n0, j, e, q):
                G = E_ * l + 2 * j + e
                n = n0 + 3 * e + q // 4
                if q % 4 == 0:
                    act.wait_ge(S(f"w_full{n % NSLOT}"), landed(n) + 16 * j)
                wait(act, S("w_used"), NQ * G + q + 1 - NB)
                f(WS[q % NB][0][:, :], slot(n)[:, QUARTER * (q % 4):QUARTER * (q % 4 + 1)], ACT.Copy).then_inc(S("w_hi"), 1)

            def xg_hi(G, half):
                act.wait_ge(S("gb_mm" if half else "ga_mm"), G + 1)
                f(Xg[0][:, 4 * half:4 * half + 4, :].rearrange("p c n -> p (c n)"), bank(half), ACT.Copy).then_inc(S("xg_hi"), 1)

            def expert(l, n0, j, e, first, last):
                G = E_ * l + 2 * j + e
                more = not (last and e == 1)
                for q in range(NB, 8):
                    w_hi(l, n0, j, e, q)
                act.wait_ge(S("w_used"), NQ * G + 4)
                f(HS, bank(2), ACT.Silu).then_inc(S("hs_ready"), 1)
                for q in range(8, NQ):
                    w_hi(l, n0, j, e, q)
                if more:
                    xg_hi(G + 1, 0)
                act.wait_ge(S("turn_mm"), G + 1)
                f(HT[0][:, :], bank(2), ACT.Copy).then_inc(S("ht_hi"), 1)
                if more:
                    xg_hi(G + 1, 1)
                act.wait_ge(S("sgt_mm"), G + 1)
                f(SG[e][:, :], bank(3, T), ACT.Copy)
                f(gsl[e], ps[:, 3, 400:401], ACT.Copy).then_inc(S("sg_ready"), 1)
                if more:
                    for q in range(NB):
                        w_hi(l, n0, j + e, 1 - e, q)
                act.wait_ge(S("w_used"), NQ * G + NQ)
                act.wait_ge(S("sg_ready"), G + 1)
                for hf in range(2):
                    f(YY[e][0][:, 512 * hf:512 * hf + 512], bank(4 + hf), ACT.Identity, scale=gsl[e]).then_inc(S("y_hi"), 1)

            def experts(l, n0):
                for q in range(2):
                    w_hi(l, n0, 0, 0, q)
                act.wait_ge(S("rt_mm"), l + 1)
                act.wait_ge(S("rt_zero"), l + 1)
                f(rt[0][:, 0:32], ps[:, 6, 0:32], ACT.Sigmoid)
                f(rt[0][0:TOK[2][1], 32:48], ps[0:TOK[2][1], 6, 32:48], ACT.Sigmoid).then_inc(S("s_ready"), 1)
                for t, (t0, n) in enumerate(TOK):
                    for hf in range(2):
                        act.wait_ge(S("xtm_mm"), 6 * l + 2 * t + hf + 1)
                        copy(XTM[0:n, t, 512 * hf:512 * hf + 512], ps[0:n, 2 * t + hf, :]).then_inc(S("xtm_ready"), 1)
                for q in range(2, NB):
                    w_hi(l, n0, 0, 0, q)
                act.wait_ge(S("route_ready"), l + 1)
                overflow(act, l, "act", lambda i, b, n: more_block(n))
                xg_hi(E_ * l, 0)
                xg_hi(E_ * l, 1)
                for e in range(2):
                    expert(l, n0, 0, e, True, False)
                with act.Fori(1, PAIRS - 1) as j:
                    for e in range(2):
                        expert(l, n0, j, e, False, False)
                for e in range(2):
                    expert(l, n0, PAIRS - 1, e, False, True)

            def pw_hi(place, n0, m0, co):
                n = n0 + co // 4
                if co % 4 == 0:
                    act.wait_ge(S(f"w_full{slot_no(n)}"), landed(n))
                wait(act, S("proj_mm"), m0 + co - 1)
                f(PW[place][(m0 + co) % 2][0][:, :].rearrange("p (k n) -> p k n", k=NC),
                  w_in(n)[:, :, P * (co % 4):P * (co % 4) + P], ACT.Copy).then_inc(S("pw_hi"), 1)

            def px_hi(place, X, c):
                f(x_part(place, 0, c), X[:, c, :], ACT.Copy).then_inc(S("px_hi"), 1)

            pw_hi(0, L_WO, 0, 0)
            for c in range(NC):
                act.wait_ge(S("z_ready"), after("z_ready", c + 1))
                px_hi(0, T3, c)
            for co in range(1, NC):
                pw_hi(0, L_WO, 0, co)
            layer_norm(0, 0, 0)
            experts(0, L_MOE0)
            layer_norm(1, 0, 1, lambda: pw_hi(1, L_KV, 8, 0))
            for c in range(NC):
                act.wait_ge(S("x_ready"), 8 + c + 1)
                px_hi(1, xT, c)
            pw_hi(1, L_KV, 8, 1)
            for i, X in enumerate((aKT, aVT, aQT)):
                for c in range(NC):
                    j = 8 * i + c
                    if j + 2 < 24:
                        pw_hi(1, L_KV, 8, j + 2)
                    act.wait_ge(S("proj_mm"), 8 + j + 1)
                    copy(X[:, c, :], bank(c % 4, T)).then_inc(S("kvq_ev"), 1)
            act.wait_ge(S("lam_s"), 1)
            f(lams[:, 2:4], lams[:, 0:2], ACT.Exp).then_inc(S("lam_e"), 1)
            units = [(t, h) for t in range(3) for h in range(NH)]

            def weights_out(u):
                t, h = units[u]
                nq = KTILE[t][1]
                act.wait_ge(S("p_tr"), u + 1)
                if u >= 2:
                    act.wait_ge(S("p_av"), u - 1)
                for lo, hi in ((0, min(t + 1, 2)), (2, t + 1)):
                    if lo < hi:
                        k = KTILE[lo][1]
                        i = copy(AT[u % 2][0:k, lo:hi, 0:nq],
                                 ps[0:k, 4 + u % 2, P * lo:P * hi].rearrange("p (k n) -> p k n", n=P)[:, :, 0:nq])
                i.then_inc(S("p_at"), 1)

            NU = len(units)
            for u in range(NU + 1):
                if u >= 1:
                    weights_out(u - 1)
                if u < NU:
                    t, h = units[u]
                    nq = KTILE[t][1]
                    nk = KTILE[t][0] + nq
                    act.wait_ge(S("p_nb"), u + 1)
                    if u >= 2:
                        act.wait_ge(S("p_tr"), u - 1)
                    for j in range(2):
                        f(PP[u % 2][0:nq, j, 0:nk], ps[0:nq, 2 * (u % 2) + j, 0:nk], ACT.Exp, scale=0.125,
                          bias=st4[u % 2][0:nq, j:j + 1], accum_out=st4[u % 2][0:nq, 2 + j:3 + j]).then_inc(S("p_exp"), 1)
            for b in range(SB):
                for hf in range(2):
                    act.wait_ge(S("kt_mm"), 4 * b + hf + 1)
                    copy(KTs[b % 2][:, 4 * hf:4 * hf + 4, 0:P], bank(hf).rearrange("p (c n) -> p c n", c=4)).then_inc(S("kts_a"), 1)
                act.wait_ge(S("s_nb"), b + 1)
                if b >= 2:
                    act.wait_ge(S("s_tr"), b - 1)
                st = st4[b % 2]
                f(PS[b % 2], ps[:, SCB[b % 2], 0:320], ACT.Exp, scale=0.125, bias=st[:, 0:1],
                  accum_out=st[:, 2:3]).then_inc(S("s_exp"), 1)
            act.wait_ge(S("s_oev"), SB)
            for c in range(NC):
                f(aSQ[:, c, :], aOT[:, c, :], ACT.Square).then_inc(S("sl_sq"), 1)
            act.wait_ge(S("sl_mm"), after("sl_mm", 1))
            f(norm16[1], ps[0:H, 0, 0:T], ACT.Sqrt, scale=1.0 / P, bias=eps_ln[0:H]).then_inc(S("sl_s"), 1)
            act.wait_ge(S("out_ktm"), 64)
            act.wait_ge(S("out_vtm"), 64)
            pw_hi(1, L_DO, 32, 0)
            for c in range(NC):
                act.wait_ge(S("z2_ready"), after("z2_ready", c + 1))
                px_hi(1, aOT, c)
            for co in range(1, NC):
                pw_hi(1, L_DO, 32, co)
            layer_norm(2, 1, 0)
            experts(1, L_MOE1)
            layer_norm(3, 1, 1)
            for t in range(3):
                n = P if t < 2 else TS
                act.wait_ge(S("yo_mm"), 2 * t + 1)
                copy(OUTT[0:n, t, 0:512], ps[0:n, 2 * t, :]).then_inc(S("y_rows"), 1)

        @block.vector
        def _(dve):
            prime(dve, "dve")
            tt, tsc, stt, cp = dve.tensor_tensor, dve.tensor_scalar, dve.scalar_tensor_tensor, dve.tensor_copy
            for t, (t0, n) in enumerate(TOK):
                for hf in range(2):
                    dve.wait_ge(S("xt_mm"), 2 * t + hf + 1)
                    cp(xT[:, 4 * hf:4 * hf + 4, t0:t0 + n], ps[:, 1 + 2 * t + hf, 0:4 * n].rearrange("p (c n) -> p c n", c=4))
            dve.drain()
            tt(sgT[:, :, 1:T], xT[:, :, 0:T - 1], xT[:, :, 1:T], ALU.subtract)
            dve.wait_ge(S("par_mm"), 1)
            cp(par[:, 0:104], ps[:, 0, 0:104])
            cp(par[:, 104:169], ps[:, 0, 128:193])
            cp(ssT, ps[:, 0, 256:320])
            dve.drain()
            tsc(oneka, ka, -1.0, 1.0, ALU.mult, ALU.add)
            tsc(sgT[:, :, 0:1], xT[:, :, 0:1], -1.0, None, ALU.mult)
            tt(sgT[:, :, TP:T:SS], ssT.rearrange("p (b c) -> p c b", c=NC), xT[:, :, TP:T:SS], ALU.subtract)
            dve.drain()
            def mix(i, chunks):
                m, X = ((0, T1), (2, T2), (3, T3), (1, T1), (4, T2), (5, T3))[i]
                for c in chunks:
                    stt(X[:, c, :], sgT[:, c, :], mixv[m][:, c:c + 1], xT[:, c, :], ALU.mult, ALU.add
                        ).then_inc(S("mix_ready"), 1)

            def rw_lo(n):
                dve.wait_ge(S("rw_hi"), n + 1)
                hi, lo = [v[:, :].rearrange("p (k n) -> p k n", k=NC) for v in PWR[n % 2]]
                tt(lo, w_in(L_RKV + n // 4)[:, :, P * (n % 4):P * (n % 4) + P], hi.bitcast(F32), ALU.subtract
                   ).then_inc(S("rw_lo"), 1)

            def rx_lo(i, c):
                dve.wait_ge(S("rx_hi"), 8 * i + c + 1)
                tt(rx_part(i, 1, c), (T1, T2, T3)[i][:, c, :], rx_part(i, 0, c).bitcast(F32), ALU.subtract
                   ).then_inc(S("rx_lo"), 1)

            mix(0, (0, 1))
            rw_lo(0)
            for c in range(NC):
                mix(0, range(c + 2, min(c + 3, NC)))
                rx_lo(0, c)
            halves = (range(0, 4), range(4, 8))
            mixes = {1: (1, 0), 2: (1, 1), 3: (2, 0), 4: (2, 1), 9: (3, 0), 10: (3, 1), 17: (4, 0), 18: (4, 1)}
            for n in range(24):
                if n % 8 == 0 and n:
                    for c in range(NC):
                        rx_lo(n // 8, c)
                if n + 1 < 24:
                    rw_lo(n + 1)
                if n in mixes:
                    i, hf = mixes[n]
                    if i >= 3:
                        dve.wait_ge(S("rkv_mm"), after("rkv_mm", 8 * (i - 2)))
                    mix(i, halves[hf])
            dve.wait_ge(S("rkv_mm"), after("rkv_mm", 24))
            mix(5, range(NC))
            dve.wait_ge(S("kks_ev"), after("kks_ev", 8))
            tsc(kkn, kkn, 1e-12, -1.0, ALU.max, ALU.mult)
            dve.drain()
            dve.reciprocal(kkn, kkn)
            dve.memset(STZ, 0.0)
            dve.drain()
            dve.wait_ge(S("lora_mm"), after("lora_mm", 1))
            for c in range(NC):
                stt(T1[:, c, :], kT_[:, c, :], kk0[:, c:c + 1], kkn[:, c, :], ALU.mult, ALU.mult)
            dve.wait_ge(S("lz_ev"), after("lz_ev", 16))
            dve.drain()
            stt(T2, T1, -1.0, T3, ALU.mult, ALU.mult)
            dve.drain()
            for c in range(NC):
                tsc(T3[:, c, :], T3[:, c, :], ka[:, c:c + 1], oneka[:, c:c + 1], ALU.mult, ALU.add)
            dve.drain()
            tt(kT_, kT_, T3, ALU.mult)
            dve.drain()
            dve.wait_ge(S("in_rconst"), 16)
            for c in range(NC):
                dve.tensor_tensor_scan(T3[:, c, :], rc("scan"), sgT[:, c, :], 0.0, ALU.mult, ALU.add)
            dve.memset(LM, 0.0)
            dve.drain().then_inc(S("prep_ready"), 1)
            dve.wait_ge(S("nat_ev"), after("nat_ev", 8))
            dve.nop().then_inc(S("st_ready"), 1)
            dve.wait_ge(S("prep_ready"), 1)

            def operands(n, par, t0, w, part):
                cols, rav, bk, ex = bass.ds(t0, w), RAV[par], BK[par], EX[par]
                if part == 0:
                    tt(ex[2][:, :, 0:w], T3[:, :, cols], sgT[:, :, cols], ALU.subtract).then_inc(S("lx_ready"), 1)
                if part == 1:
                    if not isinstance(n, int) or n > 0:
                        dve.wait_ge(S("o_mm"), after("o_mm", 1 * n - 1))
                    dve.wait_ge(S("ex_ready"), 3 * n + 3)
                    tt(rav[:, :, 0:w], rT[:, :, cols], ex[0][:, :, 0:w], ALU.mult)
                    tt(rav[:, :, 64:64 + w], T1[:, :, cols], ex[2][:, :, 0:w], ALU.mult)
                if part == 2:
                    cp(rav[:, :, 128:128 + w], vT_[:, :, cols])
                    tt(bk[:, :, 0:w], T2[:, :, cols], ex[1][:, :, 0:w], ALU.mult)
                if part == 3:
                    tt(bk[:, :, 64:64 + w], kT_[:, :, cols], ex[1][:, :, 0:w], ALU.mult).then_inc(S("ops_ready"), 1)

            def chunk(n, par, t0, w, sample, nxt):
                cols = bass.ds(t0, w)
                dve.wait_ge(S("sa_mm"), after("sa_mm", 2 * n))
                cp(XI, ident.unsqueeze(1).to_broadcast([P, NC, P]))
                cp(XU, ident.unsqueeze(1).to_broadcast([P, NC, P]))
                for hf in range(2):
                    dve.wait_ge(S("avt_mm"), 2 * n + hf + 1)
                    cp(SAV[64:128, 8 * hf:8 * hf + 8, :].rearrange("p h n -> p (h n)"), ps[64:128, 2 + hf, :]
                       ).then_inc(S("sv_ready"), 1)
                mask = rc("masks" if sample else "maskp").unsqueeze(1).to_broadcast([P, 4, P])
                gv = GH.rearrange("p (c e) n -> p e c n", e=2)
                for hp in range(2):
                    for hf in range(2):
                        dve.wait_ge(S("gh_mm"), 4 * n + 2 * hp + hf + 1)
                        tt(gv[:, hp, 4 * hf:4 * hf + 4, :], bank(4 + 2 * hp + hf).rearrange("p (c n) -> p c n", c=4),
                           mask, ALU.mult).then_inc(S("gh_ready"), 1)

                def level(name, m):
                    return rc(name)[:, P * m:P * m + P].bitcast(U32).unsqueeze(1).to_broadcast([P, 4, P])

                def c4(b):
                    return bank(b).rearrange("p (c n) -> p c n", c=4)

                dve.drain()
                dve.wait_ge(S("lm_ready"), 2 * n + 2)
                apart(dve)
                for hf in range(2):
                    dve.copy_predicated(XI[:, 4 * hf:4 * hf + 4, :], level("low", 0), LM[:, 4 * hf:4 * hf + 4, :])
                for hf in range(2):
                    dve.wait_ge(S("lt_mm"), 2 * n + hf + 1)
                    apart(dve)
                    i = dve.copy_predicated(XU[:, 4 * hf:4 * hf + 4, :], level("up", 0), c4(2 + hf))
                i.then_inc(S("inv_ready"), 1)
                levels = 2 if sample else LEVELS - 1
                for lv in range(1, levels + 1):
                    for hf in range(2):
                        h4 = slice(4 * hf, 4 * hf + 4)
                        bx = (6, 7) if hf == 0 else (0, 1)
                        dve.wait_ge(S("xu_mm"), 10 * n + 2 * (lv - 1) + hf + 1)
                        apart(dve)
                        if lv < levels:
                            dve.copy_predicated(XI[:, h4, :], level("low", lv), c4(bx[0]))
                        dve.copy_predicated(XU[:, h4, :], level("up", lv), c4(bx[1])).then_inc(S("inv_ready"), 1)
                    if nxt and lv != 2:
                        operands(n + 1, 1 - par, *nxt, max(lv - 2, 0))
                for hf in range(2):
                    h4 = slice(4 * hf, 4 * hf + 4)
                    dve.wait_ge(S("u_mm"), 2 * n + hf + 1)
                    dve.wait_ge(S("mv_ready"), 2 * n + hf + 1)
                    tt(U[:, h4, :].rearrange("p c n -> p (c n)"), bank(2 + hf, 256),
                       MV[:, h4, :].rearrange("p c n -> p (c n)"), ALU.add).then_inc(S("u_ready"), 1)
                if sample:
                    dve.wait_ge(S("o_mm"), after("o_mm", 1 * n + 1))
                    tt(T3[:, :, cols], bank(6).rearrange("p (c t) -> p c t", c=NC), QS[:, :, 0, :], ALU.add
                       ).then_inc(S("o_ready"), 1)
                else:
                    dve.wait_ge(S("st_mm"), 1 * n + 1)
                    for hp in range(2):
                        q = slice(64 * hp, 64 * hp + 64)
                        tt(STZ[q, :, q], bank(7).rearrange("p (c n) -> p c n", c=NC)[q], STZ[q, :, q], ALU.add)
                    dve.drain()
                    for hp in range(2):
                        q = slice(64 * hp, 64 * hp + 64)
                        i = tt(STZ[q, :, q], STZ[q, :, q], EX[par][0][q, :, w - 1:w].to_broadcast([64, NC, 64]), ALU.mult)
                    i.then_inc(S("st_ready"), 1)

            for part in range(4):
                operands(0, 0, 0, C, part)
            with dve.Fori(0, NFULL // 2) as i:
                for side in range(2):
                    t0 = (2 * i + side) * C
                    chunk(2 * i + side, side, t0, C, False, (t0 + C, C))
            for v in (RAV[0], BK[0]):
                dve.memset(v.rearrange("p c (w t) -> p (c w) t", t=C)[:, :, TP % C:C], 0.0)
            dve.drain().then_inc(S("tail_ready"), 1)
            chunk(NFULL, 0, NFULL * C, TP - NFULL * C, False, (TP, TS))
            chunk(NFULL + 1, 1, TP, TS, True, None)

            def state_update(dve, c):
                dve.wait_ge(S("ss_mm"), after("ss_mm", 2 * c + 2))
                v = STS[:, c, :, :]
                tt(v, bank(6 + c % 2).rearrange("p (b n) -> p b n", b=SB), v, ALU.add)
                dve.drain()
                tt(v, v, EX[1][0][:, c, SS - 1:TS:SS].unsqueeze(2).to_broadcast([P, SB, N]), ALU.mult
                   ).then_inc(S("sts_ready"), 1)

            for h in range(H):
                c, hp = h // 2, h % 2
                if h >= 2:
                    dve.wait_ge(S("ss_mm"), after("ss_mm", h - 1))
                if h == 0:
                    dve.wait_ge(S("sa_ready"), after("sa_ready", 2 * (NFULL + 2)))
                tt(SAVB[h % 2], SAV[:, h, :].unsqueeze(1).to_broadcast([P, SB, N]),
                   rc("bm").unsqueeze(2).to_broadcast([P, SB, N]), ALU.mult).then_inc(S("savb_ready"), 1)
                if hp and c >= 1:
                    state_update(dve, c - 1)
            state_update(dve, NC - 1)

            tt(rT, rT, kT_, ALU.mult)
            dve.drain()
            for c in range(NC):
                tsc(rT[:, c, :], rT[:, c, :], rkv_[:, c:c + 1], None, ALU.mult).then_inc(S("rkr_ready"), 1)
            for c in range(NC):
                dve.wait_ge(S("gn_mm"), after("gn_mm", c + 1))
                stt(sgT[:, c, :], bank(c % 4, T), -1.0 / N, T3[:, c, :], ALU.mult, ALU.add).then_inc(S("gn_c"), 1)
            dve.wait_ge(S("gn_s"), after("gn_s", 1))
            dve.reciprocal(norm16[0], norm16[0]).then_inc(S("gr_ready"), 1)
            for c in range(NC):
                dve.wait_ge(S("bn_mm"), after("bn_mm", c + 1))
                tt(T2[:, c, :], bank(c % 4, T), vT_[:, c, :], ALU.mult).then_inc(S("bn_ev"), 1)
            dve.drain()
            for c in range(NC):
                tsc(T2[:, c, :], T2[:, c, :], lnx1[:, c:c + 1], None, ALU.add)
            for c in range(NC):
                dve.wait_ge(S("gr_mm"), after("gr_mm", c + 1))
                tt(sgT[:, c, :], sgT[:, c, :], bank(4 + c % 4, T), ALU.mult).then_inc(S("gr_ev"), 1)
            dve.drain()
            for c in range(NC):
                stt(sgT[:, c, :], sgT[:, c, :], lnx0[:, c:c + 1], T2[:, c, :], ALU.mult, ALU.add)
            dve.drain()

            def pw_lo(place, n0, m0, co):
                dve.wait_ge(S("pw_hi"), m0 + co + 1)
                hi, lo = [v[:, :].rearrange("p (k n) -> p k n", k=NC) for v in PW[place][(m0 + co) % 2]]
                tt(lo, w_in(n0 + co // 4)[:, :, P * (co % 4):P * (co % 4) + P], hi.bitcast(F32), ALU.subtract
                   ).then_inc(S("pw_lo"), 1)

            def px_lo(place, X, x0, c):
                dve.wait_ge(S("px_hi"), x0 + c + 1)
                tt(x_part(place, 1, c), X[:, c, :], x_part(place, 0, c).bitcast(F32), ALU.subtract).then_inc(S("px_lo"), 1)

            for c in range(NC + 1):
                if c < NC:
                    dve.wait_ge(S("g_mm"), after("g_mm", c + 1))
                    tt(T3[:, c, :], sgT[:, c, :], bank(c % 4, T), ALU.mult).then_inc(S("z_ready"), 1)
                if c == 0:
                    pw_lo(0, L_WO, 0, 0)
                else:
                    px_lo(0, T3, 0, c - 1)
            pw_lo(0, L_WO, 0, 1)

            def residual(place, n0, base_mm):
                for c in range(NC):
                    dve.wait_ge(S("proj_mm"), base_mm + c + 1)
                    stt(YA[:, c, :], xT[:, c, :], ALPHA, bank(c % 4, T), ALU.mult, ALU.add).then_inc(S("ln_in"), 1)
                    if c + 2 < NC:
                        pw_lo(place, n0, base_mm, c + 2)

            def layer_norm(i, meanwhile=None):
                dve.wait_ge(S("ln_mean"), i + 1)
                for c in range(NC):
                    tt(CT[:, c, :], YA[:, c, :], bank(6, T), ALU.subtract).then_inc(S("ln_c"), 1)
                if meanwhile:
                    meanwhile()
                dve.wait_ge(S("ln_rs"), i + 1)
                dve.reciprocal(RS, RS)
                dve.drain()
                for c in range(NC):
                    tt(CT[:, c, :], CT[:, c, :], RS, ALU.mult).then_inc(S("ln_n"), 1)

            def select(par):
                dve.drain()
                return tt(SelM[par], mc("iota").unsqueeze(1).to_broadcast([P, 3, CAP]),
                          rkp[par].unsqueeze(2).to_broadcast([P, 3, CAP]), ALU.is_equal)

            def pick(par, i):
                cp(rkp[par].unsqueeze(2), rank3[:, :, bass.ds(i, 1)])
                cp(gtp[par].unsqueeze(2), gate3[:, :, bass.ds(i, 1)])

            def more_block(i, b, n):
                tsc(rkp[0], rkp[0], -float(CAP), None, ALU.add)
                select(0).then_inc(S("o_dve"), 1)
                dve.wait_ge(*over("o_silu", n, 1))
                tt(HS, HS, bank(3), ALU.mult).then_inc(S("o_dve"), 1)
                for c in range(NC):
                    dve.wait_ge(*over("o_scatter", n, c + 1))
                    tt(YA[:, c, :], YA[:, c, :], bank(6 + c % 2, T), ALU.add).then_inc(S("o_dve"), 1)

            def w_lo(l, n0, j, e, q):
                G = E_ * l + 2 * j + e
                dve.wait_ge(S("w_hi"), NQ * G + q + 1)
                tt(WS[q % NB][1][:, :], slot(n0 + 3 * e + q // 4)[:, QUARTER * (q % 4):QUARTER * (q % 4 + 1)],
                   WS[q % NB][0][:, :].bitcast(F32), ALU.subtract).then_inc(S("w_lo"), 1)

            def xg_lo(G, half):
                dve.wait_ge(S("xg_hi"), 2 * G + half + 1)
                h, lo = [x[:, 4 * half:4 * half + 4, :].rearrange("p c n -> p (c n)") for x in Xg]
                tt(lo, bank(half), h.bitcast(F32), ALU.subtract).then_inc(S("xg_lo"), 1)

            def adds(s_):
                for c in range(NC):
                    dve.wait_ge(S("sc_mm"), 8 * s_ + c + 1)
                    tt(YA[:, c, :], YA[:, c, :], bank(6 + c % 2, T), ALU.add).then_inc(S("add_done"), 1)

            def expert(l, n0, j, e, first, last):
                G = E_ * l + 2 * j + e
                more = not (last and e == 1)
                for q in range(NB, NQ - 1):
                    w_lo(l, n0, j, e, q)
                dve.wait_ge(S("hs_ready"), G + 1)
                dve.wait_ge(S("w_used"), NQ * G + 8)
                tt(HS, HS, bank(3), ALU.mult).then_inc(S("h_ready"), 1)
                w_lo(l, n0, j, e, NQ - 1)
                if more:
                    xg_lo(G + 1, 0)
                dve.wait_ge(S("ht_hi"), G + 1)
                tt(HT[1][:, :], bank(2), HT[0][:, :].bitcast(F32), ALU.subtract).then_inc(S("ht_lo"), 1)
                if more:
                    xg_lo(G + 1, 1)
                if e == 0 and not first:
                    adds(PAIRS * l + j - 1)
                if not last:
                    dve.wait_ge(S("sgt_mm"), G + 1)
                    pick(e, 2 * j + e + 2)
                    select(e).then_inc(S("sel_ready"), 1)
                if more:
                    for q in range(NB):
                        w_lo(l, n0, j + e, 1 - e, q)
                for hf in range(2):
                    dve.wait_ge(S("y_hi"), 2 * G + hf + 1)
                    v = slice(512 * hf, 512 * hf + 512)
                    stt(YY[e][1][:, v], bank(4 + hf), gsl[e], YY[e][0][:, v].bitcast(F32), ALU.mult, ALU.subtract
                        ).then_inc(S("y_lo"), 1)

            def experts(l, n0):
                dve.memset(rt[0], 0.0).then_inc(S("rt_zero"), 1)
                dve.wait_ge(S("x_ready"), 16 * l + 8)
                dve.memset(YA, 0.0)
                for q in range(2):
                    w_lo(l, n0, 0, 0, q)
                dve.wait_ge(S("in_mconst"), 48 * (l + 1))
                dve.wait_ge(S("s_ready"), l + 1)

                def v3(x):
                    return x.rearrange("p (t n) -> p t n", t=3)

                def g12(x):
                    return x.rearrange("p (g n) -> p g n", n=4)

                score, sel, a1, a2, oh, msk0, msk, _ = rt
                gm, ga, gb, gc = gs
                m12 = ga[:, 0:12]
                tt(v3(sel), v3(score), rbB.unsqueeze(1).to_broadcast([P, 3, E_]), ALU.add)
                dve.drain()
                for d, o, k in ((1, 0, 3), (2, 3, 2), (3, 5, 1)):
                    tt(pr6[:, :, o:o + k], g12(sel)[:, :, 0:k], g12(sel)[:, :, d:d + k], ALU.add)
                dve.drain()
                dve.tensor_reduce(gm, pr6, AX, ALU.max)
                dve.drain()
                top1 = cntf[:, 0:3]

                def first_best(dst, val, tmp, width, weight):
                    dve.tensor_reduce(top1, v3(val), AX, ALU.max)
                    dve.drain()
                    tt(v3(tmp), v3(val), top1.unsqueeze(2).to_broadcast([P, 3, width]), ALU.is_equal)
                    dve.drain()
                    tt(v3(tmp), v3(tmp), weight.unsqueeze(1).to_broadcast([P, 3, width]), ALU.mult)
                    dve.drain()
                    dve.tensor_reduce(top1, v3(tmp), AX, ALU.max)
                    dve.drain()
                    tt(v3(dst), top1.unsqueeze(2).to_broadcast([P, 3, width]),
                       weight.unsqueeze(1).to_broadcast([P, 3, width]), ALU.is_equal)
                    dve.drain()

                first_best(gb, gm, ga, G_, mc("w4"))
                gmask = gb.unsqueeze(2).to_broadcast([P, 12, 4])
                tsc(gc, gb, BIG, -BIG, ALU.mult, ALU.add)
                tt(g12(a1), g12(sel), gmask, ALU.mult)
                dve.drain()
                tt(g12(a1), g12(a1), gc.unsqueeze(2).to_broadcast([P, 12, 4]), ALU.add)
                dve.drain()
                first_best(msk0, a1, a2, E_, mc("w16"))
                stt(a1, msk0, -2 * BIG, a1, ALU.mult, ALU.add)
                dve.drain()
                first_best(oh, a1, a2, E_, mc("w16"))
                tt(msk, msk0, oh, ALU.add)
                dve.drain()
                tt(v3(msk), v3(msk), mc("valid").unsqueeze(2).to_broadcast([P, 3, E_]), ALU.mult).then_inc(S("msk_ready"), 1)
                dve.drain()
                tt(a1, score, msk, ALU.mult)
                dve.drain()
                dve.tensor_reduce(top1, v3(a1), AX, ALU.add)
                dve.drain()
                tsc(top1, top1, 1e-37, None, ALU.max)
                dve.drain()
                dve.reciprocal(top1, top1)
                dve.drain()
                tt(gate3, v3(a1), top1.unsqueeze(2).to_broadcast([P, 3, E_]), ALU.mult)
                tsc(a2, msk, -1e6, 1e6, ALU.mult, ALU.add)
                dve.wait_ge(S("rk_mm"), l + 1)
                dve.drain()
                tt(rank3.rearrange("p t n -> p (t n)"), a2, ps[:, 7, 0:48], ALU.add)
                dve.tensor_reduce(cntp[:, 0:1], ps[:, 7, 64:80], AX, ALU.max)
                cp(cnt_i[0:1, 0:E_], ps[0:1, 7, 64:80])
                dve.drain()
                cp(cnt_i[0:1, E_:E_ + 1], cntp[0:1, 0:1])
                dve.drain().then_inc(S("route_ready"), 1)
                dve.wait_ge(S("route_ready"), l + 1)
                overflow(dve, l, "dve", more_block, lambda i: pick(0, i))
                dve.drain()
                for e in range(2):
                    pick(e, e)
                    select(e).then_inc(S("sel_ready"), 1)
                for q in range(2, NB):
                    w_lo(l, n0, 0, 0, q)
                xg_lo(E_ * l, 0)
                xg_lo(E_ * l, 1)
                for e in range(2):
                    expert(l, n0, 0, e, True, False)
                with dve.Fori(1, PAIRS - 1) as j:
                    for e in range(2):
                        expert(l, n0, j, e, False, False)
                for e in range(2):
                    expert(l, n0, PAIRS - 1, e, False, True)
                adds(PAIRS * (l + 1) - 1)
                dve.drain()
                for c in range(NC):
                    stt(YA[:, c, :], xT[:, c, :], ALPHA, YA[:, c, :], ALU.mult, ALU.add).then_inc(S("ln_in"), 1)

            residual(0, L_WO, 0)
            layer_norm(0)
            experts(0, L_MOE0)
            layer_norm(1, lambda: pw_lo(1, L_KV, 8, 0))
            for c in range(NC):
                px_lo(1, xT, 8, c)
            for co in range(1, 24):
                pw_lo(1, L_KV, 8, co)
            dve.wait_ge(S("in_aconst"), 32)
            lt4 = lamt.rearrange("p (a b n) -> p a b n", a=2, b=2)
            tt(lamp.rearrange("p (a n) -> p a n", a=2), lt4[:, :, 0, :], lt4[:, :, 1, :], ALU.mult)
            dve.drain()
            dve.tensor_reduce(lams[:, 0:2], lamp.rearrange("p (a n) -> p a n", a=2), AX, ALU.add).then_inc(S("lam_s"), 1)
            for i, (X, name) in enumerate(((KTM, "k"), (VTM, "v"))):
                for t, (t0, n) in enumerate(KTILE):
                    for hf in range(2):
                        j = 2 * t + hf
                        dve.wait_ge(S(f"{name}tr_mm"), after(f"{name}tr_mm", j + 1))
                        cp(X[0:n, t, 512 * hf:512 * hf + 512], ps[0:n, 4 + j % 4, :]).then_inc(S(f"{name}tm_ready"), 1)
            dve.wait_ge(S("lam_e"), 1)
            tt(lams[:, 4:5], lams[:, 3:4], lams[:, 2:3], ALU.subtract)
            dve.drain()
            tsc(lams[:, 4:5], lams[:, 4:5], -LI, None, ALU.add)
            dve.drain()
            tsc(lams[:, 6:7], lams[:, 4:5], -1.0, None, ALU.add)
            dve.drain()
            tt(lams[:, 5:6], lams[:, 6:7], ac("odd"), ALU.mult)
            dve.drain()
            tsc(lams[:, 5:6], lams[:, 5:6], 1.0, None, ALU.add)
            dve.wait_ge(S("kvq_ev"), 24)
            for v in Qbd:
                dve.memset(v, 0.0)
            dve.drain()
            units = [(t, h) for t in range(3) for h in range(NH)]
            NU = len(units)
            for u in range(NU + 2):
                if 1 <= u <= NU:
                    t, h = units[u - 1]
                    nq = KTILE[t][1]
                    nk = KTILE[t][0] + nq
                    st, p = st4[(u - 1) % 2], PP[(u - 1) % 2]
                    dve.wait_ge(S("p_exp"), 2 * u)
                    dve.reciprocal(st[0:nq, 4:6], st[0:nq, 2:4])
                    dve.drain()
                    tt(st[0:nq, 5:6], st[0:nq, 5:6], lams[0:nq, 4:5], ALU.mult)
                    tsc(p[0:nq, 0, 0:nk], p[0:nq, 0, 0:nk], st[0:nq, 4:5], None, ALU.mult)
                    dve.drain()
                    stt(p[0:nq, 0, 0:nk], p[0:nq, 1, 0:nk], st[0:nq, 5:6], p[0:nq, 0, 0:nk], ALU.mult, ALU.add
                        ).then_inc(S("p_am"), 1)
                if u < NU:
                    t, h = units[u]
                    nq = KTILE[t][1]
                    nk = KTILE[t][0] + nq
                    st = st4[u % 2]
                    dve.wait_ge(S("p_sc"), u + 1)
                    b = 2 * (u % 2)
                    dve.tensor_reduce(st[0:nq, 0:2], ps[0:nq, b:b + 2, 0:nk], AX, ALU.max)
                    dve.drain()
                    tsc(st[0:nq, 0:2], st[0:nq, 0:2], -0.125, None, ALU.mult).then_inc(S("p_nb"), 1)
                if u >= 2:
                    t, h = units[u - 2]
                    q0, nq = KTILE[t]
                    dve.wait_ge(S("p_av"), u - 1)
                    cp(aOT[:, h, q0:q0 + nq], ps[:, 6 + u % 2, 0:nq]).then_inc(S("p_oev"), 1)
            def sample_queries(b):
                if b >= 2:
                    dve.wait_ge(S("s_sc"), b - 1)
                for hp in range(2):
                    q = slice(64 * hp, 64 * hp + 64)
                    qv = Qbd[b % 2][q, SS * hp:SS * hp + 1152].rearrange("p (c n) -> p c n", n=144)[:, :, 0:SS]
                    i = cp(qv, aQT[q, :, TP + SS * b:TP + SS * b + SS])
                i.then_inc(S("qbd_ready"), 1)

            def sample_keys(b):
                for hf in range(2):
                    dve.wait_ge(S("kt_mm"), 4 * b + 3 + hf)
                    cp(KTs[b % 2][:, 4 * hf:4 * hf + 4, P:2 * P], bank(2 + hf).rearrange("p (c n) -> p c n", c=4)
                       ).then_inc(S("kts_d"), 1)

            def sample_max(b):
                dve.wait_ge(S("s_sc"), b + 1)
                st = st4[b % 2]
                dve.tensor_reduce(st[:, 0:1], ps[:, SCB[b % 2], 0:320], AX, ALU.max)
                dve.drain()
                tsc(st[:, 0:1], st[:, 0:1], -0.125, None, ALU.mult).then_inc(S("s_nb"), 1)

            dve.wait_ge(S("kvq_ev"), 24)
            sample_queries(0)
            sample_keys(0)
            sample_max(0)
            for b in range(SB):
                if b + 1 < SB:
                    sample_queries(b + 1)
                st = st4[b % 2]
                dve.wait_ge(S("s_exp"), b + 1)
                dve.reciprocal(st[:, 4:5], st[:, 2:3])
                dve.drain()
                tsc(PS[b % 2], PS[b % 2], st[:, 4:5], lams[:, 5:6], ALU.mult, ALU.mult).then_inc(S("s_am"), 1)
                if b + 1 < SB:
                    sample_keys(b + 1)
                dve.wait_ge(S("s_tr"), b + 1)
                for lo, hi, k in ((0, 2, P), (2, 3, TS)):
                    v = ps[0:k, 5, P * lo:P * hi].rearrange("p (k m q) -> p k m q", m=2, q=SS)
                    dve.tensor_reduce(ATs[b % 2][0:k, lo:hi, :].rearrange("p k (h q) -> p (k h) q", q=SS),
                                      v.rearrange("p k m q -> p k q m"), AX, ALU.add).then_inc(S("s_at"), 1)
                if b + 1 < SB:
                    sample_max(b + 1)
                dve.wait_ge(S("past_mm"), b + 1)
                cp(aOT[:, :, TP + SS * b:TP + SS * b + SS], ps[:, 6, 0:64].rearrange("p (h q) -> p h q", q=SS)
                   ).then_inc(S("s_oev"), 1)
            dve.wait_ge(S("sl_s"), after("sl_s", 1))
            dve.reciprocal(norm16[1], norm16[1])
            dve.drain()
            tsc(norm16[1], norm16[1], 1.0 - LI, None, ALU.mult).then_inc(S("sr_ready"), 1)
            for c in range(NC + 1):
                if c < NC:
                    dve.wait_ge(S("sr_mm"), after("sr_mm", c + 1))
                    stt(aOT[:, c, :], aOT[:, c, :], subv, bank(4 + c % 4, T), ALU.mult, ALU.mult).then_inc(S("z2_ready"), 1)
                if c == 0:
                    pw_lo(1, L_DO, 32, 0)
                else:
                    px_lo(1, aOT, 16, c - 1)
            pw_lo(1, L_DO, 32, 1)
            residual(1, L_DO, 32)
            layer_norm(2)
            experts(1, L_MOE1)
            layer_norm(3)
            for t in range(3):
                n = P if t < 2 else TS
                dve.wait_ge(S("yo_mm"), 2 * t + 2)
                cp(OUTT[0:n, t, 512:1024], ps[0:n, 2 * t + 1, :]).then_inc(S("y_rows"), 1)


_INS = ["x_prompt", "x_sample", "cache_k", "cache_v", "page_table", "state_wkv", "state_shift", "meta_tokens",
        "rwkv_mix", "rwkv_w_rkv", "rwkv_decay_w0", "rwkv_decay_w1", "rwkv_decay_w2", "rwkv_a_w0", "rwkv_a_w1",
        "rwkv_a_w2", "rwkv_g_w1", "rwkv_g_w2", "rwkv_kk_ka", "rwkv_r_k", "rwkv_lnx", "rwkv_w_out", "w_kv_shared",
        "diff_w_q", "diff_lambda", "diff_subln", "diff_w_out", "router_w", "router_b", "moe_w_gate", "moe_w_up",
        "moe_w_down", "post_ln"]
_OUTS = [("y_prompt", (1, SEQ, D)), ("y_sample", (SB, SS, D)), ("new_k_prompt", (1, TP, 2 * NH, N)),
         ("new_v_prompt", (1, TP, NH, P)), ("new_wkv_prompt", (1, 1, H, N, N)), ("new_shift_prompt", (1, 1, D)),
         ("new_k_sample", (SB, SS, 2 * NH, N)), ("new_v_sample", (SB, SS, NH, P)),
         ("new_wkv_sample", (SB, 1, H, N, N)), ("new_shift_sample", (SB, 1, D))]


def kernel(**inputs):
    import numpy as _np
    import concourse.bacc as _bacc
    from concourse.bass_utils import run_bass_kernel_spmd as _run

    nc = _bacc.Bacc("TRN2", target_bir_lowering=False, num_devices=1)
    const, at = constants()
    arrays, I, O = {"in_const": const}, {}, {}
    for name in _INS:
        arrays["in_" + name] = _np.ascontiguousarray(inputs[name])
    for key, a in arrays.items():
        I[key[3:]] = nc.dram_tensor(key, a.shape, mybir.dt.from_np(a.dtype), kind="ExternalInput").ap()
    for name, shape in _OUTS:
        O[name] = nc.dram_tensor("out_" + name, shape, F32, kind="ExternalOutput").ap()
    build(nc, I, O, const, at)
    r = _run(nc, [arrays], core_ids=[0])
    return tuple(r.results[0]["out_" + name] for name, _ in _OUTS)
```
